# Optimizing a Trainium2 kernel written in Bass

```python
import math
import jax
import jax.numpy as jnp
from jax import lax
import numpy as np

D_MODEL = 1024
BATCH = 1
SEQ = 512
DEPTH = 2

GRID_W = 64
CTX_LEN = 256
N_MIXERS = 3
LN_EPS = 1e-5

HY_ORDER = 2
HY_DIRS = 2
HY_EMB = 33
HY_BANDS = (HY_EMB - 1) // 2
HY_FF = 64
HY_SHORT = 3
HY_DECAY_TARGET = 1e-2
HY_DECAY_SHORT_PCT = 0.3
HY_DECAY_LONG_PCT = 1.5

GLA_HEADS = 4
GLA_DK = D_MODEL // 2
GLA_DV = D_MODEL
GLA_RANK = 16
GLA_TAU = 16.0
GLA_CHUNK = 64

GM_CHUNK = 128
GM_HEADS = 4

N_EXPERTS = 32
N_GROUPS = 4
TOP_K = 2
D_EXPERT = 512
MOE_BLOCK = 128

kernel_name = "hybrid_hyena_gla_gmlp_moe_flow_backbone"

def layer_norm(x, g, b):
    xf = x.astype(jnp.float32)
    mu = jnp.mean(xf, -1, keepdims=True)
    var = jnp.mean(jnp.square(xf - mu), -1, keepdims=True)
    return ((xf - mu) * lax.rsqrt(var + LN_EPS) * g + b).astype(x.dtype)

def sincos_2d(rows, cols, d):
    q = d // 4
    omega = 1.0 / (10000.0 ** (jnp.arange(q, dtype=jnp.float32) / q))
    pr = jnp.arange(rows, dtype=jnp.float32)[:, None] * omega
    pc = jnp.arange(cols, dtype=jnp.float32)[:, None] * omega
    er = jnp.concatenate([jnp.sin(pr), jnp.cos(pr)], -1)
    ec = jnp.concatenate([jnp.sin(pc), jnp.cos(pc)], -1)
    emb = jnp.concatenate([jnp.broadcast_to(er[:, None, :], (rows, cols, 2 * q)),
                           jnp.broadcast_to(ec[None, :, :], (rows, cols, 2 * q))], -1)
    return emb.reshape(rows * cols, 4 * q)

def depthwise_conv_centred(u, w, b):
    k = w.shape[0]
    y = lax.conv_general_dilated(u, w[:, None, :].astype(u.dtype), (1,), [(k // 2, k // 2)],
                                 dimension_numbers=("NWC", "WIO", "NWC"),
                                 feature_group_count=u.shape[-1])
    return y + b

def hyena_filters(L, w1, b1, w2, b2, w3, b3, w4):
    f32 = jnp.float32
    t = jnp.linspace(0.0, 1.0, L, dtype=f32)[:, None]
    wpos = 2.0 * math.pi * jnp.arange(L, dtype=f32)[:, None] / L
    bands = jnp.linspace(1e-4, HY_BANDS - 1, HY_BANDS, dtype=f32)[None, :]
    z = jnp.concatenate([t, jnp.cos(bands * wpos), -jnp.sin(bands * wpos)], -1)
    hf = jnp.sin(z @ w1 + b1)
    hf = jnp.sin(hf @ w2 + b2)
    hf = jnp.sin(hf @ w3 + b3)
    hf = (hf @ w4).astype(f32).reshape(L, HY_ORDER, HY_DIRS, -1)
    d = hf.shape[-1]
    max_decay = math.log(HY_DECAY_TARGET) / HY_DECAY_SHORT_PCT
    min_decay = math.log(HY_DECAY_TARGET) / HY_DECAY_LONG_PCT
    deltas = jnp.abs(jnp.linspace(min_decay, max_decay, d, dtype=f32))
    window = jnp.exp(-t * deltas)
    return hf * window[:, None, None, :]

def bidir_fftconv(u, h_fwd, h_bwd):
    L = u.shape[1]
    taps = jnp.concatenate([h_fwd[:1] + h_bwd[:1], h_fwd[1:],
                            jnp.zeros_like(h_fwd[:1]), h_bwd[:0:-1]], 0)
    kf = jnp.fft.rfft(taps, axis=0)
    uf = jnp.fft.rfft(u.astype(jnp.float32), n=2 * L, axis=1)
    return jnp.fft.irfft(uf * kf[None], n=2 * L, axis=1)[:, :L]

def hyena_mixer(a, w_in, b_in, conv_w, conv_b, f_w1, f_b1, f_w2, f_b2, f_w3, f_b3, f_w4,
                skip, w_out, b_out):
    L = a.shape[1]
    z = depthwise_conv_centred(a @ w_in + b_in, conv_w, conv_b)
    v, x1, x2 = jnp.split(z.astype(jnp.float32), 3, axis=-1)
    filt = hyena_filters(L, f_w1, f_b1, f_w2, f_b2, f_w3, f_b3, f_w4)
    y = v
    for n, gate in enumerate((x1, x2)):
        y = gate * (bidir_fftconv(y, filt[:, n, 0], filt[:, n, 1]) + y * skip[n])
    return y.astype(a.dtype) @ w_out + b_out

def gla_project(a, w_in, w_gate, b_gate):
    B, L, _ = a.shape
    z = a @ w_in
    dk, dv = GLA_DK, GLA_DV
    q = z[..., :dk]
    k = z[..., dk:2 * dk]
    v = z[..., 2 * dk:2 * dk + dv]
    r = z[..., 2 * dk + dv:2 * dk + 2 * dv]
    lr = z[..., 2 * dk + 2 * dv:].reshape(B, L, HY_DIRS, GLA_RANK)
    glog = jax.nn.log_sigmoid((jnp.einsum('bldr,drk->bldk', lr, w_gate) + b_gate).astype(jnp.float32)) / GLA_TAU

    def heads(t):
        return t.reshape(B, L, GLA_HEADS, -1).astype(jnp.float32)

    dkh = dk // GLA_HEADS
    return (heads(q) * (dkh ** -0.5), heads(k), heads(v), r,
            heads(glog[:, :, 0]), heads(glog[:, :, 1]))

def gla_chunked(q, k, v, g, s0):
    B, L, H, _ = q.shape
    C = GLA_CHUNK
    nc = L // C

    def to_chunks(t):
        return t.reshape(B, nc, C, H, t.shape[-1]).transpose(1, 0, 3, 2, 4)

    mask = jnp.tril(jnp.ones((C, C), bool))

    def step(s, inp):
        qi, ki, vi, gi = inp
        b = jnp.cumsum(gi, axis=2)
        diff = jnp.where(mask[:, :, None], b[:, :, :, None, :] - b[:, :, None, :, :], -jnp.inf)
        att = jnp.einsum('bhtd,bhsd,bhtsd->bhts', qi, ki, jnp.exp(diff))
        o = jnp.einsum('bhts,bhsv->bhtv', att, vi) + jnp.einsum('bhtd,bhdv->bhtv', qi * jnp.exp(b), s)
        b_last = b[:, :, -1:, :]
        s = s * jnp.exp(b_last[:, :, 0, :, None]) + jnp.einsum('bhsd,bhsv->bhdv', ki * jnp.exp(b_last - b), vi)
        return s, o

    s, o = lax.scan(step, s0, (to_chunks(q), to_chunks(k), to_chunks(v), to_chunks(g)))
    o = o.transpose(1, 0, 3, 2, 4).reshape(B, L, H, v.shape[-1])
    return o, s

def gla_final_state(k, v, g):
    b = jnp.cumsum(g, axis=1)
    return jnp.einsum('blhd,blhv->bhdv', k * jnp.exp(b[:, -1:] - b), v)

def gla_output(o, r, norm_g, w_out):
    B, L, H, dvh = o.shape
    mu = jnp.mean(o, -1, keepdims=True)
    var = jnp.mean(jnp.square(o - mu), -1, keepdims=True)
    on = (o - mu) * lax.rsqrt(var + LN_EPS) * norm_g.reshape(H, dvh)
    y = on.reshape(B, L, H * dvh) * jax.nn.silu(r.astype(jnp.float32))
    return y.astype(r.dtype) @ w_out

def gla_mixer(a, ac, w_in, w_gate, b_gate, norm_g, w_out, ctx_out):
    def flip(t):
        return t[:, ::-1]

    q, k, v, r, gf, gb = gla_project(a, w_in, w_gate, b_gate)
    qc, kc, vc, rc, gfc, gbc = gla_project(ac, w_in, w_gate, b_gate)
    if ctx_out:
        zero = jnp.zeros((ac.shape[0], GLA_HEADS, GLA_DK // GLA_HEADS, GLA_DV // GLA_HEADS), jnp.float32)
        ocf, s_f = gla_chunked(qc, kc, vc, gfc, zero)
        ocb, s_b = gla_chunked(flip(qc), flip(kc), flip(vc), flip(gbc), zero)
        yc = gla_output(ocf + flip(ocb), rc, norm_g, w_out)
    else:
        s_f = gla_final_state(kc, vc, gfc)
        s_b = gla_final_state(flip(kc), flip(vc), flip(gbc))
        yc = None
    of, _ = gla_chunked(q, k, v, gf, s_f)
    ob, _ = gla_chunked(flip(q), flip(k), flip(v), flip(gb), s_b)
    y = gla_output(of + flip(ob), r, norm_g, w_out)
    return y, yc

def gmlp_mixer(a, w_in, b_in, ln_g, ln_b, ws, bs, w_out, b_out):
    B, L, D = a.shape
    z = jax.nn.gelu(a @ w_in + b_in)
    u, v = jnp.split(z, 2, axis=-1)
    v = layer_norm(v, ln_g, ln_b)
    nc = L // GM_CHUNK
    vc = v.reshape(B, nc, GM_CHUNK, GM_HEADS, D // GM_HEADS)
    vm = jnp.einsum('gts,bnsgc->bntgc', ws, vc) + bs.T[None, None, :, :, None]
    return (u * vm.reshape(B, L, D)) @ w_out + b_out

def route(tok, router_w, router_b):
    n = tok.shape[0]
    gsz = N_EXPERTS // N_GROUPS
    s = jax.nn.sigmoid((tok @ router_w).astype(jnp.float32))
    grp = (s + router_b).reshape(n, N_GROUPS, gsz)
    gscore = jnp.sum(lax.top_k(grp, TOP_K)[0], -1)
    g = jnp.argmax(gscore, -1)
    in_grp = grp[jnp.arange(n), g]
    _, loc = lax.top_k(in_grp, TOP_K)
    eid = g[:, None] * gsz + loc
    w = jnp.take_along_axis(s, eid, axis=1)
    return eid, w / jnp.sum(w, -1, keepdims=True)

def moe_layer(tok, router_w, router_b, w1, w3, w2):
    n, d = tok.shape
    e_n = w1.shape[0]
    eid, w = route(tok, router_w, router_b)
    nk = n * TOP_K
    e_flat = eid.reshape(-1)
    tok_flat = jnp.repeat(jnp.arange(n, dtype=jnp.int32), TOP_K)
    order = jnp.argsort(e_flat)
    e_s, tok_s, w_s = e_flat[order], tok_flat[order], w.reshape(-1)[order]
    counts = jnp.bincount(e_flat, length=e_n)
    start = jnp.cumsum(counts) - counts
    padded = (counts + MOE_BLOCK - 1) // MOE_BLOCK * MOE_BLOCK
    pend = jnp.cumsum(padded)
    pstart = pend - padded
    dest = pstart[e_s] + jnp.arange(nk, dtype=jnp.int32) - start[e_s]
    p = (nk + MOE_BLOCK - 1) // MOE_BLOCK * MOE_BLOCK + e_n * MOE_BLOCK
    nblk = p // MOE_BLOCK
    buf_tok = jnp.full((p,), n, jnp.int32).at[dest].set(tok_s)
    buf_w = jnp.zeros((p,), w.dtype).at[dest].set(w_s)
    blk_e = jnp.clip(jnp.searchsorted(pend, jnp.arange(nblk) * MOE_BLOCK, side='right'), 0, e_n - 1)
    x_pad = jnp.concatenate([tok, jnp.zeros((1, d), tok.dtype)], 0)
    xb = x_pad[buf_tok].reshape(nblk, MOE_BLOCK, d)

    def expert_block(args):
        xi, e = args
        return (jax.nn.silu(xi @ w1[e]) * (xi @ w3[e])) @ w2[e]

    yb = lax.map(expert_block, (xb, blk_e)).reshape(p, d)
    out = jnp.zeros((n + 1, d), jnp.float32).at[buf_tok].add(yb.astype(jnp.float32) * buf_w[:, None])
    return out[:n].astype(tok.dtype)

def setup_inputs(seed: int = 0) -> dict:
    key = jax.random.key(seed)
    keys = iter(jax.random.split(key, 64))
    f32 = jnp.float32
    D = D_MODEL
    beta = (8.0 * DEPTH) ** -0.25
    n_a = len(range(0, DEPTH, N_MIXERS))
    n_b = len(range(1, DEPTH, N_MIXERS))
    n_c = len(range(2, DEPTH, N_MIXERS))
    hy_ch = HY_ORDER * HY_DIRS * D
    gla_in = 2 * GLA_DK + 2 * GLA_DV + HY_DIRS * GLA_RANK

    def nrm(shape, scale):
        return jax.random.normal(next(keys), shape, f32) * scale

    return {
        "x": nrm((BATCH, SEQ, D), 1.0),
        "c": nrm((BATCH, D), 1.0),
        "ctx": nrm((BATCH, CTX_LEN, D), 1.0),
        "c_ctx": nrm((D,), 1.0),
        "w_mod": nrm((DEPTH, D, 6 * D), 0.5 * D ** -0.5),
        "b_mod": nrm((DEPTH, 6 * D), 0.01),
        "ln_g": 1.0 + nrm((DEPTH, 2, D), 0.05),
        "ln_b": nrm((DEPTH, 2, D), 0.02),
        "hy_w_in": nrm((n_a, D, 3 * D), D ** -0.5),
        "hy_b_in": nrm((n_a, 3 * D), 0.02),
        "hy_conv_w": nrm((n_a, HY_SHORT, 3 * D), HY_SHORT ** -0.5),
        "hy_conv_b": nrm((n_a, 3 * D), 0.02),
        "hy_f_w1": nrm((n_a, HY_EMB, HY_FF), HY_EMB ** -0.5),
        "hy_f_b1": nrm((n_a, HY_FF), 0.1),
        "hy_f_w2": nrm((n_a, HY_FF, HY_FF), HY_FF ** -0.5),
        "hy_f_b2": nrm((n_a, HY_FF), 0.1),
        "hy_f_w3": nrm((n_a, HY_FF, HY_FF), HY_FF ** -0.5),
        "hy_f_b3": nrm((n_a, HY_FF), 0.1),
        "hy_f_w4": nrm((n_a, HY_FF, hy_ch), 0.02),
        "hy_skip": nrm((n_a, HY_ORDER, D), 0.5),
        "hy_w_out": nrm((n_a, D, D), beta * D ** -0.5),
        "hy_b_out": nrm((n_a, D), 0.02),
        "gla_w_in": nrm((n_b, D, gla_in), D ** -0.5),
        "gla_w_gate": nrm((n_b, HY_DIRS, GLA_RANK, GLA_DK), GLA_RANK ** -0.5),
        "gla_b_gate": nrm((n_b, HY_DIRS, GLA_DK), 0.1),
        "gla_norm_g": 1.0 + nrm((n_b, GLA_DV), 0.05),
        "gla_w_out": nrm((n_b, GLA_DV, D), beta * GLA_DV ** -0.5),
        "gm_w_in": nrm((n_c, D, 2 * D), D ** -0.5),
        "gm_b_in": nrm((n_c, 2 * D), 0.02),
        "gm_ln_g": 1.0 + nrm((n_c, D), 0.05),
        "gm_ln_b": nrm((n_c, D), 0.02),
        "gm_ws": nrm((n_c, GM_HEADS, GM_CHUNK, GM_CHUNK), GM_CHUNK ** -0.5),
        "gm_bs": 1.0 + nrm((n_c, GM_HEADS, GM_CHUNK), 0.02),
        "gm_w_out": nrm((n_c, D, D), beta * D ** -0.5),
        "gm_b_out": nrm((n_c, D), 0.02),
        "router_w": nrm((D, N_EXPERTS), D ** -0.5),
        "router_b": nrm((N_EXPERTS,), 0.01),
        "moe_w1": nrm((DEPTH, N_EXPERTS, D, D_EXPERT), D ** -0.5),
        "moe_w3": nrm((DEPTH, N_EXPERTS, D, D_EXPERT), D ** -0.5),
        "moe_w2": nrm((DEPTH, N_EXPERTS, D_EXPERT, D), beta * D_EXPERT ** -0.5),
    }

def reference(x, c, ctx, c_ctx, w_mod, b_mod, ln_g, ln_b,
              hy_w_in, hy_b_in, hy_conv_w, hy_conv_b, hy_f_w1, hy_f_b1, hy_f_w2, hy_f_b2,
              hy_f_w3, hy_f_b3, hy_f_w4, hy_skip, hy_w_out, hy_b_out,
              gla_w_in, gla_w_gate, gla_b_gate, gla_norm_g, gla_w_out,
              gm_w_in, gm_b_in, gm_ln_g, gm_ln_b, gm_ws, gm_bs, gm_w_out, gm_b_out,
              router_w, router_b, moe_w1, moe_w3, moe_w2):
    alpha = (2.0 * DEPTH) ** 0.25
    B, L, D = x.shape
    rows = L // GRID_W
    h = x + sincos_2d(rows, GRID_W, D).astype(x.dtype)[None]
    hc = ctx
    gla_layers = list(range(1, DEPTH, N_MIXERS))
    last_ctx = gla_layers[-1] if gla_layers else -1
    s_lat = jax.nn.silu(c)
    s_ctx = jax.nn.silu(c_ctx)
    yc = None
    cm = None
    ac = None
    for i in range(DEPTH):
        kind, j = i % N_MIXERS, i // N_MIXERS
        ctx_full = i < last_ctx
        m = jnp.split(s_lat @ w_mod[i] + b_mod[i], 6, axis=-1)
        sh1, sc1, g1, sh2, sc2, g2 = [t[:, None, :] for t in m]
        a = h * (1.0 + sc1) + sh1
        if i <= last_ctx:
            cm = jnp.split(s_ctx @ w_mod[i] + b_mod[i], 6, axis=-1)
            ac = hc * (1.0 + cm[1]) + cm[0]
        if kind == 0:
            hy = (hy_w_in[j], hy_b_in[j], hy_conv_w[j], hy_conv_b[j], hy_f_w1[j], hy_f_b1[j],
                  hy_f_w2[j], hy_f_b2[j], hy_f_w3[j], hy_f_b3[j], hy_f_w4[j], hy_skip[j],
                  hy_w_out[j], hy_b_out[j])
            y = hyena_mixer(a, *hy)
            if ctx_full:
                yc = hyena_mixer(ac, *hy)
        elif kind == 1:
            y, yc = gla_mixer(a, ac, gla_w_in[j], gla_w_gate[j], gla_b_gate[j], gla_norm_g[j],
                              gla_w_out[j], ctx_full)
        else:
            gm = (gm_w_in[j], gm_b_in[j], gm_ln_g[j], gm_ln_b[j], gm_ws[j], gm_bs[j],
                  gm_w_out[j], gm_b_out[j])
            y = gmlp_mixer(a, *gm)
            if ctx_full:
                yc = gmlp_mixer(ac, *gm)
        h = layer_norm(alpha * h + g1 * y, ln_g[i, 0], ln_b[i, 0])
        a = h * (1.0 + sc2) + sh2
        if ctx_full:
            hc = layer_norm(alpha * hc + cm[2] * yc, ln_g[i, 0], ln_b[i, 0])
            ac = hc * (1.0 + cm[4]) + cm[3]
            tok = jnp.concatenate([a.reshape(-1, D), ac.reshape(-1, D)], 0)
        else:
            tok = a.reshape(-1, D)
        f = moe_layer(tok, router_w, router_b, moe_w1[i], moe_w3[i], moe_w2[i])
        n_lat = B * L
        h = layer_norm(alpha * h + g2 * f[:n_lat].reshape(B, L, D), ln_g[i, 1], ln_b[i, 1])
        if ctx_full:
            hc = layer_norm(alpha * hc + cm[5] * f[n_lat:].reshape(hc.shape), ln_g[i, 1], ln_b[i, 1])
    return h


_drawn_inputs = setup_inputs


def setup_inputs(seed=0):
    import zlib

    import numpy as np

    out = dict(_drawn_inputs(seed))
    spreads = {}
    factors = {'ctx': 7.647, 'c_ctx': 8.0, 'hy_b_out': 8.0, 'gla_b_gate': 8.0, 'gla_norm_g': 8.0}
    for name, (base, spread) in spreads.items():
        noise = np.random.default_rng([zlib.crc32(name.encode()), seed]).standard_normal(out[name].shape)
        drawn = base * np.exp(spread * noise) if base else spread * noise
        out[name] = jnp.asarray(drawn.astype(out[name].dtype))
    for name, factor in factors.items():
        out[name] = (out[name] * factor).astype(out[name].dtype)
    return out
```

```python
from contextlib import ExitStack

import numpy as np
import concourse.bass as bass
import concourse.mybir as mybir

F32 = mybir.dt.float32
I32 = mybir.dt.int32
U32 = mybir.dt.uint32
ALU = mybir.AluOpType
ACT = mybir.ActivationFunctionType
AX = mybir.AxisListType
ds = bass.ds

P = 128
D = 1024
KD = D // P
LAT, CTX = 512, 256
NT = LAT + CTX
CL, CC = LAT // P, CTX // P
COL = 512
UNIT = KD * COL
SLOTS = 6
E_N, GRP, GSZ = 32, 4, 8
D_E = 512
SB = 64
ALPHA = (2.0 * 2) ** 0.25
EPS = 1e-5
HF = 64
HEADS, DKH, DVH = 4, 128, 256
N_MOD = 24
TAU = 16.0
LEVELS = 7

MAGIC = 12582912.0
PI2_HI = 6.28125
PI2_LO = 2.0 * np.pi - 6.28125


def blocks_max(tokens):
    return 2 * tokens // SB + E_N


class PsumPlan:

    def __init__(self):
        self.total = 0
        self.used = [0] * 8
        self.of = {}

    def add(self, name, bank=None):
        bank = self.total % 8 if bank is None else bank
        self.total += 1
        self.of[name] = (bank, self.total, self.used[bank])
        self.used[bank] += 1
        return self.of[name]


class Ring:

    def __init__(self):
        self.at = 0
        self.loads = [0] * SLOTS
        self.of = {}

    def add(self, name, loads=1):
        slot = self.at % SLOTS
        self.of[name] = (slot, self.loads[slot])
        self.loads[slot] += loads
        self.at += 1

    def skip(self, n):
        self.at += n


def build(nc, t, out):
    ctx = ExitStack()

    def sem(name):
        return ctx.enter_context(nc.semaphore(name))

    def scratch(name, shape, dt=F32):
        return nc.dram_tensor(name, shape, dt, kind="Internal").ap()

    ring = ctx.enter_context(nc.sbuf_tensor("ring", [P, SLOTS * UNIT], F32))
    arena = ctx.enter_context(nc.sbuf_tensor("arena", [P, 26624], F32))
    keep = ctx.enter_context(nc.sbuf_tensor("keep", [P, 2000], F32))
    psum = [ctx.enter_context(nc.psum_tensor(f"bank{i}", [P, 512], F32)) for i in range(8)]

    KB = 256

    def at(kb, n, lo=0, hi=P):
        o = int(kb * KB)
        return arena[lo:hi, o:o + n]

    def slot(s, lo=0, n=UNIT):
        return ring[:, s * UNIT + lo:s * UNIT + lo + n]

    mod_d = scratch("mod_d", [2, N_MOD, 4, P])
    h0_d = scratch("h0_d", [LAT, D])

    ident = keep[:, 0:128]
    hf_sum = keep[:, 128:128 + NT]
    hf_diff = keep[:, 896:896 + NT]
    modT = keep[:, 1664:1856].rearrange("p (l r v k) -> p l r v k", l=2, r=2, v=6)
    smallT = keep[:, 1856:1984]
    sgn, rowmask, eps = keep[:, 1984:1985], keep[:, 1985:1986], keep[:, 1986:1987]

    def conv_w(j, ch):
        return smallT[:, 24 * j + ch:24 * j + ch + 1]

    def b_in(ch):
        return smallT[:, 72 + ch:73 + ch]

    def conv_b(ch):
        return smallT[:, 96 + ch:97 + ch]

    aT = at(0, KD * NT).rearrange("p (k n) -> p k n", k=KD)
    aT_l = [aT, at(24, KD * NT).rearrange("p (k n) -> p k n", k=KD)]
    x_rows = at(24, 6 * D).rearrange("p (c d) -> p c d", c=6)
    pe_rows = at(48, 4 * D).rearrange("p (c d) -> p c d", c=4)
    mod_acc = at(72, N_MOD * P).rearrange("p (n c) -> p n c", n=N_MOD)
    cond_rows = at(84, P, 0, 16)
    s_cols = at(84.5, KD * 32).rearrange("p (k c) -> p k c", k=KD)
    small_rows = at(86, P)
    mod_rows = at(87, 2 * P, 0, 96).rearrange("p (l c) -> p l c", l=2)
    hf1, hf2 = at(88, NT, 0, HF), at(91, NT, 0, HF)
    arg_u, arg_t = at(64, NT), at(67, NT)
    zT = at(96, NT, 0, 33)
    taps = [at(96, 772), arena[:, 96 * KB + 772:96 * KB + 1544]]
    fw = arena[:, 26120:26120 + 256]
    f_w1, f_w2, f_w3 = fw[0:33, 0:HF], fw[0:HF, HF:2 * HF], fw[0:HF, 2 * HF:4 * HF]
    f_b = arena[:, 26376:26380]
    zc = [at(72, NT), at(75, NT)]
    v_t = at(24, 6 * D).rearrange("p (c d) -> p c d", c=6)
    x1_t = at(48, 6 * D).rearrange("p (c d) -> p c d", c=6)
    x2T = at(72, KD * NT).rearrange("p (k n) -> p k n", k=KD)
    filt = [at(8 * i, 4 * COL).rearrange("p (c d) -> p c d", c=4) for i in (0, 1)]
    z_re = at(16, 4 * COL).rearrange("p (c d) -> p c d", c=4)
    z_im = at(96, 4 * COL).rearrange("p (c d) -> p c d", c=4)

    units = Ring()
    for u in range(N_MOD):
        units.add(("mod", u))
    for j in range(6):
        units.add(("hy_in", j))
    units.add(("filt", 0), 0)
    units.add(("dft", 0))
    units.add(("idft", 0))
    units.add(("hy_out", 0))
    units.add(("hy_out", 1))
    units.skip(1)
    moe_first = {}
    moe_first[0] = list(units.loads)
    assert units.at % SLOTS == 0
    for e in range(E_N * 3):
        units.add(("moe0", e))
    for j in range(6):
        units.add(("gla_in", j))
    units.skip(4)
    for j in range(2):
        units.add(("gla_out", j))
    moe_first[1] = list(units.loads)

    k_re, k_im, k_ny, prod_a, prod_b = (slot(5, COL * i, COL) for i in range(5))
    win = [slot(5, COL * (5 + i), COL) for i in (0, 1)]
    skip_row = ring[0:1, 5 * UNIT + 7 * COL:5 * UNIT + 8 * COL]

    landed = [sem(f"landed{i}") for i in range(SLOTS)]
    psum_filled = sem("psum_filled")
    psum_drained = [sem(f"psum_drained{i}") for i in range(8)]
    keep_in, cond_in, small_in, x_in, pe_in, ctx_in, fw_in = (
        sem(n) for n in ("keep_in", "cond_in", "small_in", "x_in", "pe_in", "ctx_in", "fw_in"))
    bias_in, filt_in = sem("bias_in"), sem("filt_in")
    mod_zeroed, cols_zeroed, cond_silu = sem("mod_zeroed"), sem("cols_zeroed"), sem("cond_silu")
    mod_filled, mod_drained, mod_stored = sem("mod_filled"), sem("mod_drained"), sem("mod_stored")
    mod_back, modT_done = sem("mod_back"), sem("modT_done")
    pe_added, h0_stored = sem("pe_added"), sem("h0_stored")
    act_link, dve_link, pool_link = sem("act_link"), sem("dve_link"), sem("pool_link")
    sin_arg, sin_done, hf_done = sem("sin_arg"), sem("sin_done"), sem("hf_done")
    edges_zeroed, conv_done = sem("edges_zeroed"), sem("conv_done")
    win_in = [sem("win_in0"), sem("win_in1")]
    skip_in, skip_added = sem("skip_in"), sem("skip_added")
    k_ready, products, z_ready = sem("k_ready"), sem("products"), sem("z_ready")

    router_w = keep[:, 128:384].rearrange("p (k e) -> p k e", k=KD)
    router_b = keep[:, 384:416]
    before, ones = keep[:, 416:544], keep[:, 544:672]
    token_id, ramp8, ramp4 = keep[:, 672:678], keep[:, 678:686], keep[:, 686:690]
    scores = keep[:, 690:882]
    pair_w = keep[:, 882:894].rearrange("p (k c) -> p k c", k=2)
    dest = keep[:, 894:906].bitcast(U32).rearrange("p (k c) -> p k c", k=2)
    starts = keep[0:1, 906:940].bitcast(I32)
    slot_tok = keep[0:SB, 940:998].bitcast(U32)
    cur_tok = keep[0:SB, 998:999].bitcast(U32)
    stats = keep[:, 1000:1012].rearrange("p (h s) -> p h s", h=2)
    mean_var, dev, rdev = keep[:, 1012:1014], keep[:, 1014:1015], keep[:, 1015:1016]
    h_rows = at(0, 6 * D).rearrange("p (c d) -> p c d", c=6)
    temps = [at(72 + 0.75 * i, 192) for i in range(16)]
    slot_rows = at(90, SB, 0, P)

    tok_l = [scratch(f"tok{l}", [(NT, LAT)[l], D]) for l in (0, 1)]
    slot_l = [scratch(f"slot{l}", [(blocks_max((NT, LAT)[l]) + 1) * SB, 1]) for l in (0, 1)]
    y_d = scratch("y", [blocks_max(NT) * SB, D])

    CHUNKS_OF = [list(range(6)), list(range(CL))]
    mixed = [x2T, at(24, KD * LAT).rearrange("p (k n) -> p k n", k=KD)]
    BC = [["bout", "g1l", "g1c", "lng", "lnb", "sc2l", "sc2c", "sh2l", "sh2c"],
          ["g1l", "lng", "lnb", "sc2l", "sh2l"]]
    bc0 = [24, 72]
    bcast = [{n: at(bc0[l] + 4 * i, D) for i, n in enumerate(BC[l])} for l in (0, 1)]
    a2 = [at(60, D), at(64, D)]
    a2T = at(68, D).rearrange("p (k n) -> p k n", k=KD)
    resid = at(96, D)
    tmp = [at(100, COL), at(102, COL)]

    x_slots = at(24, D, 0, SB)
    xT = at(28, KD * SB).rearrange("p (k n) -> p k n", k=KD)
    gate_act = [at(30, P), at(30.5, P)]
    hid = [at(31, P), at(31.5, P)]
    hidT = [at(32, P), at(32.5, P)]
    y_out = at(33, COL)
    y_pair = [[at(36, D), at(40, D)], [at(44, D), at(48, D)]]
    mix = [at(52, D), at(56, D)]
    bc2 = {n: at(60 + 4 * i, D) for i, n in enumerate(["g2l", "g2c", "lng", "lnb"])}

    bc_in, sc2_done, res_in, res_used = sem("bc_in"), sem("sc2_done"), sem("res_in"), sem("res_used")
    var_ready, dev_done, normed, a2_done = sem("var_ready"), sem("dev_done"), sem("normed"), sem("a2_done")
    tok_stored, route_in, h_ready = sem("tok_stored"), sem("route_in"), sem("h_ready")
    picked, starts_done, dest_done, slot_zero = sem("picked"), sem("starts_done"), sem("dest_done"), sem("slot_zero")
    slot_cleared, scattered, slots_back, table_done = (
        sem("slot_cleared"), sem("scattered"), sem("slots_back"), sem("table_done"))
    L2 = (0, 1)
    x_copied = [sem(f"x_copied{l}") for l in L2]
    x_landed = [sem(f"x_landed{l}") for l in L2]
    x_turned = [sem(f"x_turned{l}") for l in L2]
    gather_go = [sem(f"gather_go{l}") for l in L2]
    xT_done = [sem(f"xT_done{l}") for l in L2]
    up_filled = [sem(f"up_filled{l}") for l in L2]
    gate_done = [sem(f"gate_done{l}") for l in L2]
    hid_done = [sem(f"hid_done{l}") for l in L2]
    hid_turned = [sem(f"hid_turned{l}") for l in L2]
    hidT_done = [sem(f"hidT_done{l}") for l in L2]
    y_filled = [sem(f"y_filled{l}") for l in L2]
    y_copied = [sem(f"y_copied{l}") for l in L2]
    y_stored = [sem(f"y_stored{l}") for l in L2]
    bc2_in, pair_in, mixed_done, h_next = (
        [sem("bc2_in"), None], [sem("pair_in0"), sem("pair_in1")], sem("mixed_done"), sem("h_next"))
    y_filled_up, combine_go = sem("y_filled_up"), sem("combine_go")
    scaled, out_stored, layer_done = sem("scaled"), sem("out_stored"), sem("layer_done")

    def gchunk(l, c):
        return c + len(CHUNKS_OF[0]) * l


    h1_d = scratch("h1_d", [LAT, D])
    r_rows = at(0, CL * D).rearrange("p (c d) -> p c d", c=CL)
    masks = at(16, LEVELS * P).rearrange("p (l n) -> p l n", l=LEVELS)
    prod = at(19.5, 4 * P)
    gate_w = [keep[0:32, 1016:1016 + COL], at(21.5, COL, 0, 32)]
    qk = at(48, HEADS * 2 * LAT).rearrange("p (h m n) -> p h m n", h=HEADS, m=2)
    k_ctx = at(64, HEADS * CTX).rearrange("p (h n) -> p h n", h=HEADS)
    v_rows = at(68, 6 * D).rearrange("p (c d) -> p c d", c=6)
    lrT = at(92, NT, 0, 32)
    soft = at(95, NT)
    kt_rows = at(99, 4 * P)
    state = at(101, 2 * DVH).rearrange("p (r n) -> p r n", r=2)
    lr_w = at(103, KD * 32).rearrange("p (k c) -> p k c", k=KD)
    norm_g = at(40, D)
    g_stats = keep[:, 1528:1552].rearrange("p (c s) -> p c s", c=CL)
    g_mv = keep[:, 1552:1560].rearrange("p (c s) -> p c s", c=CL)
    g_dev, g_rdev = keep[:, 1560:1564], keep[:, 1564:1568]
    lev = [ring[:, 1024 * i:1024 * i + 1024] for i in range(3)]
    att_near = ring[:, 3072:3584]
    att_next = ring[:, 3584:4096]
    att_far = ring[:, 4096:5120]
    cums = [ring[:, 5120 + 1536 * i:5120 + 1536 * (i + 1)].rearrange("p (r n) -> p r n", r=2) for i in (0, 1)]
    o_rows = slot(2).rearrange("p (c d) -> p c d", c=CL)

    h1_stored, gla_in, zero_w, gates_abs = sem("h1_stored"), sem("gla_small_in"), sem("zero_w"), sem("gates_abs")
    gates_ln, cum_done, args_done, exps_done = sem("gates_ln"), sem("cum_done"), sem("args_done"), sem("exps_done")
    scaled_qk, prod_done, near_done = sem("scaled_qk"), sem("prod_done"), sem("near_done")
    norm_in, o_var, o_dev, o_normed, o_gained = (
        sem("norm_in"), sem("o_var"), sem("o_dev"), sem("o_normed"), sem("o_gained"))
    silu_done, y_rows_done = sem("silu_done"), sem("y_rows_done")
    combined = sem("combined")

    N_LV = LEVELS + 5
    LV_CTX, LV_STATE = LEVELS + 3, LEVELS + 4
    ITEMS = [(h, lv) for h in range(HEADS) for lv in range(N_LV)]

    PROJ = ([("v", 0, c) for c in range(6)] + [("v", 1, c) for c in range(6)] +
            [("r", half, c) for half in (0, 1) for c in range(CL)])
    PROJ_AT = {}
    for hd, first, n in ((0, 0, 6), (1, 6, 5), (2, 11, 5), (3, 16, 4)):
        for j in range(n):
            PROJ_AT[(hd, min(2 * j, N_LV - 3))] = PROJ_AT.get((hd, min(2 * j, N_LV - 3)), []) + [PROJ[first + j]]

    def last_use(i):
        hd, lv = ITEMS[i]
        if lv == LV_CTX:
            return ("kt", hd)
        if lv == LV_STATE:
            return ("o", hd, CL - 1)
        if lv == LEVELS + 2:
            return ("att", i, 1)
        return ("att", i, 0)

    def buffer_free(eng, i):
        if i >= 3 and ITEMS[i - 3][1] != 0:
            filled(eng, last_use(i - 3))

    def scaled_items(i):
        return sum(1 for q in range(i + 1) if ITEMS[q][1] != 0)

    def arg_items(i):
        return sum(1 for q in range(i + 1) if ITEMS[q][1] not in (0, LV_STATE))

    plan = PsumPlan()

    def filled(eng, name):
        eng.wait_ge(psum_filled, plan.of[name][1])

    def evacuated(eng, name):
        b, _, used = plan.of[name]
        eng.wait_ge(psum_drained[b], used + 1)

    def drained(name):
        return psum_drained[plan.of[name][0]]

    def res(name):
        return psum[plan.of[name][0]]

    def unit_landed(eng, name):
        s, k = units.of[name]
        eng.wait_ge(landed[s], 16 * (k + 1))

    def unit(name):
        return slot(units.of[name][0])

    def made(eng, n):
        i, f = CHUNKS[n - 1]
        eng.wait_ge(products, 2 * n)
        evacuated(eng, ("x", 0, i, f))
        evacuated(eng, ("x", 1, i, f))

    STREAMS = [("lat", 0, LAT, 0), ("ctx", 1, CTX, LAT)]

    STEPS = [(s, half, o) for s in (0, 1) for half in (0, 1) for o in (0, 1)]
    last_step = len(STEPS) - 1
    CHUNKS = [(i, f) for i, (s, _, _) in enumerate(STEPS) for f in range((CL, CC)[s])]

    filt_u = slot(units.of[("filt", 0)][0])
    w4 = filt_u[:, 0:2 * D].rearrange("p (o c) -> p o c", o=2)
    c_small = filt_u[:, 2 * D:].rearrange("p (i a c n) -> p i a c n", i=2, a=2, c=CC)
    dft = slot(units.of[("dft", 0)][0]).rearrange("p (a c n) -> p a c n", a=2, c=CL)
    idft = slot(units.of[("idft", 0)][0]).rearrange("p (a c n) -> p a c n", a=2, c=CL)

    def basis(s, inverse, a):
        if s:
            return c_small[:, inverse, a]
        return (idft if inverse else dft)[:, a]

    block = ctx.enter_context(nc.Block())

    @block.tensor
    def _(pe):
        def begin(name, bank=None):
            b, _, used = plan.add(name, bank)
            if used:
                pe.wait_ge(psum_drained[b], used)
            return psum[b]

        def turn(dst, src, n=P):
            return pe.transpose(dst, src, ident[0:n, 0:n])

        def cond_columns():
            pe.wait_ge(keep_in, 32)
            pe.wait_ge(cond_silu, 1)
            turn(begin("cond_T", 6)[:, 0:16], cond_rows[:, :], 16).then_inc(psum_filled, 1)
            pe.wait_ge(small_in, 16 * 4)
            turn(begin("small_T", 7)[:, 0:P], small_rows[:, :]).then_inc(psum_filled, 1)

        def modulation():
            evacuated(pe, "cond_T")
            with pe.Fori(0, N_MOD // SLOTS) as i:
                for u in range(SLOTS):
                    pe.wait_ge(landed[u], 16 * i + 16)
                    pe.wait_ge(mod_drained, SLOTS * i + u + 1)
                    w = slot(u).rearrange("p (k c) -> p k c", k=KD)
                    for k in range(KD):
                        for q in range(4):
                            mm = pe.matmul(psum[u][32 * q:32 * q + 32, 0:P], s_cols[:, k, :],
                                           w[:, k, P * q:P * q + P], start=(k == 0), stop=(k == KD - 1))
                    mm.then_inc(mod_filled, 1)
            pe.wait_ge(mod_drained, N_MOD + SLOTS)
            pe.wait_ge(mod_back, 64)
            for l in range(2):
                turn(begin(("mod_T", l), l)[:, 0:96], mod_rows[:, l, :], 96).then_inc(psum_filled, 1)

        def modulated_columns():
            pe.wait_ge(pe_added, 1)
            for k in range(KD):
                b = begin(("aT0", 0, k))
                for c in range(CL):
                    mm = turn(b[:, P * c:P * c + P], x_rows[:, c, P * k:P * k + P])
                mm.then_inc(psum_filled, 1)
            pe.wait_ge(ctx_in, 16)
            for k in range(KD):
                b = begin(("aT0", 1, k))
                for c in range(CC):
                    mm = turn(b[:, P * c:P * c + P], x_rows[:, CL + c, P * k:P * k + P])
                mm.then_inc(psum_filled, 1)

        def filter_mlp(j):
            w = (f_w1, f_w2, f_w3)[j]
            x = (zT, hf1, hf2)[j]
            m = 2 * HF if j == 2 else HF
            if j == 0:
                pe.wait_ge(fw_in, 16 * 9)
            else:
                pe.wait_ge(sin_done, j)
            for _, s, n, o in STREAMS:
                pe.matmul(begin(("mlp", j, s))[0:m, 0:n], w, x[:, o:o + n],
                          start=True, stop=True).then_inc(psum_filled, 1)

        def project(ch):
            j, cc = ch // 4, ch % 4
            if ch == 0:
                evacuated(pe, ("aT0", 1, KD - 1))
                evacuated(pe, ("aT0", 0, KD - 1))
            if cc == 0:
                unit_landed(pe, ("hy_in", j))
            w = unit(("hy_in", j)).rearrange("p (k c) -> p k c", k=KD)
            for _, s, n, o in STREAMS:
                b = begin(("proj", s, ch))
                for k in range(KD):
                    mm = pe.matmul(b[:, 0:n], w[:, k, P * cc:P * cc + P], aT[:, k, o:o + n],
                                   start=(k == 0), stop=(k == KD - 1))
                mm.then_inc(psum_filled, 1)

        def token_major(ch):
            pe.wait_ge(conv_done, ch + 1)
            for _, s, n, o in STREAMS:
                b = begin(("tm", s, ch))
                for c in range(n // P):
                    mm = turn(b[:, P * c:P * c + P], zc[ch % 2][:, o + P * c:o + P * c + P])
                mm.then_inc(psum_filled, 1)

        def filters(i):
            s, half, o = STEPS[i]
            if i == 0:
                pe.wait_ge(hf_done, 1)
                pe.wait_ge(filt_in, 48)
            for tc in range((CL, CC)[s]):
                for a, hf in enumerate((hf_sum, hf_diff)):
                    col = LAT * s + P * tc
                    pe.matmul(begin(("filt", i, tc, a))[:, :], hf[:, col:col + P],
                              w4[:, o, COL * half:COL * half + COL],
                              start=True, stop=True).then_inc(psum_filled, 1)

        def spectra(i):
            s, half, o = STEPS[i]
            n = (CL, CC)[s]
            pe.wait_ge(skip_added, i + 1)
            for a in (0, 1):
                evacuated(pe, ("filt", i, n - 1, a))
            if i == 0:
                unit_landed(pe, ("dft", 0))
            for f in range(n):
                parts = [("k", 0, filt[0]), ("k", 1, filt[1])] + [("ny", 1, filt[0])] * (f == 0)
                for name, a, src in parts:
                    b = begin((name, a, i, f))
                    m = 1 if name == "ny" else P
                    for c in range(n):
                        mm = pe.matmul(b[0:m, :], basis(s, 0, a)[:, c, P * f:P * f + m], src[:, c, :],
                                       start=(c == 0), stop=(c == n - 1))
                    mm.then_inc(psum_filled, 1)
                if f == 0:
                    if o:
                        evacuated(pe, ("y", i - 1, n - 1))
                    elif i == 0:
                        evacuated(pe, ("tm", 0, 15))
                        evacuated(pe, ("tm", 1, 15))
                for a in (0, 1):
                    b = begin(("x", a, i, f))
                    for c in range(n):
                        mm = pe.matmul(b[:, :], basis(s, 0, a)[:, c, P * f:P * f + P],
                                       v_t[:, CL * s + c, COL * half:COL * half + COL],
                                       start=(c == 0), stop=(c == n - 1))
                    mm.then_inc(psum_filled, 1)

        def inverse(i):
            s, half, o = STEPS[i]
            n = (CL, CC)[s]
            base = sum((CL, CC)[q] for q, _, _ in STEPS[:i])
            pe.wait_ge(z_ready, 2 * (base + n))
            if i == 0:
                unit_landed(pe, ("idft", 0))
            if o == 0:
                for c in range(n):
                    b = begin(("y", i, c))
                    for f in range(n):
                        for a, z in enumerate((z_re, z_im)):
                            mm = pe.matmul(b[:, :], basis(s, 1, a)[:, f, P * c:P * c + P], z[:, f, :],
                                           start=(f == 0 and a == 0), stop=(f == n - 1 and a == 1))
                    mm.then_inc(psum_filled, 1)
            else:
                for cc in range(4):
                    b = begin(("y", i, cc))
                    for f in range(n):
                        for a, z in enumerate((z_re, z_im)):
                            mm = pe.matmul(b[:, 0:n * P], z[:, f, P * cc:P * cc + P], basis(s, 1, a)[:, f, :],
                                           start=(f == 0 and a == 0), stop=(f == n - 1 and a == 1))
                    mm.then_inc(psum_filled, 1)

        cond_columns()
        modulation()
        filter_mlp(0)
        modulated_columns()
        for ch in range(24):
            project(ch)
            if ch in (1, 3):
                filter_mlp((ch + 1) // 2)
            if 1 <= ch <= 16:
                token_major(ch - 1)
        filters(0)
        for i in range(len(STEPS)):
            spectra(i)
            if i < last_step:
                filters(i + 1)
            inverse(i)

        def out_project(l, c):
            src = mixed[l]
            w = ("hy_out", "gla_out")[l]
            for half in (0, 1):
                if c == 0:
                    unit_landed(pe, (w, half))
                b = begin(("out", l, c, half))
                wt = unit((w, half)).rearrange("p (k c) -> p k c", k=KD)
                for k in range(KD):
                    mm = pe.matmul(b[:, :], src[:, k, P * c:P * c + P], wt[:, k, :],
                                   start=(k == 0), stop=(k == KD - 1))
                mm.then_inc(psum_filled, 1)

        def route_logits(l, c):
            g = gchunk(l, c)
            pe.wait_ge(a2_done, g + 1)
            for h in (0, 1):
                b = begin(("a2T", l, c, h))
                for k in range(4):
                    mm = turn(b[:, P * k:P * k + P], a2[c % 2][:, P * (4 * h + k):P * (4 * h + k) + P])
                mm.then_inc(psum_filled, 1)
            for h in (0, 1):
                evacuated(pe, ("a2T", l, c, h))
            if c == 0 and l == 0:
                pe.wait_ge(route_in, 48)
            b = begin(("logit", l, c))
            for k in range(KD):
                mm = pe.matmul(b[:, 0:E_N], a2T[:, k, :], router_w[:, k, :],
                               start=(k == 0), stop=(k == KD - 1))
            mm.then_inc(psum_filled, 1)

        def ranks(l):
            n = len(CHUNKS_OF[l])
            pe.wait_ge(picked, l + 1)
            chosen = temps[7]
            b = begin(("rank", l))
            for c in range(n):
                for q in range(c + 1):
                    mm = pe.matmul(b[:, E_N * c:E_N * c + E_N], before if q == 0 else ones,
                              chosen[:, E_N * (c - q):E_N * (c - q) + E_N], start=(q == 0), stop=(q == c))
            mm.then_inc(psum_filled, 1)
            b = begin(("count", l))
            for c in range(n):
                mm = pe.matmul(b[:, 0:E_N], ones, chosen[:, E_N * c:E_N * c + E_N],
                               start=(c == 0), stop=(c == n - 1))
            mm.then_inc(psum_filled, 1)

        def slot_table(l):
            nb = blocks_max((NT, LAT)[l]) + 1
            pe.wait_ge(slots_back, 16 * (l + 1))
            turn(begin(("slots", l))[0:SB, 0:nb], slot_rows[0:nb, :], nb).then_inc(psum_filled, 1)

        def experts(l):
            pX, pG, pH, pY = psum[0], psum[1:3], psum[3:5], psum[5]
            for b in range(6):
                if plan.used[b]:
                    pe.wait_ge(psum_drained[b], plan.used[b])
            pe.wait_ge(starts_done, l + 1)

            def turn_rows():
                for k in range(KD):
                    mm = turn(pX[:, SB * k:SB * k + SB], x_slots[:, P * k:P * k + P], SB)
                mm.then_inc(x_turned[l], 1)

            pe.wait_ge(x_landed[l], 16)
            turn_rows()
            with pe.Fori(0, E_N // 2) as pair:
                for par in (0, 1):
                    lo = pe.value_load(starts[:, ds(2 * pair + par, 1)], min_val=0, max_val=blocks_max(NT))
                    hi = pe.value_load(starts[:, ds(2 * pair + par + 1, 1)], min_val=1, max_val=blocks_max(NT))
                    s = 3 * par
                    w13 = ring[:, s * UNIT:(s + 2) * UNIT].rearrange("p (m k c) -> p m k c", m=2, k=KD)
                    w2 = slot(s + 2).rearrange("p (f c) -> p f c", f=4)
                    with pe.Fori(lo, hi) as b:
                        for q in range(3):
                            pe.wait_ge(landed[s + q], 16 * pair + 16 * (moe_first[l][s + q] + 1))
                        pe.wait_ge(xT_done[l], b + 1)
                        for c in (0, 1):
                            for k in range(KD):
                                for half in (0, 1):
                                    col = 256 * half + P * c
                                    mm = pe.matmul(pG[c][SB * half:SB * half + SB, 0:256].rearrange(
                                        "p (m c) -> p m c", m=2), xT[:, k, :], w13[:, :, k, col:col + P],
                                        start=(k == 0), stop=(k == KD - 1))
                            mm.then_inc(up_filled[l], 1)
                        pe.wait_ge(x_landed[l], 16 * b + 32)
                        pe.wait_ge(hid_done[l], 2 * b + 1)
                        turn(pH[0][:, 0:P], hid[0]).then_inc(hid_turned[l], 1)
                        turn_rows()
                        pe.wait_ge(hid_done[l], 2 * b + 2)
                        turn(pH[1][:, 0:P], hid[1]).then_inc(hid_turned[l], 1)
                        pe.wait_ge(y_copied[l], b + 1)
                        for c in (0, 1):
                            pe.wait_ge(hidT_done[l], 2 * b + c + 1)
                            for f in (0, 1):
                                for half in (0, 1):
                                    mm = pe.matmul(pY[SB * half:SB * half + SB, :],
                                                   hidT[c][:, SB * f:SB * f + SB],
                                                   w2[:, 2 * f + c, COL * half:COL * half + COL],
                                                   start=(c == 0 and f == 0), stop=(c == 1 and f == 1))
                        mm.then_inc(y_filled[l], 1)
            total = pe.value_load(starts[:, E_N:E_N + 1], min_val=1, max_val=blocks_max(NT))
            pe.wait_ge(xT_done[l], total + 1)
            pe.wait_ge(y_copied[l], total + 1)
            pe.wait_ge(starts_done, l + 1)

        def finish(l):
            last = len(CHUNKS_OF[l]) - 1
            for c in CHUNKS_OF[l]:
                out_project(l, c)
                if c:
                    route_logits(l, c - 1)
            route_logits(l, last)
            ranks(l)
            slot_table(l)
            experts(l)

        evacuated(pe, ("y", last_step, 3))
        finish(0)

        def columns1():
            pe.wait_ge(h_next, 6)
            for s, chunks in ((0, range(CL)), (1, range(CL, 6))):
                for k in range(KD):
                    b = begin(("aT1", s, k))
                    for i, c in enumerate(chunks):
                        mm = turn(b[:, P * i:P * i + P], h_rows[:, c, P * k:P * k + P])
                    mm.then_inc(psum_filled, 1)

        def low_rank():
            pe.wait_ge(gla_in, 16 * 4)
            for s in (0, 1):
                for k in range(KD):
                    evacuated(pe, ("aT1", s, k))
            for _, s, n, o in STREAMS:
                b = begin(("lr", s))
                for k in range(KD):
                    mm = pe.matmul(b[0:32, 0:n], lr_w[:, k, :], aT_l[1][:, k, o:o + n],
                                   start=(k == 0), stop=(k == KD - 1))
                mm.then_inc(psum_filled, 1)

        def gates(hd):
            if hd == 0:
                evacuated(pe, ("lr", 0))
                evacuated(pe, ("lr", 1))
                pe.wait_ge(zero_w, 1)
            for r in (0, 1):
                for _, s, n, o in STREAMS:
                    pe.matmul(begin(("g", hd, r, s))[:, 0:n], gate_w[r][:, P * hd:P * hd + P], lrT[:, o:o + n],
                              start=True, stop=True).then_inc(psum_filled, 1)

        def queries_keys():
            for m in (0, 1):
                unit_landed(pe, ("gla_in", m))
                w = unit(("gla_in", m)).rearrange("p (k c) -> p k c", k=KD)
                for hd in range(HEADS):
                    for _, s, n, o in STREAMS[:1 + m]:
                        b = begin(("qk", m, hd, s))
                        for k in range(KD):
                            mm = pe.matmul(b[:, 0:n], w[:, k, P * hd:P * hd + P], aT_l[1][:, k, o:o + n],
                                           start=(k == 0), stop=(k == KD - 1))
                        mm.then_inc(psum_filled, 1)

        def value_gate(name):
            kind, half, c = name
            j = (2 if kind == "v" else 4) + half
            if c == 0:
                unit_landed(pe, ("gla_in", j))
            w = unit(("gla_in", j)).rearrange("p (k c) -> p k c", k=KD)
            b = begin(name)
            for k in range(KD):
                mm = pe.matmul(b[:, :], aT_l[1][:, k, P * c:P * c + P], w[:, k, :],
                               start=(k == 0), stop=(k == KD - 1))
            mm.then_inc(psum_filled, 1)

        def attention(i):
            hd, lv = ITEMS[i]
            if lv == 0:
                q, key = qk[:, hd, 0, :], qk[:, hd, 1, :]
                evacuated(pe, ("qk", 0, hd, 0))
                evacuated(pe, ("qk", 1, hd, 0))
            else:
                q, key = lev[i % 3][:, 0:LAT], lev[i % 3][:, LAT:2 * LAT]
                pe.wait_ge(scaled_qk, scaled_items(i))
            if lv <= LEVELS + 1:
                b = begin(("att", i, 0))
                for s in range(CL):
                    u = s if lv <= LEVELS else s ^ 1
                    mm = pe.matmul(b[:, P * s:P * s + P], key[:, P * s:P * s + P], q[:, P * u:P * u + P],
                                   start=True, stop=True)
                mm.then_inc(psum_filled, 1)
            elif lv == LEVELS + 2:
                for h in (0, 1):
                    b = begin(("att", i, h))
                    for s in (0, 1):
                        sb, u = 2 * h + s, 2 * (1 - h)
                        mm = pe.matmul(b[:, 2 * P * s:2 * P * s + 2 * P], key[:, P * sb:P * sb + P],
                                       q[:, P * u:P * u + 2 * P], start=True, stop=True)
                    mm.then_inc(psum_filled, 1)
            elif lv == LV_CTX:
                b = begin(("kt", hd))
                for j in range(4):
                    mm = turn(b[:, P * j:P * j + P], lev[i % 3][:, P * j:P * j + P])
                mm.then_inc(psum_filled, 1)
            else:
                context_state(hd)
                outputs(i, hd)

        def context_state(hd):
            evacuated(pe, ("kt", hd))
            for c in (CL, CL + 1):
                evacuated(pe, ("v", hd // 2, c))
            b = begin(("st", hd))
            for r in (0, 1):
                for c in range(CC):
                    mm = pe.matmul(b[:, DVH * r:DVH * r + DVH], kt_rows[:, P * (CC * r + c):P * (CC * r + c) + P],
                                   v_rows[:, CL + c, DVH * hd:DVH * hd + DVH], start=(c == 0), stop=(c == CC - 1))
            mm.then_inc(psum_filled, 1)

        def outputs(i, hd):
            q = lev[i % 3]
            evacuated(pe, ("st", hd))
            pe.wait_ge(near_done, LEVELS * (hd + 1))
            for s in range(CL):
                evacuated(pe, ("v", hd // 2, s))
            j = i - 2
            evacuated(pe, ("att", j - 1, 0))
            evacuated(pe, ("att", j - 2, 0))
            evacuated(pe, ("att", N_LV * hd, 0))
            for h in (0, 1):
                evacuated(pe, ("att", j, h))
            for u in range(CL):
                b = begin(("o", hd, u))
                for s in range(CL):
                    if s == u:
                        a = att_near[:, P * s:P * s + P]
                    elif s == u ^ 1:
                        a = att_next[:, P * s:P * s + P]
                    else:
                        a = att_far[:, 2 * P * s + P * (u % 2):2 * P * s + P * (u % 2) + P]
                    pe.matmul(b[:, 0:DVH], a, v_rows[:, s, DVH * hd:DVH * hd + DVH], start=(s == 0), stop=False)
                for r in (0, 1):
                    mm = pe.matmul(b[:, 0:DVH], q[:, LAT * r + P * u:LAT * r + P * u + P], state[:, r, :],
                                   start=False, stop=(r == 1))
                mm.then_inc(psum_filled, 1)

        def output_columns():
            pe.wait_ge(y_rows_done, CL)
            for k in range(KD):
                b = begin(("yT", k))
                for c in range(CL):
                    mm = turn(b[:, P * c:P * c + P], r_rows[:, c, P * k:P * k + P])
                mm.then_inc(psum_filled, 1)
            for k in range(KD):
                evacuated(pe, ("yT", k))

        columns1()
        low_rank()
        queries_keys()
        gates(0)
        for i, (hd, lv) in enumerate(ITEMS):
            for name in PROJ_AT.get((hd, lv), []):
                value_gate(name)
            attention(i)
            if lv == 5 and hd + 1 < HEADS:
                gates(hd + 1)
        output_columns()
        finish(1)

    @block.scalar
    def _(act):
        links = [0]

        def link(ins):
            ins.then_inc(act_link, 1)
            links[0] += 1
            act.wait_ge(act_link, links[0])

        def early_loads():
            act.dma_start(keep[:, 0:128], t["ident"]).then_inc(keep_in, 16)
            act.dma_start(cond_rows[0:8, :], t["c"].rearrange("b (k p) -> (b k) p", p=P)).then_inc(cond_in, 16)
            act.dma_start(cond_rows[8:16, :], t["c_ctx"].rearrange("(k p) -> k p", p=P)).then_inc(cond_in, 16)
            act.dma_start(keep[:, 1984:1987], t["marks"]).then_inc(keep_in, 16)
            act.dma_start(small_rows[0:72, :],
                          t["hy_conv_w"].rearrange("o j (c p) -> (o j c) p", p=P)).then_inc(small_in, 16)
            act.dma_start(small_rows[72:96, :],
                          t["hy_b_in"].rearrange("o (c p) -> (o c) p", p=P)).then_inc(small_in, 16)
            act.dma_start(small_rows[96:120, :],
                          t["hy_conv_b"].rearrange("o (c p) -> (o c) p", p=P)).then_inc(small_in, 16)
            act.dma_start(small_rows[120:128, :],
                          t["gla_b_gate"].rearrange("o r (c p) -> (o r c) p", p=P)).then_inc(small_in, 16)
            act.wait_ge(mod_zeroed, 1)
            bias = t["b_mod"].rearrange("l (n q c) -> q (l n) c", q=4, c=P)
            for q in range(4):
                for r in range(2):
                    act.dma_start(mod_acc[32 * q + r:32 * q + r + 1, :, :],
                                  bias[q:q + 1]).then_inc(bias_in, 16)
            act.dma_start(x_rows[:, 0:CL, :],
                          t["x"].rearrange("b (c p) d -> p (b c) d", p=P)).then_inc(x_in, 16)
            act.dma_start(pe_rows, t["pos"].rearrange("(c p) d -> p c d", p=P)).then_inc(pe_in, 16)
            act.dma_start(x_rows[:, CL:6, :],
                          t["ctx"].rearrange("b (c p) d -> p (b c) d", p=P)).then_inc(ctx_in, 16)
            act.dma_start(zT, t["zT"]).then_inc(fw_in, 16)
            act.dma_start(f_w1, t["hy_f_w1"][0]).then_inc(fw_in, 16)
            act.dma_start(f_w2, t["hy_f_w2"][0]).then_inc(fw_in, 16)
            for i in (0, 1):
                act.dma_start(f_w3[:, HF * i:HF * i + HF], t["hy_f_w3"][0]).then_inc(fw_in, 16)
            act.dma_start(f_b[0:HF, 0:1], t["hy_f_b1"].rearrange("o p -> p o")).then_inc(fw_in, 16)
            act.dma_start(f_b[0:HF, 1:2], t["hy_f_b2"].rearrange("o p -> p o")).then_inc(fw_in, 16)
            for i in (0, 1):
                act.dma_start(f_b[HF * i:HF * i + HF, 2:3],
                              t["hy_f_b3"].rearrange("o p -> p o")).then_inc(fw_in, 16)

        def cond():
            act.wait_ge(cond_in, 32)
            act.activation(cond_rows, cond_rows, ACT.Silu).then_inc(cond_silu, 1)

        def store_mod():
            act.wait_ge(mod_drained, N_MOD + SLOTS)
            for q in range(4):
                act.dma_start(mod_d[:, :, q, :], mod_acc[32 * q:32 * q + 2, :, :]).then_inc(mod_stored, 16)
            act.wait_ge(mod_stored, 64)
            for l in range(2):
                for r in range(2):
                    rows = mod_d[r, 12 * l:12 * l + 12].rearrange("n q c -> (n q) c")
                    act.dma_start(mod_rows[48 * r:48 * r + 48, l, :], rows).then_inc(mod_back, 16)

        def store_h0():
            act.wait_ge(pe_added, 1)
            act.dma_start(h0_d.rearrange("(c p) d -> p c d", p=P), x_rows[:, 0:CL, :]).then_inc(h0_stored, 16)

        def sines(j):
            m = 2 * HF if j == 2 else HF
            dst = (hf1, hf2, hf_sum)[j]
            act.wait_ge(sin_arg, j + 1)
            act.activation(dst[0:m, :], arg_u[0:m, :], ACT.Sin).then_inc(sin_done, 1)

        def biased(ch):
            if ch == 0:
                act.wait_ge(edges_zeroed, 4)
                evacuated(act, "small_T")
            if ch >= 2:
                act.wait_ge(conv_done, ch - 1)
            tap = taps[ch % 2]
            for _, s, n, o in STREAMS:
                name = ("proj", s, ch)
                filled(act, name)
                lo = 1 + s * (LAT + 2)
                act.activation(tap[:, lo:lo + n], res(name)[:, 0:n], ACT.Identity,
                               bias=b_in(ch)).then_inc(drained(name), 1)

        def gather_rows(ch):
            if ch == 0:
                act.wait_ge(h0_stored, 16)
            dst = (v_t, x1_t)[ch // 8]
            for _, s, n, o in STREAMS:
                name = ("tm", s, ch)
                filled(act, name)
                act.copy(dst[:, CL * s:CL * s + n // P, P * (ch % 8):P * (ch % 8) + P],
                         res(name)[:, 0:n].rearrange("p (c x) -> p c x", x=P)).then_inc(drained(name), 1)

        def load_windows(i):
            s, half, o = STEPS[i]
            n = (CL, CC)[s]
            if i == 0:
                filled(act, ("proj", 1, 23))
            if i:
                act.wait_ge(skip_added, i)
            act.dma_start(skip_row, t["hy_skip"][0, o:o + 1, COL * half:COL * half + COL]).then_inc(skip_in, 16)
            for tc in range(n):
                g = win_loads[0]
                if g >= 2:
                    evacuated(act, win_use[g - 2])
                act.dma_start(win[g % 2], t[("window_lat", "window_ctx")[s]][
                    P * tc:P * tc + P, COL * half:COL * half + COL]).then_inc(win_in[g % 2], 16)
                win_loads[0] += 1

        win_loads = [0]
        win_use = [("filt", i, tc, 1) for i in range(len(STEPS)) for tc in range((CL, CC)[STEPS[i][0]])]

        def keep_spectra(i):
            s, half, o = STEPS[i]
            n = (CL, CC)[s]
            base = sum((CL, CC)[q] for q, _, _ in STEPS[:i])
            for f in range(n):
                if base + f:
                    made(act, base + f)
                if i == 0 and f == 0:
                    filled(act, ("proj", 1, 23))
                filled(act, ("k", 0, i, f))
                act.copy(k_re, res(("k", 0, i, f))[:, :]).then_inc(drained(("k", 0, i, f)), 1)
                filled(act, ("k", 1, i, f))
                if f:
                    act.copy(k_im, res(("k", 1, i, f))[:, :]).then_inc(drained(("k", 1, i, f)), 1)
                else:
                    act.activation(k_im, res(("k", 1, i, f))[:, :], ACT.Copy,
                                   scale=rowmask).then_inc(drained(("k", 1, i, f)), 1)
                    evacuated(act, ("k", 0, i, f))
                    link(act.copy(k_ny, k_re))
                    filled(act, ("ny", 1, i, f))
                    act.copy(k_ny[0:1, :], res(("ny", 1, i, f))[0:1, :]).then_inc(drained(("ny", 1, i, f)), 1)

        early_loads()
        cond()
        store_h0()
        store_mod()
        for ch in range(24):
            if ch == 2:
                sines(1)
            if ch == 4:
                sines(2)
            if ch == 0:
                sines(0)
            biased(ch)
            if 1 <= ch <= 16:
                gather_rows(ch - 1)
        load_windows(0)
        for i in range(len(STEPS)):
            keep_spectra(i)
            if i < last_step:
                load_windows(i + 1)

        def load_vectors(l):
            def put(dst, row):
                act.dma_start(dst, row.partition_broadcast(P)).then_inc(bc_in, 16)

            def mod_row(r, v):
                return mod_d[r, 12 * l + 2 * v:12 * l + 2 * v + 2].rearrange("n q c -> (n q c)")

            vec = {"lng": t["ln_g"][l, 0], "lnb": t["ln_b"][l, 0], "g1l": mod_row(0, 2), "sh2l": mod_row(0, 3),
                   "sc2l": mod_row(0, 4)}
            if l == 0:
                vec.update({"bout": t["hy_b_out"][0], "g1c": mod_row(1, 2), "sh2c": mod_row(1, 3),
                            "sc2c": mod_row(1, 4)})
            for n in BC[l]:
                put(bcast[l][n], vec[n])

        def load_vectors2(l):
            def mod_row(r, v):
                return mod_d[r, 12 * l + 2 * v:12 * l + 2 * v + 2].rearrange("n q c -> (n q c)")

            for n, row in (("g2l", mod_row(0, 5)), ("g2c", mod_row(1, 5)), ("lng", t["ln_g"][l, 1]),
                           ("lnb", t["ln_b"][l, 1])):
                act.dma_start(bc2[n], row.partition_broadcast(P)).then_inc(bc2_in[0], 16)

        def load_router():
            filled(act, ("filt", last_step, CC - 1, 1))
            act.dma_start(router_w, t["router_w"].rearrange("(k p) e -> p k e", p=P)).then_inc(route_in, 16)
            act.dma_start(router_b, t["router_b"].partition_broadcast(P)).then_inc(route_in, 16)
            act.dma_start(keep[:, 416:690], t["route_c"]).then_inc(route_in, 16)

        def load_resid(l, c):
            if gchunk(l, c):
                act.wait_ge(res_used, gchunk(l, c))
            src = (h0_d, h1_d)[l][P * c:P * c + P] if c < CL else t["ctx"][0, P * (c - CL):P * (c - CL) + P]
            act.dma_start(resid, src).then_inc(res_in, 16)

        def deviation(n):
            act.wait_ge(var_ready, n)
            act.activation(dev, mean_var[:, 1:2], ACT.Sqrt, bias=eps).then_inc(dev_done, 1)

        def store_tokens(l, c):
            act.wait_ge(a2_done, gchunk(l, c) + 1)
            act.dma_start(tok_l[l][P * c:P * c + P], a2[c % 2]).then_inc(tok_stored, 16)

        def route_scores(l, c):
            for h in (0, 1):
                filled(act, ("a2T", l, c, h))
                act.copy(a2T[:, 4 * h:4 * h + 4, :], res(("a2T", l, c, h))[:, :].rearrange(
                    "p (k n) -> p k n", k=4)).then_inc(drained(("a2T", l, c, h)), 1)
            filled(act, ("logit", l, c))
            act.activation(scores[:, E_N * c:E_N * c + E_N], res(("logit", l, c))[:, 0:E_N],
                           ACT.Sigmoid).then_inc(drained(("logit", l, c)), 1)

        def clear_slots(l):
            act.wait_ge(slot_zero, l + 1)
            nb = blocks_max((NT, LAT)[l]) + 1
            act.dma_start(slot_l[l].rearrange("(b s) o -> b (s o)", s=SB), slot_rows[0:nb, :]).then_inc(slot_cleared, 16)

        def read_slots(l):
            n = 2 * (len(CHUNKS_OF[0]) if l == 0 else len(CHUNKS_OF[0]) + len(CHUNKS_OF[1]))
            act.wait_ge(scattered, 16 * n)
            nb = blocks_max((NT, LAT)[l]) + 1
            act.dma_start(slot_rows[0:nb, :], slot_l[l].rearrange("(b s) o -> b (s o)", s=SB)).then_inc(slots_back, 16)

        def experts(l):
            pG, pY = psum[1:3], psum[5]
            act.wait_ge(starts_done, l + 1)
            total = act.value_load(starts[:, E_N:E_N + 1], min_val=1, max_val=blocks_max(NT))
            with act.Fori(0, total) as b:
                for c in (0, 1):
                    act.wait_ge(up_filled[l], 2 * b + c + 1)
                    act.activation(gate_act[c], pG[c][:, 0:P], ACT.Silu).then_inc(gate_done[l], 1)
                act.wait_ge(y_stored[l], 32 * b + 32)
                act.wait_ge(y_filled[l], b + 1)
                act.copy(y_out, pY[:, :]).then_inc(y_copied[l], 1)
                act.wait_ge(y_copied[l], b + 2)
                rows = y_d.rearrange("(b s) d -> b s d", s=SB)[ds(b, 1)].rearrange("o s d -> (o s) d")
                for half in (0, 1):
                    act.dma_start(rows[:, COL * half:COL * half + COL],
                                  y_out[SB * half:SB * half + SB, :]).then_inc(y_stored[l], 16)

        def finish(l):
            chunks = CHUNKS_OF[l]
            for c in chunks:
                load_resid(l, c)
                deviation(gchunk(l, c) + 1 + 6 * l)
                if c:
                    route_scores(l, c - 1)
                store_tokens(l, c)
            route_scores(l, chunks[-1])
            clear_slots(l)
            read_slots(l)
            load_vectors2(l)
            experts(l)
            for c in chunks:
                deviation(gchunk(l, c) + 1 + len(CHUNKS_OF[0]) + (len(CHUNKS_OF[1]) if l else 0))
                if l:
                    act.wait_ge(h_next, gchunk(l, c) + 1)
                    act.dma_start(out[0, P * c:P * c + P], h_rows[:, c, :]).then_inc(out_stored, 16)

        load_router()
        filled(act, ("x", 1, last_step, CC - 1))
        evacuated(act, ("y", last_step - 1, CC - 1))
        load_vectors(0)
        filled(act, ("y", last_step, 3))
        finish(0)

        def spill():
            for c in range(CL):
                act.wait_ge(h_next, c + 1)
                act.dma_start(h1_d[P * c:P * c + P], h_rows[:, c, :]).then_inc(h1_stored, 16)

        def load_gla():
            filled(act, ("aT1", 1, KD - 1))
            act.dma_start(lr_w, t["gla_w_in"][0, :, 3072:3104].rearrange("(k p) c -> p k c", p=P)).then_inc(gla_in, 16)
            act.wait_ge(zero_w, 2)
            for r in (0, 1):
                act.dma_start(gate_w[r][16 * r:16 * r + 16, :], t["gla_w_gate"][0, r]).then_inc(gla_in, 16)
            act.dma_start(masks, t["masks"].rearrange("p (l n) -> p l n", n=P)).then_inc(gla_in, 16)
            for _, s, n, o in STREAMS:
                filled(act, ("lr", s))
                act.copy(lrT[:, o:o + n], res(("lr", s))[0:32, 0:n]).then_inc(drained(("lr", s)), 1)

        def gates(hd):
            for r in (0, 1):
                n_dir = 2 * hd + r
                if n_dir:
                    act.wait_ge(cum_done, 2 * n_dir)
                for _, s, n, o in STREAMS:
                    filled(act, ("g", hd, r, s))
                    act.activation(soft[:, o:o + n], res(("g", hd, r, s))[:, 0:n], ACT.Abs,
                                   bias=smallT[:, 120 + 4 * r + hd:121 + 4 * r + hd]).then_inc(gates_abs, 1)
                act.wait_ge(gates_abs, 2 * n_dir + 2)
                link(act.activation(soft, soft, ACT.Exp, scale=-1.0))
                act.activation(soft, soft, ACT.Ln, bias=1.0).then_inc(gates_ln, 1)

        def evac_qk():
            for m in (0, 1):
                for hd in range(HEADS):
                    for _, s, n, o in STREAMS[:1 + m]:
                        name = ("qk", m, hd, s)
                        filled(act, name)
                        dst = k_ctx[:, hd, :] if s else qk[:, hd, m, :]
                        act.activation(dst, res(name)[:, 0:n], ACT.Copy,
                                       scale=(1.0 if m else float(DKH) ** -0.5)).then_inc(drained(name), 1)

        def evac_value(name):
            kind, half, c = name
            dst = (v_rows if kind == "v" else r_rows)[:, c, COL * half:COL * half + COL]
            if kind == "r" and half == 0 and c == 0:
                act.wait_ge(h1_stored, 16 * CL)
            filled(act, name)
            act.copy(dst, res(name)[:, :]).then_inc(drained(name), 1)

        def exponentials(i):
            hd, lv = ITEMS[i]
            if lv == 0:
                return
            if lv == LV_STATE:
                buffer_free(act, i)
                act.activation(lev[i % 3].rearrange("p (r n) -> p r n", r=2), cums[hd % 2][:, :, 0:LAT],
                               ACT.Exp, scale=1.0 / TAU).then_inc(exps_done, 1)
            else:
                n = 2 * CTX if lv == LV_CTX else 2 * LAT
                act.wait_ge(args_done, arg_items(i))
                act.activation(lev[i % 3][:, 0:n], lev[i % 3][:, 0:n], ACT.Exp,
                               scale=1.0 / TAU).then_inc(exps_done, 1)

        def after_item(i):
            hd, lv = ITEMS[i]
            if lv == LEVELS + 2:
                for h in (0, 1):
                    filled(act, ("att", i, h))
                    act.copy(att_far[:, COL * h:COL * h + COL], res(("att", i, h))[:, :]).then_inc(
                        drained(("att", i, h)), 1)
            if lv == LV_CTX:
                filled(act, ("kt", hd))
                act.copy(kt_rows, res(("kt", hd))[:, :]).then_inc(drained(("kt", hd)), 1)
            if lv == LV_STATE:
                filled(act, ("st", hd))
                act.copy(state.rearrange("p r n -> p (r n)"), res(("st", hd))[:, :]).then_inc(drained(("st", hd)), 1)

        def head_deviation(hd):
            act.wait_ge(o_var, CL * (hd + 1))
            act.activation(g_dev, g_mv[:, :, 1], ACT.Sqrt, bias=eps).then_inc(o_dev, 1)

        def gla_tail():
            for c in range(CL):
                for half in (0, 1):
                    evacuated(act, ("r", half, c))
                act.activation(r_rows[:, c, :], r_rows[:, c, :], ACT.Silu).then_inc(silu_done, 1)
            for k in range(0, KD, 2):
                filled(act, ("yT", k))
                act.copy(mixed[1][:, k, :], res(("yT", k))[:, :]).then_inc(drained(("yT", k)), 1)

        spill()
        load_gla()
        evac_qk()
        gates(0)
        exponentials(1)
        for i, (hd, lv) in enumerate(ITEMS):
            if i and i + 1 < len(ITEMS):
                exponentials(i + 1)
            for name in PROJ_AT.get((hd, lv), []):
                evac_value(name)
            after_item(i)
            if lv == 5 and hd + 1 < HEADS:
                gates(hd + 1)
            if lv == 2 and hd:
                head_deviation(hd - 1)
        head_deviation(HEADS - 1)
        filled(act, ("r", 1, CL - 1))
        act.dma_start(norm_g, t["gla_norm_g"][0].partition_broadcast(P)).then_inc(norm_in, 16)
        gla_tail()
        filled(act, ("o", HEADS - 1, CL - 1))
        load_vectors(1)
        finish(1)

    @block.vector
    def _(dve):
        links = [0]

        def link(ins):
            ins.then_inc(dve_link, 1)
            links[0] += 1
            dve.wait_ge(dve_link, links[0])

        def start():
            dve.memset(mod_acc, 0.0).then_inc(mod_zeroed, 1)
            dve.memset(s_cols, 0.0).then_inc(cols_zeroed, 1)
            filled(dve, "cond_T")
            dve.wait_ge(cols_zeroed, 1)
            dve.tensor_copy(s_cols[:, :, 0:2], res("cond_T")[:, 0:16].rearrange("p (r k) -> p k r", r=2)) \
               .then_inc(drained("cond_T"), 1)
            filled(dve, "small_T")
            dve.tensor_copy(smallT, res("small_T")[:, 0:P]).then_inc(drained("small_T"), 1)
            dve.memset(keep[:, 1987:1988], 0.0).then_inc(mod_drained, SLOTS)

        def modulation():
            dve.wait_ge(bias_in, 16 * 8)
            dve.wait_ge(mod_zeroed, 1)
            with dve.Fori(0, N_MOD // SLOTS) as i:
                for u in range(SLOTS):
                    dve.wait_ge(mod_filled, SLOTS * i + u + 1)
                    cols = mod_acc[:, ds(SLOTS * i + u, 1), :].rearrange("p o c -> p (o c)")
                    dve.tensor_tensor(cols, psum[u][:, 0:P], cols, ALU.add).then_inc(mod_drained, 1)
            for l in range(2):
                filled(dve, ("mod_T", l))
                dve.tensor_copy(modT[:, l], res(("mod_T", l))[:, 0:96].rearrange(
                    "p (r v k) -> p r v k", r=2, v=6)).then_inc(drained(("mod_T", l)), 1)
            evacuated(dve, ("mod_T", 0))
            evacuated(dve, ("mod_T", 1))
            for l in range(2):
                scale = modT[:, l, :, 1, :]
                dve.tensor_scalar(scale, scale, 1.0, None, ALU.add).then_inc(modT_done, 1)

        def modulated(l, names):
            dve.wait_ge(modT_done, 2)
            for s, k in names:
                name = (f"aT{l}", s, k)
                n, o = ((LAT, 0), (CTX, LAT))[s]
                filled(dve, name)
                dve.tensor_scalar(aT_l[l][:, k, o:o + n], res(name)[:, 0:n], modT[:, l, s, 1, k:k + 1],
                                  modT[:, l, s, 0, k:k + 1], ALU.mult, ALU.add).then_inc(drained(name), 1)

        def sine_argument(j):
            m = 2 * HF if j == 2 else HF
            u, r = arg_u[0:m, :], arg_t[0:m, :]
            if j == 0:
                dve.wait_ge(fw_in, 16 * 9)
            else:
                dve.wait_ge(sin_done, j)
            for _, s, n, o in STREAMS:
                name = ("mlp", j, s)
                filled(dve, name)
                dve.tensor_scalar(u[:, o:o + n], res(name)[0:m, 0:n], f_b[0:m, j:j + 1], None,
                                  ALU.add).then_inc(drained(name), 1)
            evacuated(dve, ("mlp", j, 0))
            evacuated(dve, ("mlp", j, 1))
            link(dve.tensor_scalar(r, u, float(1.0 / (2.0 * np.pi)), MAGIC, ALU.mult, ALU.add))
            link(dve.tensor_scalar(r, r, MAGIC, None, ALU.subtract))
            link(dve.scalar_tensor_tensor(u, r, -PI2_HI, u, ALU.mult, ALU.add))
            link(dve.scalar_tensor_tensor(u, r, -PI2_LO, u, ALU.mult, ALU.add))
            dve.tensor_scalar(u, u, 3.1415925, -3.1415925, ALU.min, ALU.max).then_inc(sin_arg, 1)

        def short_conv(ch):
            if ch == 0:
                dve.wait_ge(mod_stored, 64)
            if ch < 16:
                dst = zc[ch % 2]
                if ch >= 2:
                    filled(dve, ("tm", 1, ch - 2))
            else:
                dst = x2T[:, ch - 16, :]
                if ch == 16:
                    filled(dve, ("tm", 1, 15))
            parts = []
            for _, s, n, o in STREAMS:
                evacuated(dve, ("proj", s, ch))
                tap = taps[ch % 2][:, s * (LAT + 2):s * (LAT + 2) + n + 2]
                parts.append((dst[:, o:o + n], tap, n))
            for y, tap, n in parts:
                ins = dve.tensor_scalar(y, tap[:, 1:n + 1], conv_w(1, ch), conv_b(ch), ALU.mult, ALU.add)
                ins.then_inc(dve_link, 1)
                links[0] += 1
            dve.wait_ge(dve_link, links[0])
            for y, tap, n in parts:
                ins = dve.scalar_tensor_tensor(y, tap[:, 0:n], conv_w(0, ch), y, ALU.mult, ALU.add)
                ins.then_inc(dve_link, 1)
                links[0] += 1
            dve.wait_ge(dve_link, links[0])
            (y0, tap0, n0), (y1, tap1, n1) = parts
            ins = dve.scalar_tensor_tensor(y0, tap0[:, 2:n0 + 2], conv_w(2, ch), y0, ALU.mult, ALU.add)
            link(ins)
            dve.scalar_tensor_tensor(y1, tap1[:, 2:n1 + 2], conv_w(2, ch), y1, ALU.mult,
                                     ALU.add).then_inc(conv_done, 1)

        windows = [0]

        def windowed(i):
            s, half, o = STEPS[i]
            n = (CL, CC)[s]
            for tc in range(n):
                g = windows[0]
                dve.wait_ge(win_in[g % 2], 16 * (g // 2 + 1))
                for a in (0, 1):
                    name = ("filt", i, tc, a)
                    filled(dve, name)
                    dve.tensor_tensor(filt[a][:, tc, :], res(name)[:, :], win[g % 2],
                                      ALU.mult).then_inc(drained(name), 1)
                windows[0] += 1
            evacuated(dve, ("filt", i, 0, 0))
            dve.wait_ge(skip_in, 16 * (i + 1))
            dve.tensor_tensor(filt[0][0:1, 0, :], filt[0][0:1, 0, :], skip_row, ALU.add).then_inc(skip_added, 1)

        def multiply(i):
            s, half, o = STEPS[i]
            n = (CL, CC)[s]
            base = sum((CL, CC)[q] for q, _, _ in STEPS[:i])
            for f in range(n):
                for name in [("k", 0, i, f), ("k", 1, i, f)] + [("ny", 1, i, f)] * (f == 0):
                    evacuated(dve, name)
                if base + f:
                    dve.wait_ge(z_ready, 2 * (base + f))
                filled(dve, ("x", 0, i, f))
                dve.tensor_tensor(z_re[:, f, :], res(("x", 0, i, f))[:, :], k_re, ALU.mult).then_inc(products, 1)
                dve.tensor_tensor(z_im[:, f, :], res(("x", 0, i, f))[:, :], k_im,
                                  ALU.mult).then_inc(drained(("x", 0, i, f)), 1)
                filled(dve, ("x", 1, i, f))
                ny = k_re if f else k_ny
                dve.tensor_tensor(prod_a, res(("x", 1, i, f))[:, :], k_im, ALU.mult).then_inc(products, 1)
                dve.tensor_tensor(prod_b, res(("x", 1, i, f))[:, :], ny,
                                  ALU.mult).then_inc(drained(("x", 1, i, f)), 1)

        def gated(i):
            s, half, o = STEPS[i]
            n = (CL, CC)[s]
            if i == 0:
                evacuated(dve, ("tm", 0, 15))
                evacuated(dve, ("tm", 1, 15))
            if o == 0:
                for c in range(n):
                    name = ("y", i, c)
                    filled(dve, name)
                    cols = slice(COL * half, COL * half + COL)
                    dve.tensor_tensor(v_t[:, CL * s + c, cols], res(name)[:, :], x1_t[:, CL * s + c, cols],
                                      ALU.mult).then_inc(drained(name), 1)
            else:
                for cc in range(4):
                    name = ("y", i, cc)
                    filled(dve, name)
                    dst = x2T[:, 4 * half + cc, LAT * s:LAT * s + n * P]
                    dve.tensor_tensor(dst, res(name)[:, 0:n * P], dst, ALU.mult).then_inc(drained(name), 1)

        start()
        modulation()
        sine_argument(0)
        modulated(0, [(0, k) for k in range(KD)] + [(1, k) for k in range(KD)])
        for tap in taps:
            for c in (0, LAT + 1, LAT + 2, LAT + 3 + CTX):
                ins = dve.memset(tap[:, c:c + 1], 0.0)
                if c in (0, LAT + 3 + CTX):
                    ins.then_inc(edges_zeroed, 1)
        for ch in range(24):
            if ch == 2:
                sine_argument(1)
            if ch == 4:
                sine_argument(2)
                dve.wait_ge(sin_done, 3)
                dve.wait_ge(keep_in, 32)
                dve.tensor_scalar(hf_diff, hf_sum, sgn, None, ALU.mult).then_inc(hf_done, 1)
            short_conv(ch)
        filled(dve, ("proj", 1, 23))
        windowed(0)
        for i in range(len(STEPS)):
            multiply(i)
            if i < last_step:
                windowed(i + 1)
            gated(i)

        def normalise(n, h):
            for half in (0, 1):
                ins = dve.bn_stats(stats[:, half, :], h[:, COL * half:COL * half + COL])
            link(ins)
            if n > 1:
                dve.wait_ge(dev_done, n - 1)
            dve.bn_aggr(mean_var, stats).then_inc(var_ready, 1)
            dve.wait_ge(dev_done, n)
            link(dve.reciprocal(rdev, dev))
            dve.wait_ge(var_ready, n)
            dve.tensor_scalar(h, h, mean_var[:, 0:1], rdev, ALU.subtract, ALU.mult).then_inc(normed, 1)

        def residual(l, c):
            b = bcast[l]
            r = "l" if c < CL else "c"
            g = gchunk(l, c)
            if c == 0:
                dve.wait_ge(bc_in, 16 * (len(BC[0]) + (len(BC[1]) if l else 0)))
                for n in ("sc2l", "sc2c"):
                    if n in b:
                        dve.tensor_scalar(b[n], b[n], 1.0, None, ALU.add).then_inc(sc2_done, 1)
            dve.wait_ge(res_in, 16 * (g + 1))
            for half in (0, 1):
                cols = slice(COL * half, COL * half + COL)
                name = ("out", l, c, half)
                filled(dve, name)
                if l == 0:
                    dve.tensor_tensor(tmp[half], res(name)[:, :], b["bout"][:, cols],
                                      ALU.add).then_inc(drained(name), 1)
                    evacuated(dve, name)
                    link(dve.tensor_tensor(tmp[half], tmp[half], b["g1" + r][:, cols], ALU.mult))
                else:
                    dve.tensor_tensor(tmp[half], res(name)[:, :], b["g1" + r][:, cols],
                                      ALU.mult).then_inc(drained(name), 1)
                    evacuated(dve, name)
                ins = dve.scalar_tensor_tensor(h_rows[:, c, cols], resid[:, cols], ALPHA, tmp[half],
                                               ALU.mult, ALU.add)
                if half:
                    ins.then_inc(res_used, 1)
                else:
                    link(ins)
            dve.wait_ge(res_used, g + 1)

        def choose(l):
            n = len(CHUNKS_OF[l])
            w = n * E_N
            BIG = -1.0e30

            def t4(x):
                return x[:, 0:w].rearrange("p (c g e) -> p c g e", c=n, g=GRP)

            def t3(x):
                return x[:, 0:w].rearrange("p (c e) -> p c e", c=n)

            def g3(x, m=GRP):
                return x[:, 0:n * m].rearrange("p (c g) -> p c g", c=n)

            def over8(x):
                return g3(x).unsqueeze(3).broadcast_to([P, n, GRP, GSZ])

            S = scores
            biased, first, second, work, m1, m2, gs, chosen, pick, gm = temps[0:10]
            evacuated(dve, ("logit", l, n - 1))
            link(dve.tensor_tensor(t3(biased), t3(S), router_b.unsqueeze(1).broadcast_to([P, n, E_N]), ALU.add))

            def first_max(src, m, hot):
                link(dve.tensor_reduce(g3(m), t4(src), AX.X, ALU.max))
                link(dve.tensor_tensor(t4(work), t4(src), over8(m), ALU.is_equal))
                link(dve.tensor_tensor(t4(work), t4(work), ramp8.unsqueeze(1).unsqueeze(1).broadcast_to(
                    [P, n, GRP, GSZ]), ALU.mult))
                link(dve.tensor_reduce(g3(pick), t4(work), AX.X, ALU.max))
                link(dve.tensor_tensor(t4(hot), t4(work), over8(pick), ALU.is_equal))

            first_max(biased, m1, first)
            link(dve.scalar_tensor_tensor(biased[:, 0:w], first[:, 0:w], BIG, biased[:, 0:w], ALU.mult, ALU.add))
            first_max(biased, m2, second)
            link(dve.tensor_tensor(g3(gs), g3(m1), g3(m2), ALU.add))
            link(dve.tensor_reduce(gm[:, 0:n], g3(gs), AX.X, ALU.max))
            link(dve.tensor_tensor(g3(gs), g3(gs), gm[:, 0:n].unsqueeze(2).broadcast_to([P, n, GRP]), ALU.is_equal))
            link(dve.tensor_tensor(g3(gs), g3(gs), ramp4.unsqueeze(1).broadcast_to([P, n, GRP]), ALU.mult))
            link(dve.tensor_reduce(gm[:, 0:n], g3(gs), AX.X, ALU.max))
            link(dve.tensor_tensor(g3(gs), g3(gs), gm[:, 0:n].unsqueeze(2).broadcast_to([P, n, GRP]), ALU.is_equal))
            link(dve.tensor_tensor(t4(first), t4(first), over8(gs), ALU.mult))
            link(dve.tensor_tensor(t4(second), t4(second), over8(gs), ALU.mult))
            dve.tensor_tensor(chosen[:, 0:w], first[:, 0:w], second[:, 0:w], ALU.add).then_inc(picked, 1)

            for k, hot in enumerate((first, second)):
                link(dve.tensor_tensor(work[:, 0:w], S[:, 0:w], hot[:, 0:w], ALU.mult))
                link(dve.tensor_reduce(pair_w[:, k, 0:n], t3(work), AX.X, ALU.add))
            link(dve.tensor_tensor(gm[:, 0:n], pair_w[:, 0, 0:n], pair_w[:, 1, 0:n], ALU.add))
            link(dve.reciprocal(gm[:, 0:n], gm[:, 0:n]))
            for k in (0, 1):
                link(dve.tensor_tensor(pair_w[:, k, 0:n], pair_w[:, k, 0:n], gm[:, 0:n], ALU.mult))

            rank, blocks, ends, place = temps[10:14]
            blocks_i = blocks[:, 64:64 + E_N].bitcast(I32)
            filled(dve, ("count", l))
            dve.tensor_scalar(blocks_i, res(("count", l))[:, 0:E_N], float(SB - 1), None,
                              ALU.add).then_inc(drained(("count", l)), 1)
            evacuated(dve, ("count", l))
            link(dve.tensor_scalar(blocks_i, blocks_i, 6, None, ALU.logical_shift_right))
            link(dve.tensor_scalar(blocks[:, 0:E_N], blocks_i, 1.0, None, ALU.max))
            link(dve.memset(ends[:, 0:1], 0.0))
            link(dve.tensor_tensor_scan(ends[:, 1:E_N + 1], ones[:, 0:E_N], blocks[:, 0:E_N], 0.0,
                                        ALU.mult, ALU.add))
            dve.tensor_copy(starts[:, 0:E_N + 1], ends[0:1, 0:E_N + 1]).then_inc(starts_done, 1)
            link(dve.tensor_scalar(place[:, 0:E_N], ends[:, 0:E_N], float(SB), None, ALU.mult))
            dve.tensor_tensor(t3(rank), res(("rank", l))[:, 0:w].rearrange("p (c e) -> p c e", c=n),
                              place[:, 0:E_N].unsqueeze(1).broadcast_to([P, n, E_N]),
                              ALU.add).then_inc(drained(("rank", l)), 1)
            evacuated(dve, ("rank", l))
            for k, hot in enumerate((first, second)):
                link(dve.tensor_tensor(work[:, 0:w], rank[:, 0:w], hot[:, 0:w], ALU.mult))
                link(dve.tensor_reduce(gm[:, 6:6 + n], t3(work), AX.X, ALU.add))
                dve.tensor_copy(dest[:, k, 0:n], gm[:, 6:6 + n]).then_inc(dest_done, 1)

            nb = blocks_max((NT, LAT)[l]) + 1
            filled(dve, ("slots", l))
            dve.tensor_copy(slot_tok[:, 0:nb], res(("slots", l))[0:SB, 0:nb]).then_inc(drained(("slots", l)), 1)
            dve.memset(keep[:, 1988 + 2 * l:1989 + 2 * l], 0.0).then_inc(y_copied[l], 1)
            dve.memset(keep[:, 1989 + 2 * l:1990 + 2 * l], 0.0).then_inc(y_stored[l], 32)

        def experts(l):
            pX, pG, pH = psum[0], psum[1:3], psum[3:5]
            dve.wait_ge(starts_done, l + 1)
            total = dve.value_load(starts[:, E_N:E_N + 1], min_val=1, max_val=blocks_max(NT))
            dve.wait_ge(x_turned[l], 1)
            dve.tensor_copy(xT, pX[:, :].rearrange("p (k n) -> p k n", k=KD)).then_inc(xT_done[l], 1)
            with dve.Fori(0, total) as b:
                for c in (0, 1):
                    dve.wait_ge(gate_done[l], 2 * b + c + 1)
                    dve.tensor_tensor(hid[c], pG[c][:, P:2 * P], gate_act[c], ALU.mult).then_inc(hid_done[l], 1)
                for c in (0, 1):
                    dve.wait_ge(hid_turned[l], 2 * b + c + 1)
                    dve.tensor_copy(hidT[c], pH[c][:, 0:P]).then_inc(hidT_done[l], 1)
                dve.wait_ge(x_turned[l], b + 2)
                dve.tensor_copy(xT, pX[:, :].rearrange("p (k n) -> p k n", k=KD)).then_inc(xT_done[l], 1)

        def combine(l, c):
            g = gchunk(l, c)
            r = "l" if c < CL else "c"
            pair, m = y_pair[c % 2], mix[c % 2]
            if c == 0:
                dve.wait_ge(bc2_in[0], 64 * (l + 1))
            n_pair = sum(1 for q in range(g + 1) if (q if q < 6 else q - 6) % 2 == c % 2)
            dve.wait_ge(pair_in[c % 2], 32 * n_pair)
            link(dve.tensor_scalar(m, pair[0], pair_w[:, 0, c:c + 1], None, ALU.mult))
            dve.scalar_tensor_tensor(m, pair[1], pair_w[:, 1, c:c + 1], m, ALU.mult,
                                     ALU.add).then_inc(mixed_done, 1)
            dve.wait_ge(scaled, g + 1)
            link(dve.scalar_tensor_tensor(h_rows[:, c, :], h_rows[:, c, :], ALPHA, m, ALU.mult, ALU.add))
            normalise(g + 1 + len(CHUNKS_OF[0]) + (len(CHUNKS_OF[1]) if l else 0), h_rows[:, c, :])

        def finish(l):
            for c in CHUNKS_OF[l]:
                residual(l, c)
                normalise(gchunk(l, c) + 1 + 6 * l, h_rows[:, c, :])
            filled(dve, ("logit", l, CHUNKS_OF[l][-1]))
            dve.memset(slot_rows, 0.0).then_inc(slot_zero, 1)
            choose(l)
            experts(l)
            for c in CHUNKS_OF[l]:
                combine(l, c)

        finish(0)

        def gates(hd):
            cum = cums[hd % 2]
            for r in (0, 1):
                n_dir = 2 * hd + r
                for _, s, n, o in STREAMS:
                    name = ("g", hd, r, s)
                    dve.wait_ge(gates_abs, 2 * n_dir + s + 1)
                    dve.tensor_scalar(cum[:, r, o:o + n], res(name)[:, 0:n],
                                      smallT[:, 120 + 4 * r + hd:121 + 4 * r + hd], 0.0,
                                      ALU.add, ALU.min).then_inc(drained(name), 1)
                dve.wait_ge(gates_ln, n_dir + 1)
                for _, s, n, o in STREAMS:
                    evacuated(dve, ("g", hd, r, s))
                    m, l = cum[:, r, o:o + n], soft[:, o:o + n]
                    if r:
                        m, l = backwards(m, n), backwards(l, n)
                    dve.tensor_tensor_scan(m, m, l, 0.0, ALU.add, ALU.subtract).then_inc(cum_done, 1)

        def backwards(x, n):
            return x[:, n - 1::-1]

        def arguments(i):
            hd, lv = ITEMS[i]
            if lv in (0, LV_STATE):
                return
            cum = cums[hd % 2]
            dve.wait_ge(cum_done, 4 * (hd + 1))
            buffer_free(dve, i)
            buf = lev[i % 3]
            if lv == LV_CTX:
                for r, edge in ((0, NT - 1), (1, LAT)):
                    ins = dve.tensor_scalar(buf[:, CTX * r:CTX * r + CTX], cum[:, r, LAT:NT], -1.0,
                                            cum[:, r, edge:edge + 1], ALU.mult, ALU.add)
                ins.then_inc(args_done, 1)
                return
            h = 1 << (lv - 1)
            f = cum[:, 0, 0:LAT].rearrange("p (b m h) -> p b m h", m=2, h=h)
            g = cum[:, 1, 0:LAT].rearrange("p (b m h) -> p b m h", m=2, h=h)
            q = buf[:, 0:LAT].rearrange("p (b m h) -> p b m h", m=2, h=h)
            k = buf[:, LAT:2 * LAT].rearrange("p (b m h) -> p b m h", m=2, h=h)
            shape = [P, LAT // (2 * h), h]
            mid_f = f[:, :, 0, h - 1:h].broadcast_to(shape)
            mid_g = g[:, :, 1, 0:1].broadcast_to(shape)
            dve.tensor_tensor(q[:, :, 1, :], f[:, :, 1, :], mid_f, ALU.subtract)
            dve.tensor_tensor(q[:, :, 0, :], g[:, :, 0, :], mid_g, ALU.subtract)
            dve.tensor_tensor(k[:, :, 0, :], mid_f, f[:, :, 0, :], ALU.subtract)
            dve.tensor_tensor(k[:, :, 1, :], mid_g, g[:, :, 1, :], ALU.subtract).then_inc(args_done, 1)

        def masked(i):
            hd, lv = ITEMS[i]
            if lv <= LEVELS:
                name = ("att", i, 0)
                filled(dve, name)
                pairs = res(name)[:, :].rearrange("p (b n) -> p b n", b=CL)
                if lv == 0:
                    if hd:
                        dve.wait_ge(near_done, LEVELS * hd)
                    dve.scalar_tensor_tensor(att_near.rearrange("p (b n) -> p b n", b=CL), pairs, 2.0,
                                             ident.unsqueeze(1).broadcast_to([P, CL, P]),
                                             ALU.mult, ALU.mult).then_inc(drained(name), 1)
                else:
                    n = LEVELS * hd + lv
                    if n > 1:
                        dve.wait_ge(near_done, n - 1)
                    dve.tensor_tensor(prod.rearrange("p (b n) -> p b n", b=CL), pairs,
                                      masks[:, lv - 1, :].unsqueeze(1).broadcast_to([P, CL, P]),
                                      ALU.mult).then_inc(drained(name), 1)
            elif lv == LEVELS + 1:
                name = ("att", i, 0)
                filled(dve, name)
                dve.tensor_copy(att_next, res(name)[:, :]).then_inc(drained(name), 1)
            elif lv == LV_STATE:
                for u in range(CL):
                    name = ("o", hd, u)
                    filled(dve, name)
                    if hd and u == 0:
                        dve.wait_ge(o_var, CL * hd)
                    dve.bn_stats(g_stats[:, u, :], res(name)[:, 0:DVH])
                    dve.tensor_copy(o_rows[:, u, DVH * hd:DVH * hd + DVH], res(name)[:, 0:DVH]).then_inc(
                        drained(name), 1)
                evacuated(dve, ("o", hd, CL - 1))
                if hd:
                    dve.wait_ge(o_normed, hd)
                for u in range(CL):
                    dve.bn_aggr(g_mv[:, u, :], g_stats[:, u, :]).then_inc(o_var, 1)

        def normalise_head(hd):
            dve.wait_ge(o_dev, hd + 1)
            link(dve.reciprocal(g_rdev, g_dev))
            dve.wait_ge(o_var, CL * (hd + 1))
            for u in range(CL):
                o = o_rows[:, u, DVH * hd:DVH * hd + DVH]
                ins = dve.tensor_scalar(o, o, g_mv[:, u, 0:1], g_rdev[:, u:u + 1], ALU.subtract, ALU.mult)
            ins.then_inc(o_normed, 1)

        dve.memset(gate_w[0], 0.0).then_inc(zero_w, 1)
        modulated(1, [(s, k) for s in (0, 1) for k in range(KD)])
        dve.memset(gate_w[1], 0.0).then_inc(zero_w, 1)
        filled(dve, ("qk", 1, HEADS - 1, 1))
        gates(0)
        arguments(1)
        for i, (hd, lv) in enumerate(ITEMS):
            if i and i + 1 < len(ITEMS):
                arguments(i + 1)
            masked(i)
            if lv == 5 and hd + 1 < HEADS:
                gates(hd + 1)
            if lv == 4 and hd:
                normalise_head(hd - 1)
        normalise_head(HEADS - 1)
        for c in (0, 2):
            dve.wait_ge(silu_done, c + 1)
            dve.wait_ge(o_gained, HEADS)
            dve.tensor_tensor(r_rows[:, c, :], r_rows[:, c, :], o_rows[:, c, :], ALU.mult).then_inc(y_rows_done, 1)
        for k in range(1, KD, 2):
            filled(dve, ("yT", k))
            dve.tensor_copy(mixed[1][:, k, :], res(("yT", k))[:, :]).then_inc(drained(("yT", k)), 1)
        finish(1)

    @block.gpsimd
    def _(pool):
        def positions():
            pool.wait_ge(x_in, 16)
            pool.wait_ge(pe_in, 16)
            pool.tensor_tensor(x_rows[:, 0:CL, :], x_rows[:, 0:CL, :], pe_rows, ALU.add).then_inc(pe_added, 1)

        def complex_sums():
            done = 0
            for i, (s, half, o) in enumerate(STEPS):
                for f in range((CL, CC)[s]):
                    done += 1
                    made(pool, done)
                    pool.tensor_tensor(z_re[:, f, :], z_re[:, f, :], prod_a, ALU.subtract).then_inc(z_ready, 1)
                    pool.tensor_tensor(z_im[:, f, :], z_im[:, f, :], prod_b, ALU.add).then_inc(z_ready, 1)

        positions()
        complex_sums()

        def linker():
            n = [0]

            def link(ins):
                ins.then_inc(pool_link, 1)
                n[0] += 1
                pool.wait_ge(pool_link, n[0])
            return link

        link = linker()

        def affine(l, c):
            b = bcast[l]
            g = gchunk(l, c)
            r = "l" if c < CL else "c"
            h = h_rows[:, c, :]
            if c == 0:
                pool.wait_ge(sc2_done, (2, 3)[l])
            pool.wait_ge(normed, g + 1 + 6 * l)
            link(pool.tensor_tensor(h, h, b["lng"], ALU.mult))
            link(pool.tensor_tensor(h, h, b["lnb"], ALU.add))
            if c >= 2:
                pool.wait_ge(tok_stored, 16 * (g - 1))
                filled(pool, ("a2T", l, c - 2, 1))
            link(pool.tensor_tensor(a2[c % 2], h, b["sc2" + r], ALU.mult))
            pool.tensor_tensor(a2[c % 2], a2[c % 2], b["sh2" + r], ALU.add).then_inc(a2_done, 1)

        def scatter(l):
            chunks = CHUNKS_OF[l]
            pool.wait_ge(slot_cleared, 16 * (l + 1))
            for k in (0, 1):
                pool.wait_ge(dest_done, 2 * l + k + 1)
                for c in chunks:
                    pool.indirect_dma_start(
                        out=slot_l[l], out_offset=bass.IndirectOffsetOnAxis(ap=dest[:, k, c:c + 1], axis=0),
                        in_=token_id[:, c:c + 1], in_offset=None).then_inc(scattered, 16)

        def experts(l):
            def gather():
                pool.indirect_dma_start(
                    out=x_slots, out_offset=None, in_=tok_l[l],
                    in_offset=bass.IndirectOffsetOnAxis(ap=cur_tok, axis=0)).then_inc(x_landed[l], 16)

            evacuated(pool, ("slots", l))
            pool.wait_ge(y_filled_up, 16)
            pool.wait_ge(tok_stored, 16 * (gchunk(l, CHUNKS_OF[l][-1]) + 1))
            pool.wait_ge(starts_done, l + 1)
            total = pool.value_load(starts[:, E_N:E_N + 1], min_val=1, max_val=blocks_max(NT))
            pool.tensor_copy(cur_tok, slot_tok[:, 0:1]).then_inc(x_copied[l], 1)
            pool.wait_ge(x_copied[l], 1)
            gather()
            with pool.Fori(0, total) as b:
                pool.wait_ge(x_landed[l], 16 * b + 16)
                pool.tensor_copy(cur_tok, slot_tok[:, ds(b + 1, 1)]).then_inc(x_copied[l], 1)
                pool.wait_ge(x_copied[l], b + 2)
                pool.wait_ge(x_turned[l], b + 1)
                pool.sem_inc(gather_go[l], 1)
                gather()
            pool.wait_ge(y_stored[l], 32 * total + 32)
            pool.wait_ge(x_landed[l], 16 * total + 16)
            pool.wait_ge(gather_go[l], total)
            pool.tensor_tensor(keep[:, 1992:1993], eps, eps, ALU.add).then_inc(combine_go, 1)
            pool.wait_ge(combine_go, l + 1)

        def combine(l):
            chunks = CHUNKS_OF[l]
            for c in chunks:
                g = gchunk(l, c)
                if c >= 2:
                    pool.wait_ge(mixed_done, g - 1)
                for k in (0, 1):
                    pool.indirect_dma_start(
                        out=y_pair[c % 2][k], out_offset=None, in_=y_d,
                        in_offset=bass.IndirectOffsetOnAxis(ap=dest[:, k, c:c + 1], axis=0)
                    ).then_inc(pair_in[c % 2], 16)
                if c:
                    finish_rows(l, c - 1)
                pool.wait_ge(mixed_done, g + 1)
                r = "l" if c < CL else "c"
                if c == 0:
                    pool.wait_ge(bc2_in[0], 64 * (l + 1))
                pool.tensor_tensor(mix[c % 2], mix[c % 2], bc2["g2" + r], ALU.mult).then_inc(scaled, 1)
            finish_rows(l, chunks[-1])

        def finish_rows(l, c):
            n = gchunk(l, c) + 1 + len(CHUNKS_OF[0]) + (len(CHUNKS_OF[1]) if l else 0)
            h = h_rows[:, c, :]
            pool.wait_ge(normed, n)
            link(pool.tensor_tensor(h, h, bc2["lng"], ALU.mult))
            pool.tensor_tensor(h, h, bc2["lnb"], ALU.add).then_inc(h_next, 1)

        def finish(l):
            for c in CHUNKS_OF[l]:
                affine(l, c)
            scatter(l)
            experts(l)
            combine(l)

        finish(0)

        def scale_qk(i):
            hd, lv = ITEMS[i]
            if lv == 0:
                return
            pool.wait_ge(exps_done, scaled_items(i))
            buf = lev[i % 3]
            if lv == LV_CTX:
                x = buf[:, 0:2 * CTX].rearrange("p (r n) -> p r n", r=2)
                y = k_ctx[:, hd, :].unsqueeze(1).broadcast_to([P, 2, CTX])
                evacuated(pool, ("qk", 1, hd, 1))
            elif lv == LV_STATE:
                x = buf.rearrange("p (r n) -> p r n", r=2)
                y = qk[:, hd, 0, :].unsqueeze(1).broadcast_to([P, 2, LAT])
            else:
                x = buf.rearrange("p (r n) -> p r n", r=2)
                y = qk[:, hd, :, :]
                evacuated(pool, ("qk", 0, hd, 0))
                evacuated(pool, ("qk", 1, hd, 0))
            pool.tensor_tensor(x, x, y, ALU.mult).then_inc(scaled_qk, 1)

        def add_near(i):
            hd, lv = ITEMS[i]
            if 1 <= lv <= LEVELS:
                evacuated(pool, ("att", i, 0))
                if lv == 1:
                    evacuated(pool, ("att", i - 1, 0))
                else:
                    pool.wait_ge(near_done, LEVELS * hd + lv - 1)
                pool.tensor_tensor(att_near, att_near, prod, ALU.add).then_inc(near_done, 1)

        def gain(hd):
            pool.wait_ge(o_normed, hd + 1)
            if hd == 0:
                pool.wait_ge(norm_in, 16)
            cols = slice(DVH * hd, DVH * hd + DVH)
            pool.tensor_tensor(o_rows[:, :, cols], o_rows[:, :, cols],
                               norm_g[:, cols].unsqueeze(1).broadcast_to([P, CL, DVH]),
                               ALU.mult).then_inc(o_gained, 1)

        scale_qk(1)
        for i, (hd, lv) in enumerate(ITEMS):
            if i and i + 1 < len(ITEMS):
                scale_qk(i + 1)
            add_near(i)
        for hd in range(HEADS):
            gain(hd)
        for c in (1, 3):
            pool.wait_ge(silu_done, c + 1)
            pool.wait_ge(o_gained, HEADS)
            pool.tensor_tensor(r_rows[:, c, :], r_rows[:, c, :], o_rows[:, c, :], ALU.mult).then_inc(y_rows_done, 1)
        finish(1)

    @block.sync
    def _(sp):
        def modulation():
            w = t["w_mod"].rearrange("l (k p) (h u c) -> l h u p k c", p=P, u=SLOTS, c=COL)
            for u in range(SLOTS):
                sp.dma_start(slot(u).rearrange("p (k c) -> p k c", k=KD), w[0, 0, u]).then_inc(landed[u], 16)
            for n in range(1, N_MOD // SLOTS):
                for u in range(SLOTS):
                    sp.wait_ge(mod_filled, SLOTS * (n - 1) + u + 1)
                    sp.dma_start(slot(u).rearrange("p (k c) -> p k c", k=KD),
                                 w[n // 2, n % 2, u]).then_inc(landed[u], 16)

        def hyena():
            w = t["hy_w_in"][0].rearrange("(k p) (j c) -> j p k c", p=P, c=COL)
            for j in range(6):
                sp.wait_ge(mod_filled, N_MOD - SLOTS + j + 1)
                s, _ = units.of[("hy_in", j)]
                sp.dma_start(slot(s).rearrange("p (k c) -> p k c", k=KD), w[j]).then_inc(landed[s], 16)
            filled(sp, ("proj", 1, 3))
            w4_d = t["hy_f_w4"][0].rearrange("f (o r c) -> r f o c", o=2, r=2)
            for r in (0, 1):
                sp.dma_start(w4[HF * r:HF * r + HF], w4_d[r]).then_inc(filt_in, 16)
            sp.dma_start(filt_u[:, 2 * D:], t["dft_small"]).then_inc(filt_in, 16)
            s, _ = units.of[("dft", 0)]
            filled(sp, ("proj", 1, 7))
            sp.dma_start(dft, t["dft"].rearrange("a (c p) n -> p a c n", p=P)).then_inc(landed[s], 16)
            s, _ = units.of[("idft", 0)]
            filled(sp, ("proj", 1, 11))
            sp.dma_start(idft, t["idft"].rearrange("a (c p) n -> p a c n", p=P)).then_inc(landed[s], 16)
            w = t["hy_w_out"][0].rearrange("(k p) (j c) -> j p k c", p=P, c=COL)
            for j in range(2):
                s, _ = units.of[("hy_out", j)]
                filled(sp, ("proj", 1, 4 * (3 + j) + 3))
                sp.dma_start(slot(s).rearrange("p (k c) -> p k c", k=KD), w[j]).then_inc(landed[s], 16)

        modulation()
        hyena()

        def experts(l):
            w1 = t["moe_w1"][l].rearrange("e (k p) c -> e p k c", p=P)
            w3 = t["moe_w3"][l].rearrange("e (k p) c -> e p k c", p=P)
            w2 = t["moe_w2"][l].rearrange("e (k p) c -> e p k c", p=P)

            def load(e, s, dynamic):
                for q, w in enumerate((w1, w3, w2)):
                    src = w[ds(e, 1)].rearrange("o p k c -> (o p) k c") if dynamic else w[e]
                    sp.dma_start(slot(s + q).rearrange("p (k c) -> p k c", k=(8, 8, 4)[q]),
                                 src).then_inc(landed[s + q], 16)

            for e in (0, 1):
                for q in range(3):
                    free_for_experts(l, 3 * e + q)
                    w = (w1, w3, w2)[q]
                    sp.dma_start(slot(3 * e + q).rearrange("p (k c) -> p k c", k=(8, 8, 4)[q]),
                                 w[e]).then_inc(landed[3 * e + q], 16)
            sp.wait_ge(starts_done, l + 1)
            with sp.Fori(1, E_N // 2) as pair:
                for par in (0, 1):
                    done = sp.value_load(starts[:, ds(2 * pair + par - 1, 1)], min_val=1, max_val=blocks_max(NT))
                    sp.wait_ge(y_filled[l], done)
                    load(2 * pair + par, 3 * par, True)

        def fill_outputs():
            rest = blocks_max(NT) - E_N
            src = t["zeros"].rearrange("s d -> () (s d)").broadcast_to([rest, SB * D])
            sp.dma_start(y_d[E_N * SB:].rearrange("(b s) d -> b (s d)", s=SB), src).then_inc(y_filled_up, 16)

        def free_for_experts(l, s):
            if l == 0:
                filled(sp, [("k", 1, last_step, CC - 1), ("x", 1, last_step, CC - 1), ("y", last_step, 3),
                            ("out", 0, 5, 0), ("out", 0, 5, 1), ("proj", 1, 23)][s])
                if s == 0:
                    filled(sp, ("y", last_step, 3))
                if s == 5:
                    n = len(CHUNKS)
                    sp.wait_ge(z_ready, 2 * n)
                    made(sp, n)
                    sp.wait_ge(skip_added, len(STEPS))
            elif s < 4:
                filled(sp, ("o", HEADS - 1, CL - 1))
                if s == 2:
                    sp.wait_ge(y_rows_done, CL)
            else:
                filled(sp, ("out", 1, CL - 1, s - 4))

        fill_outputs()
        experts(0)

        def gla_weights():
            w = t["gla_w_in"][0, :, 0:3072].rearrange("(k p) (j c) -> j p k c", p=P, c=COL)
            wo = t["gla_w_out"][0].rearrange("(k p) (j c) -> j p k c", p=P, c=COL)
            total = sp.value_load(starts[:, E_N:E_N + 1], min_val=1, max_val=blocks_max(NT))
            before_last = sp.value_load(starts[:, E_N - 1:E_N], min_val=1, max_val=blocks_max(NT))
            for j in range(6):
                s, _ = units.of[("gla_in", j)]
                sp.wait_ge(y_filled[0], before_last if s < 3 else total)
                sp.dma_start(slot(s).rearrange("p (k c) -> p k c", k=KD), w[j]).then_inc(landed[s], 16)
            for j in range(2):
                s, _ = units.of[("gla_out", j)]
                filled(sp, ("r", j, CL - 1))
                sp.dma_start(slot(s).rearrange("p (k c) -> p k c", k=KD), wo[j]).then_inc(landed[s], 16)

        gla_weights()
        experts(1)
        sp.wait_ge(out_stored, 16 * CL)

    ctx.close()


def constants():
    f8 = np.float64
    f4 = np.float32
    q = D // 4
    omega = 1.0 / (10000.0 ** (np.arange(q, dtype=f8) / q))
    pr = np.arange(LAT // 64, dtype=f8)[:, None] * omega
    pc = np.arange(64, dtype=f8)[:, None] * omega
    er = np.concatenate([np.sin(pr), np.cos(pr)], -1)
    ec = np.concatenate([np.sin(pc), np.cos(pc)], -1)
    pos = np.concatenate([np.broadcast_to(er[:, None, :], (LAT // 64, 64, 2 * q)),
                          np.broadcast_to(ec[None, :, :], (LAT // 64, 64, 2 * q))], -1).reshape(LAT, D)

    def features(n):
        x = np.linspace(0.0, 1.0, n)[:, None]
        w = 2.0 * np.pi * np.arange(n)[:, None] / n
        bands = np.linspace(1e-4, 15, 16)[None, :]
        return np.concatenate([x, np.cos(bands * w), -np.sin(bands * w)], -1)

    def window(n):
        deltas = np.abs(np.linspace(np.log(1e-2) / 1.5, np.log(1e-2) / 0.3, D))
        return np.exp(-np.linspace(0.0, 1.0, n)[:, None] * deltas)

    def transforms(n):
        a = np.pi * np.outer(np.arange(n), np.arange(n)) / n
        c, s = np.cos(a), -np.sin(a)
        alt = (-1.0) ** np.arange(n)
        s_fwd, s_inv = s.copy(), s / n
        s_fwd[:, 0] = alt
        s_inv[0, :] = alt / (2 * n)
        c_inv = c / n
        c_inv[0, :] = 1.0 / (2 * n)
        return np.stack([c, s_fwd]), np.stack([c_inv, s_inv])

    fwd, inv = transforms(LAT)
    small = np.stack(transforms(CTX))
    small = small.reshape(2, 2, CC, P, CTX).transpose(3, 0, 1, 2, 4).reshape(P, -1)
    marks = np.ones((P, 3))
    marks[HF:, 0] = -1.0
    marks[0, 1] = 0.0
    marks[:, 2] = EPS
    i = np.arange(P)
    masks = np.zeros((P, LEVELS, P))
    for l in range(LEVELS):
        same = i[:, None] // (2 << l) == i[None] // (2 << l)
        masks[:, l] = same & (i[:, None] // (1 << l) != i[None] // (1 << l))
    token = i[:, None] + P * np.arange(NT // P)[None]
    ramps = np.concatenate([np.arange(8, 0, -1), np.arange(4, 0, -1)])
    route = np.concatenate([(i[:, None] < i[None]), np.ones((P, P)), token,
                            np.broadcast_to(ramps, (P, 12))], 1)
    out = dict(ident=np.eye(P), marks=marks, pos=pos, dft=fwd, idft=inv, dft_small=small,
               window_lat=window(LAT), window_ctx=window(CTX),
               zT=np.concatenate([features(LAT), features(CTX)], 0).T,
               masks=masks.reshape(P, -1), route_c=route, zeros=np.zeros((SB, D)))
    return {k: np.ascontiguousarray(v, dtype=f4) for k, v in out.items()}


_INS = ["x", "c", "ctx", "c_ctx", "w_mod", "b_mod", "ln_g", "ln_b", "hy_w_in", "hy_b_in", "hy_conv_w",
        "hy_conv_b", "hy_f_w1", "hy_f_b1", "hy_f_w2", "hy_f_b2", "hy_f_w3", "hy_f_b3", "hy_f_w4",
        "hy_skip", "hy_w_out", "hy_b_out", "gla_w_in", "gla_w_gate", "gla_b_gate", "gla_norm_g",
        "gla_w_out", "router_w", "router_b", "moe_w1", "moe_w3", "moe_w2"]


def kernel(**inputs):
    import numpy as _np
    import concourse.bacc as _bacc
    from concourse import mybir as _mybir
    from concourse.bass_utils import run_bass_kernel_spmd as _run

    nc = _bacc.Bacc("TRN2", target_bir_lowering=False, num_devices=1)
    arrays, tensors = {}, {}
    data = {n: _np.ascontiguousarray(inputs[n]) for n in _INS}
    for name, a in {**data, **constants()}.items():
        arrays[f"in_{name}"] = a
        tensors[name] = nc.dram_tensor(f"in_{name}", a.shape, _mybir.dt.from_np(a.dtype),
                                       kind="ExternalInput").ap()
    out = nc.dram_tensor("out_h", (1, LAT, D), F32, kind="ExternalOutput").ap()
    build(nc, tensors, out)
    r = _run(nc, [arrays], core_ids=[0])
    return r.results[0]["out_h"]
```

```python
from contextlib import ExitStack

import numpy as np
import concourse.bass as bass
import concourse.mybir as mybir

F32 = mybir.dt.float32
I32 = mybir.dt.int32
U32 = mybir.dt.uint32
ALU = mybir.AluOpType
ACT = mybir.ActivationFunctionType
AX = mybir.AxisListType
ds = bass.ds

P = 128
D = 1024
KD = D // P
LAT, CTX = 512, 256
NT = LAT + CTX
CL, CC = LAT // P, CTX // P
COL = 512
UNIT = KD * COL
SLOTS = 6
E_N, GRP, GSZ = 32, 4, 8
D_E = 512
SB = 64
ALPHA = (2.0 * 2) ** 0.25
EPS = 1e-5
HF = 64
HEADS, DKH, DVH = 4, 128, 256
N_MOD = 24
TAU = 16.0
LEVELS = 7

MAGIC = 12582912.0
PI2_HI = 6.28125
PI2_LO = 2.0 * np.pi - 6.28125


def blocks_max(tokens):
    return 2 * tokens // SB + E_N


class PsumPlan:

    def __init__(self):
        self.total = 0
        self.used = [0] * 8
        self.of = {}

    def add(self, name, bank=None):
        bank = self.total % 8 if bank is None else bank
        self.total += 1
        self.of[name] = (bank, self.total, self.used[bank])
        self.used[bank] += 1
        return self.of[name]


class Ring:

    def __init__(self):
        self.at = 0
        self.loads = [0] * SLOTS
        self.of = {}

    def add(self, name, loads=1):
        slot = self.at % SLOTS
        self.of[name] = (slot, self.loads[slot])
        self.loads[slot] += loads
        self.at += 1

    def skip(self, n):
        self.at += n


def build(nc, t, out):
    ctx = ExitStack()

    def sem(name):
        return ctx.enter_context(nc.semaphore(name))

    def scratch(name, shape, dt=F32):
        return nc.dram_tensor(name, shape, dt, kind="Internal").ap()

    ring = ctx.enter_context(nc.sbuf_tensor("ring", [P, SLOTS * UNIT], F32))
    arena = ctx.enter_context(nc.sbuf_tensor("arena", [P, 26624], F32))
    keep = ctx.enter_context(nc.sbuf_tensor("keep", [P, 2000], F32))
    psum = [ctx.enter_context(nc.psum_tensor(f"bank{i}", [P, 512], F32)) for i in range(8)]

    KB = 256

    def at(kb, n, lo=0, hi=P):
        o = int(kb * KB)
        return arena[lo:hi, o:o + n]

    def slot(s, lo=0, n=UNIT):
        return ring[:, s * UNIT + lo:s * UNIT + lo + n]

    mod_d = scratch("mod_d", [2, N_MOD, 4, P])
    h0_d = scratch("h0_d", [LAT, D])

    ident = keep[:, 0:128]
    hf_sum = keep[:, 128:128 + NT]
    hf_diff = keep[:, 896:896 + NT]
    modT = keep[:, 1664:1856].rearrange("p (l r v k) -> p l r v k", l=2, r=2, v=6)
    smallT = keep[:, 1856:1984]
    sgn, rowmask, eps = keep[:, 1984:1985], keep[:, 1985:1986], keep[:, 1986:1987]

    def conv_w(j, ch):
        return smallT[:, 24 * j + ch:24 * j + ch + 1]

    def b_in(ch):
        return smallT[:, 72 + ch:73 + ch]

    def conv_b(ch):
        return smallT[:, 96 + ch:97 + ch]

    aT = at(0, KD * NT).rearrange("p (k n) -> p k n", k=KD)
    aT_l = [aT, at(24, KD * NT).rearrange("p (k n) -> p k n", k=KD)]
    x_rows = at(24, 6 * D).rearrange("p (c d) -> p c d", c=6)
    pe_rows = at(48, 4 * D).rearrange("p (c d) -> p c d", c=4)
    mod_acc = at(72, N_MOD * P).rearrange("p (n c) -> p n c", n=N_MOD)
    cond_rows = at(84, P, 0, 16)
    s_cols = at(84.5, KD * 32).rearrange("p (k c) -> p k c", k=KD)
    small_rows = at(86, P)
    mod_rows = at(87, 2 * P, 0, 96).rearrange("p (l c) -> p l c", l=2)
    hf1, hf2 = at(88, NT, 0, HF), at(91, NT, 0, HF)
    arg_u, arg_t = at(64, NT), at(67, NT)
    zT = at(96, NT, 0, 33)
    taps = [at(96, 772), arena[:, 96 * KB + 772:96 * KB + 1544]]
    fw = arena[:, 26120:26120 + 256]
    f_w1, f_w2, f_w3 = fw[0:33, 0:HF], fw[0:HF, HF:2 * HF], fw[0:HF, 2 * HF:4 * HF]
    f_b = arena[:, 26376:26380]
    zc = [at(72, NT), at(75, NT)]
    v_t = at(24, 6 * D).rearrange("p (c d) -> p c d", c=6)
    x1_t = at(48, 6 * D).rearrange("p (c d) -> p c d", c=6)
    x2T = at(72, KD * NT).rearrange("p (k n) -> p k n", k=KD)
    filt = [at(8 * i, 4 * COL).rearrange("p (c d) -> p c d", c=4) for i in (0, 1)]
    z = [at(kb, 4 * COL).rearrange("p (r f d) -> p r f d", r=2, f=2) for kb in (16, 96)]

    units = Ring()
    for u in range(N_MOD):
        units.add(("mod", u))
    for j in range(6):
        units.add(("hy_in", j))
    units.add(("filt", 0), 0)
    units.add(("dft", 0))
    units.add(("idft", 0))
    units.add(("hy_out", 0))
    units.add(("hy_out", 1))
    units.skip(1)
    moe_first = {}
    moe_first[0] = list(units.loads)
    assert units.at % SLOTS == 0
    for e in range(E_N * 3):
        units.add(("moe0", e))
    for j in range(6):
        units.add(("gla_in", j))
    units.skip(4)
    for j in range(2):
        units.add(("gla_out", j))
    moe_first[1] = list(units.loads)

    HALF = UNIT // 2
    k_parts = [slot(5, HALF * i, HALF).rearrange("p (j d) -> p j d", j=4) for i in (0, 1)]
    win = [slot(0, 6 * COL + COL * i, COL) for i in (0, 1)]
    k_alt = slot(1, HALF, 3 * COL).rearrange("p (j d) -> p j d", j=3)
    skip_row = ring[0:1, 1 * UNIT + HALF + 3 * COL:1 * UNIT + HALF + 4 * COL]
    terms = [None] + [x.rearrange("p (a r d) -> p a r d", a=2, r=2)
                      for x in (slot(2, HALF, HALF), slot(4, 0, HALF), slot(4, HALF, HALF))]

    landed = [sem(f"landed{i}") for i in range(SLOTS)]
    psum_filled = sem("psum_filled")
    psum_drained = [sem(f"psum_drained{i}") for i in range(8)]
    keep_in, cond_in, small_in, x_in, pe_in, ctx_in, fw_in = (
        sem(n) for n in ("keep_in", "cond_in", "small_in", "x_in", "pe_in", "ctx_in", "fw_in"))
    bias_in, filt_in = sem("bias_in"), sem("filt_in")
    mod_zeroed, cols_zeroed, cond_silu = sem("mod_zeroed"), sem("cols_zeroed"), sem("cond_silu")
    mod_filled, mod_drained, mod_stored = sem("mod_filled"), sem("mod_drained"), sem("mod_stored")
    mod_back, modT_done = sem("mod_back"), sem("modT_done")
    pe_added, h0_stored = sem("pe_added"), sem("h0_stored")
    act_link, dve_link, pool_link = sem("act_link"), sem("dve_link"), sem("pool_link")
    sin_arg, sin_done, hf_done = sem("sin_arg"), sem("sin_done"), sem("hf_done")
    edges_zeroed, conv_done = sem("edges_zeroed"), sem("conv_done")
    win_in = [sem("win_in0"), sem("win_in1")]
    skip_in, skip_added = sem("skip_in"), sem("skip_added")
    z_ready = sem("z_ready")

    router_w = keep[:, 128:384].rearrange("p (k e) -> p k e", k=KD)
    router_b = keep[:, 384:416]
    before, ones = keep[:, 416:544], keep[:, 544:672]
    token_id, ramp8, ramp4 = keep[:, 672:678], keep[:, 678:686], keep[:, 686:690]
    scores = keep[:, 690:882]
    pair_w = keep[:, 882:894].rearrange("p (k c) -> p k c", k=2)
    dest = keep[:, 894:906].bitcast(U32).rearrange("p (k c) -> p k c", k=2)
    starts = keep[0:1, 906:940].bitcast(I32)
    slot_tok = keep[0:SB, 940:998].bitcast(U32)
    cur_tok = keep[0:SB, 998:999].bitcast(U32)
    stats = keep[:, 1000:1012].rearrange("p (h s) -> p h s", h=2)
    mean_var, dev, rdev = keep[:, 1012:1014], keep[:, 1014:1015], keep[:, 1015:1016]
    h_rows = at(0, 6 * D).rearrange("p (c d) -> p c d", c=6)
    temps = [at(72 + 0.75 * i, 192) for i in range(16)]
    slot_rows = at(90, SB, 0, P)

    tok_l = [scratch(f"tok{l}", [(NT, LAT)[l], D]) for l in (0, 1)]
    slot_l = [scratch(f"slot{l}", [(blocks_max((NT, LAT)[l]) + 2) * SB, 1]) for l in (0, 1)]
    y_d = scratch("y", [blocks_max(NT) * SB, D])

    CHUNKS_OF = [list(range(6)), list(range(CL))]
    mixed = [x2T, at(24, KD * LAT).rearrange("p (k n) -> p k n", k=KD)]
    BC = [["bout", "g1l", "g1c", "lng", "lnb", "sc2l", "sc2c", "sh2l", "sh2c"],
          ["g1l", "lng", "lnb", "sc2l", "sh2l"]]
    bc0 = [24, 72]
    bcast = [{n: at(bc0[l] + 4 * i, D) for i, n in enumerate(BC[l])} for l in (0, 1)]
    a2 = [at(60, D), at(64, D)]
    a2T = at(68, D).rearrange("p (k n) -> p k n", k=KD)
    resid = at(96, D)
    tmp = [at(100, COL), at(102, COL)]

    x_land, x_slots = at(52, D, 0, SB), at(24, D, 0, SB)
    xT = at(28, KD * SB).rearrange("p (k n) -> p k n", k=KD)
    gate_act = [at(30, P), at(30.5, P)]
    hid = [at(31, P), at(31.5, P)]
    hidT = [at(32, P), at(32.5, P)]
    y_out = at(33, COL)
    y_pair = [[at(kb, D), at(kb + 4, D)] for kb in (36, 44, 76, 84, 92, 24)]
    mix = [at(52, D), at(56, D)]
    bc2 = {n: at(60 + 4 * i, D) for i, n in enumerate(["g2l", "g2c", "lng", "lnb"])}

    bc_in, res_in, res_used = sem("bc_in"), sem("res_in"), sem("res_used")
    var_ready, dev_done, normed, a2_done = sem("var_ready"), sem("dev_done"), sem("normed"), sem("a2_done")
    tok_stored, route_in, h_ready = sem("tok_stored"), sem("route_in"), sem("h_ready")
    picked, starts_done, dest_done, slot_zero = sem("picked"), sem("starts_done"), sem("dest_done"), sem("slot_zero")
    slot_cleared, scattered, slots_back, table_done = (
        sem("slot_cleared"), sem("scattered"), sem("slots_back"), sem("table_done"))
    L2 = (0, 1)
    x_copied = [sem(f"x_copied{l}") for l in L2]
    x_landed = [sem(f"x_landed{l}") for l in L2]
    x_moved = [sem(f"x_moved{l}") for l in L2]
    x_turned = [sem(f"x_turned{l}") for l in L2]
    gather_go = [sem(f"gather_go{l}") for l in L2]
    xT_done = [sem(f"xT_done{l}") for l in L2]
    up_filled = [sem(f"up_filled{l}") for l in L2]
    gate_done = [sem(f"gate_done{l}") for l in L2]
    hid_done = [sem(f"hid_done{l}") for l in L2]
    hid_turned = [sem(f"hid_turned{l}") for l in L2]
    hidT_done = [sem(f"hidT_done{l}") for l in L2]
    y_filled = [sem(f"y_filled{l}") for l in L2]
    y_copied = [sem(f"y_copied{l}") for l in L2]
    y_stored = [sem(f"y_stored{l}") for l in L2]
    pair_in = [sem(f"pair_in{c}") for c in range(6)]
    bc2_in, first_scaled, mixed_done = sem("bc2_in"), sem("first_scaled"), sem("mixed_done")
    lng_done, h_next = sem("lng_done"), sem("h_next")
    y_filled_up, combine_go = sem("y_filled_up"), sem("combine_go")
    scaled, out_stored, layer_done = sem("scaled"), sem("out_stored"), sem("layer_done")

    def norm2(l, c):
        return gchunk(l, c) + 1 + len(CHUNKS_OF[0]) + (len(CHUNKS_OF[1]) if l else 0)

    def gchunk(l, c):
        return c + len(CHUNKS_OF[0]) * l


    h1_d = scratch("h1_d", [LAT, D])
    r_rows = at(0, CL * D).rearrange("p (c d) -> p c d", c=CL)
    masks = at(16, LEVELS * P).rearrange("p (l n) -> p l n", l=LEVELS)
    prod = at(19.5, 4 * P)
    gate_w = [keep[0:32, 1016:1016 + COL], at(21.5, COL, 0, 32)]
    qk = at(48, HEADS * 2 * LAT).rearrange("p (h m n) -> p h m n", h=HEADS, m=2)
    k_ctx = at(64, HEADS * CTX).rearrange("p (h n) -> p h n", h=HEADS)
    v_rows = at(68, 6 * D).rearrange("p (c d) -> p c d", c=6)
    lrT = at(92, NT, 0, 32)
    soft = at(95, NT)
    kt_rows = at(99, 4 * P)
    state = at(101, 2 * DVH).rearrange("p (r n) -> p r n", r=2)
    lr_w = at(103, KD * 32).rearrange("p (k c) -> p k c", k=KD)
    norm_g = at(40, D)
    g_stats = keep[:, 1528:1552].rearrange("p (c s) -> p c s", c=CL)
    g_mv = keep[:, 1552:1560].rearrange("p (c s) -> p c s", c=CL)
    g_dev, g_rdev = keep[:, 1560:1564], keep[:, 1564:1568]
    lev = [ring[:, 1024 * i:1024 * i + 1024] for i in range(3)]
    att_near = ring[:, 3072:3584]
    att_next = ring[:, 3584:4096]
    att_far = ring[:, 4096:5120]
    cums = [ring[:, 5120 + 1536 * i:5120 + 1536 * (i + 1)].rearrange("p (r n) -> p r n", r=2) for i in (0, 1)]
    o_rows = slot(2).rearrange("p (c d) -> p c d", c=CL)

    h1_stored, gla_in, zero_w, gates_abs = sem("h1_stored"), sem("gla_small_in"), sem("zero_w"), sem("gates_abs")
    gates_ln, cum_done, args_done, exps_done = sem("gates_ln"), sem("cum_done"), sem("args_done"), sem("exps_done")
    scaled_qk, prod_done, near_done = sem("scaled_qk"), sem("prod_done"), sem("near_done")
    norm_in, o_var, o_dev, o_normed, o_gained = (
        sem("norm_in"), sem("o_var"), sem("o_dev"), sem("o_normed"), sem("o_gained"))
    silu_done, y_rows_done = sem("silu_done"), sem("y_rows_done")
    combined = sem("combined")

    N_LV = LEVELS + 5
    LV_CTX, LV_STATE = LEVELS + 3, LEVELS + 4
    ITEMS = [(h, lv) for h in range(HEADS) for lv in range(N_LV)]

    PROJ = ([("v", 0, c) for c in range(6)] + [("v", 1, c) for c in range(6)] +
            [("r", half, c) for half in (0, 1) for c in range(CL)])
    PROJ_AT = {}
    for hd, first, n in ((0, 0, 6), (1, 6, 5), (2, 11, 5), (3, 16, 4)):
        for j in range(n):
            PROJ_AT[(hd, min(2 * j, N_LV - 3))] = PROJ_AT.get((hd, min(2 * j, N_LV - 3)), []) + [PROJ[first + j]]

    def last_use(i):
        hd, lv = ITEMS[i]
        if lv == LV_CTX:
            return ("kt", hd)
        if lv == LV_STATE:
            return ("o", hd, CL - 1)
        if lv == LEVELS + 2:
            return ("att", i, 1)
        return ("att", i, 0)

    def buffer_free(eng, i):
        if i >= 3 and ITEMS[i - 3][1] != 0:
            filled(eng, last_use(i - 3))

    def scaled_items(i):
        return sum(1 for q in range(i + 1) if ITEMS[q][1] != 0)

    def arg_items(i):
        return sum(1 for q in range(i + 1) if ITEMS[q][1] not in (0, LV_STATE))

    plan = PsumPlan()

    def filled(eng, name):
        eng.wait_ge(psum_filled, plan.of[name][1])

    def evacuated(eng, name):
        b, _, used = plan.of[name]
        eng.wait_ge(psum_drained[b], used + 1)

    def drained(name):
        return psum_drained[plan.of[name][0]]

    def res(name):
        return psum[plan.of[name][0]]

    def unit_landed(eng, name):
        s, k = units.of[name]
        eng.wait_ge(landed[s], 16 * (k + 1))

    def unit(name):
        return slot(units.of[name][0])

    def made(eng, n):
        i, f = CHUNKS[n - 1]
        evacuated(eng, ("x", 3, i, f))

    STREAMS = [("lat", 0, LAT, 0), ("ctx", 1, CTX, LAT)]

    STEPS = [(s, half, o) for s in (0, 1) for half in (0, 1) for o in (0, 1)]
    last_step = len(STEPS) - 1
    FREQ = (CL // 2, CC // 2)
    CHUNKS = [(i, f) for i, (s, _, _) in enumerate(STEPS) for f in range(FREQ[s])]

    def chunk_base(i):
        return sum(FREQ[s] for s, _, _ in STEPS[:i])

    PARTS = [(0, 0), (0, 1), (1, 0), (1, 1)]

    filt_u = slot(units.of[("filt", 0)][0])
    w4 = filt_u[:, 0:2 * D].rearrange("p (o c) -> p o c", o=2)
    c_small = filt_u[:, 2 * D:3 * D].rearrange("p (i a r c n) -> p i a r c n", i=2, a=2, r=2, c=1)
    dft = slot(units.of[("dft", 0)][0], 0, HALF).rearrange("p (a r c n) -> p a r c n", a=2, r=2, c=2)
    idft = slot(units.of[("idft", 0)][0], 0, HALF).rearrange("p (a r c n) -> p a r c n", a=2, r=2, c=2)

    def basis(s, inverse, a, par):
        if s:
            return c_small[:, inverse, a, par]
        return (idft if inverse else dft)[:, a, par]

    block = ctx.enter_context(nc.Block())

    @block.tensor
    def _(pe):
        def begin(name, bank=None):
            b, _, used = plan.add(name, bank)
            if used:
                pe.wait_ge(psum_drained[b], used)
            return psum[b]

        def turn(dst, src, n=P):
            return pe.transpose(dst, src, ident[0:n, 0:n])

        def cond_columns():
            pe.wait_ge(keep_in, 32)
            pe.wait_ge(cond_silu, 1)
            turn(begin("cond_T", 6)[:, 0:16], cond_rows[:, :], 16).then_inc(psum_filled, 1)
            pe.wait_ge(small_in, 16 * 4)
            turn(begin("small_T", 7)[:, 0:P], small_rows[:, :]).then_inc(psum_filled, 1)

        def modulation():
            evacuated(pe, "cond_T")
            with pe.Fori(0, N_MOD // SLOTS) as i:
                for u in range(SLOTS):
                    pe.wait_ge(landed[u], 16 * i + 16)
                    pe.wait_ge(mod_drained, SLOTS * i + u + 1)
                    w = slot(u).rearrange("p (k c) -> p k c", k=KD)
                    for k in range(KD):
                        for q in range(4):
                            mm = pe.matmul(psum[u][32 * q:32 * q + 32, 0:P], s_cols[:, k, :],
                                           w[:, k, P * q:P * q + P], start=(k == 0), stop=(k == KD - 1))
                    mm.then_inc(mod_filled, 1)
            pe.wait_ge(mod_drained, N_MOD + SLOTS)
            pe.wait_ge(mod_back, 64)
            for l in range(2):
                turn(begin(("mod_T", l), l)[:, 0:96], mod_rows[:, l, :], 96).then_inc(psum_filled, 1)

        def modulated_columns():
            pe.wait_ge(pe_added, 1)
            for k in range(KD):
                b = begin(("aT0", 0, k))
                for c in range(CL):
                    mm = turn(b[:, P * c:P * c + P], x_rows[:, c, P * k:P * k + P])
                mm.then_inc(psum_filled, 1)
            pe.wait_ge(ctx_in, 16)
            for k in range(KD):
                b = begin(("aT0", 1, k))
                for c in range(CC):
                    mm = turn(b[:, P * c:P * c + P], x_rows[:, CL + c, P * k:P * k + P])
                mm.then_inc(psum_filled, 1)

        def filter_mlp(j):
            w = (f_w1, f_w2, f_w3)[j]
            x = (zT, hf1, hf2)[j]
            m = 2 * HF if j == 2 else HF
            if j == 0:
                pe.wait_ge(fw_in, 16 * 9)
            else:
                pe.wait_ge(sin_done, j)
            for _, s, n, o in STREAMS:
                pe.matmul(begin(("mlp", j, s))[0:m, 0:n], w, x[:, o:o + n],
                          start=True, stop=True).then_inc(psum_filled, 1)

        def project(ch):
            j, cc = ch // 4, ch % 4
            if ch == 0:
                evacuated(pe, ("aT0", 1, KD - 1))
                evacuated(pe, ("aT0", 0, KD - 1))
            if cc == 0:
                unit_landed(pe, ("hy_in", j))
            w = unit(("hy_in", j)).rearrange("p (k c) -> p k c", k=KD)
            for _, s, n, o in STREAMS:
                b = begin(("proj", s, ch))
                for k in range(KD):
                    mm = pe.matmul(b[:, 0:n], w[:, k, P * cc:P * cc + P], aT[:, k, o:o + n],
                                   start=(k == 0), stop=(k == KD - 1))
                mm.then_inc(psum_filled, 1)

        def token_major(ch):
            pe.wait_ge(conv_done, ch + 1)
            for _, s, n, o in STREAMS:
                b = begin(("tm", s, ch))
                for c in range(n // P):
                    par, q = divmod(c, n // P // 2)
                    mm = turn(b[:, P * c:P * c + P], zc[ch % 2][:, o + 2 * P * q + par:o + 2 * P * (q + 1):2])
                mm.then_inc(psum_filled, 1)

        def filters(i):
            s, half, o = STEPS[i]
            if i == 0:
                pe.wait_ge(hf_done, 1)
                pe.wait_ge(filt_in, 48)
            for tc in range((CL, CC)[s]):
                for a, hf in enumerate((hf_sum, hf_diff)):
                    col = LAT * s + P * tc
                    pe.matmul(begin(("filt", i, tc, a))[:, :], hf[:, col:col + P],
                              w4[:, o, COL * half:COL * half + COL],
                              start=True, stop=True).then_inc(psum_filled, 1)

        def spectra(i):
            s, half, o = STEPS[i]
            n = (CL, CC)[s]
            pe.wait_ge(skip_added, i + 1)
            for a in (0, 1):
                evacuated(pe, ("filt", i, n - 1, a))
            if i == 0:
                unit_landed(pe, ("dft", 0))
            m = n // 2
            for f in range(m):
                parts = [("k", 0, P), ("k", 1, P)] + [("ny", 2, 1)] * (f == 0) + [("k", 2, P), ("k", 3, P)]
                for name, j, rows in parts:
                    a, par = PARTS[j]
                    b = begin((name, j, i, f))
                    src = filt[0] if name == "ny" else filt[a]
                    for c in range(m):
                        mm = pe.matmul(b[0:rows, :], basis(s, 0, a, par)[:, c, P * f:P * f + rows],
                                       src[:, m * par + c, :], start=(c == 0), stop=(c == m - 1))
                    mm.then_inc(psum_filled, 1)
                if f == 0:
                    if o:
                        evacuated(pe, ("y", i - 1, n - 1))
                    elif i == 0:
                        evacuated(pe, ("tm", 0, 15))
                        evacuated(pe, ("tm", 1, 15))
                for j, (a, par) in enumerate(PARTS):
                    b = begin(("x", j, i, f))
                    for c in range(m):
                        mm = pe.matmul(b[:, :], basis(s, 0, a, par)[:, c, P * f:P * f + P],
                                       v_t[:, CL * s + m * par + c, COL * half:COL * half + COL],
                                       start=(c == 0), stop=(c == m - 1))
                    mm.then_inc(psum_filled, 1)

        def inverse(i):
            s, half, o = STEPS[i]
            n = (CL, CC)[s]
            m = n // 2
            pe.wait_ge(z_ready, 6 * chunk_base(i + 1))
            if i == 0:
                unit_landed(pe, ("idft", 0))
            if o == 0:
                for c in range(n):
                    par, q = divmod(c, m)
                    b = begin(("y", i, c))
                    for f in range(m):
                        for a in (0, 1):
                            mm = pe.matmul(b[:, :], basis(s, 1, a, par)[:, f, P * q:P * q + P], z[a][:, par, f, :],
                                           start=(f == 0 and a == 0), stop=(f == m - 1 and a == 1))
                    mm.then_inc(psum_filled, 1)
            else:
                for cc in range(4):
                    b = begin(("y", i, cc))
                    for par in (0, 1):
                        for f in range(m):
                            for a in (0, 1):
                                mm = pe.matmul(b[:, m * P * par:m * P * par + m * P],
                                               z[a][:, par, f, P * cc:P * cc + P], basis(s, 1, a, par)[:, f, :],
                                               start=(f == 0 and a == 0), stop=(f == m - 1 and a == 1))
                    mm.then_inc(psum_filled, 1)

        cond_columns()
        modulation()
        filter_mlp(0)
        modulated_columns()
        for ch in range(24):
            project(ch)
            if ch in (1, 3):
                filter_mlp((ch + 1) // 2)
            if 1 <= ch <= 16:
                token_major(ch - 1)
        filters(0)
        for i in range(len(STEPS)):
            spectra(i)
            if i < last_step:
                filters(i + 1)
            inverse(i)

        def out_project(l, c):
            src = mixed[l]
            w = ("hy_out", "gla_out")[l]
            for half in (0, 1):
                if c == 0:
                    unit_landed(pe, (w, half))
                b = begin(("out", l, c, half))
                wt = unit((w, half)).rearrange("p (k c) -> p k c", k=KD)
                for k in range(KD):
                    mm = pe.matmul(b[:, :], src[:, k, P * c:P * c + P], wt[:, k, :],
                                   start=(k == 0), stop=(k == KD - 1))
                mm.then_inc(psum_filled, 1)

        def route_logits(l, c):
            g = gchunk(l, c)
            pe.wait_ge(a2_done, g + 1)
            for h in (0, 1):
                b = begin(("a2T", l, c, h))
                for k in range(4):
                    mm = turn(b[:, P * k:P * k + P], a2[c % 2][:, P * (4 * h + k):P * (4 * h + k) + P])
                mm.then_inc(psum_filled, 1)
            for h in (0, 1):
                evacuated(pe, ("a2T", l, c, h))
            if c == 0 and l == 0:
                pe.wait_ge(route_in, 48)
            b = begin(("logit", l, c))
            for k in range(KD):
                mm = pe.matmul(b[:, 0:E_N], a2T[:, k, :], router_w[:, k, :],
                               start=(k == 0), stop=(k == KD - 1))
            mm.then_inc(psum_filled, 1)

        def ranks(l):
            n = len(CHUNKS_OF[l])
            pe.wait_ge(picked, l + 1)
            chosen = temps[7]
            b = begin(("rank", l))
            for c in range(n):
                for q in range(c + 1):
                    mm = pe.matmul(b[:, E_N * c:E_N * c + E_N], before if q == 0 else ones,
                              chosen[:, E_N * (c - q):E_N * (c - q) + E_N], start=(q == 0), stop=(q == c))
            mm.then_inc(psum_filled, 1)
            b = begin(("count", l))
            for c in range(n):
                mm = pe.matmul(b[:, 0:E_N], ones, chosen[:, E_N * c:E_N * c + E_N],
                               start=(c == 0), stop=(c == n - 1))
            mm.then_inc(psum_filled, 1)

        def slot_table(l):
            nb = blocks_max((NT, LAT)[l]) + 2
            pe.wait_ge(slots_back, 16 * (l + 1))
            turn(begin(("slots", l))[0:SB, 0:nb], slot_rows[0:nb, :], nb).then_inc(psum_filled, 1)

        def experts(l):
            pX, pG, pH, pY = psum[0], psum[1:3], psum[3:5], psum[5]
            for b in range(6):
                if plan.used[b]:
                    pe.wait_ge(psum_drained[b], plan.used[b])
            pe.wait_ge(starts_done, l + 1)

            def turn_rows():
                for k in range(KD):
                    mm = turn(pX[:, SB * k:SB * k + SB], x_slots[:, P * k:P * k + P], SB)
                mm.then_inc(x_turned[l], 1)

            pe.wait_ge(x_moved[l], 1)
            turn_rows()
            with pe.Fori(0, E_N // 2) as pair:
                for par in (0, 1):
                    lo = pe.value_load(starts[:, ds(2 * pair + par, 1)], min_val=0, max_val=blocks_max(NT))
                    hi = pe.value_load(starts[:, ds(2 * pair + par + 1, 1)], min_val=1, max_val=blocks_max(NT))
                    s = 3 * par
                    w13 = ring[:, s * UNIT:(s + 2) * UNIT].rearrange("p (m k c) -> p m k c", m=2, k=KD)
                    w2 = slot(s + 2).rearrange("p (f c) -> p f c", f=4)
                    with pe.Fori(lo, hi) as b:
                        for q in (0, 1):
                            pe.wait_ge(landed[s + q], 16 * pair + 16 * (moe_first[l][s + q] + 1))
                        pe.wait_ge(xT_done[l], b + 1)
                        for c in (0, 1):
                            for k in range(KD):
                                for half in (0, 1):
                                    col = 256 * half + P * c
                                    mm = pe.matmul(pG[c][SB * half:SB * half + SB, 0:256].rearrange(
                                        "p (m c) -> p m c", m=2), xT[:, k, :], w13[:, :, k, col:col + P],
                                        start=(k == 0), stop=(k == KD - 1))
                            mm.then_inc(up_filled[l], 1)
                        pe.wait_ge(x_moved[l], b + 2)
                        pe.wait_ge(hid_done[l], 2 * b + 1)
                        turn(pH[0][:, 0:P], hid[0]).then_inc(hid_turned[l], 1)
                        turn_rows()
                        pe.wait_ge(hid_done[l], 2 * b + 2)
                        turn(pH[1][:, 0:P], hid[1]).then_inc(hid_turned[l], 1)
                        pe.wait_ge(landed[s + 2], 16 * pair + 16 * (moe_first[l][s + 2] + 1))
                        pe.wait_ge(y_copied[l], b + 1)
                        for c in (0, 1):
                            pe.wait_ge(hidT_done[l], 2 * b + c + 1)
                            for f in (0, 1):
                                for half in (0, 1):
                                    mm = pe.matmul(pY[SB * half:SB * half + SB, :],
                                                   hidT[c][:, SB * f:SB * f + SB],
                                                   w2[:, 2 * f + c, COL * half:COL * half + COL],
                                                   start=(c == 0 and f == 0), stop=(c == 1 and f == 1))
                        mm.then_inc(y_filled[l], 1)
            total = pe.value_load(starts[:, E_N:E_N + 1], min_val=1, max_val=blocks_max(NT))
            pe.wait_ge(xT_done[l], total + 1)
            pe.wait_ge(y_copied[l], total + 1)
            pe.wait_ge(starts_done, l + 1)

        def finish(l):
            last = len(CHUNKS_OF[l]) - 1
            for c in CHUNKS_OF[l]:
                out_project(l, c)
                if c:
                    route_logits(l, c - 1)
            route_logits(l, last)
            ranks(l)
            slot_table(l)
            experts(l)

        evacuated(pe, ("y", last_step, 3))
        finish(0)

        def columns1():
            pe.wait_ge(h_next, 6)
            for s, chunks in ((0, range(CL)), (1, range(CL, 6))):
                for k in range(KD):
                    b = begin(("aT1", s, k))
                    for i, c in enumerate(chunks):
                        mm = turn(b[:, P * i:P * i + P], h_rows[:, c, P * k:P * k + P])
                    mm.then_inc(psum_filled, 1)

        def low_rank():
            pe.wait_ge(gla_in, 16 * 4)
            for s in (0, 1):
                for k in range(KD):
                    evacuated(pe, ("aT1", s, k))
            for _, s, n, o in STREAMS:
                b = begin(("lr", s))
                for k in range(KD):
                    mm = pe.matmul(b[0:32, 0:n], lr_w[:, k, :], aT_l[1][:, k, o:o + n],
                                   start=(k == 0), stop=(k == KD - 1))
                mm.then_inc(psum_filled, 1)

        def gates(hd):
            if hd == 0:
                evacuated(pe, ("lr", 0))
                evacuated(pe, ("lr", 1))
                pe.wait_ge(zero_w, 1)
            for r in (0, 1):
                for _, s, n, o in STREAMS:
                    pe.matmul(begin(("g", hd, r, s))[:, 0:n], gate_w[r][:, P * hd:P * hd + P], lrT[:, o:o + n],
                              start=True, stop=True).then_inc(psum_filled, 1)

        def queries_keys():
            for m in (0, 1):
                unit_landed(pe, ("gla_in", m))
                w = unit(("gla_in", m)).rearrange("p (k c) -> p k c", k=KD)
                for hd in range(HEADS):
                    for _, s, n, o in STREAMS[:1 + m]:
                        b = begin(("qk", m, hd, s))
                        for k in range(KD):
                            mm = pe.matmul(b[:, 0:n], w[:, k, P * hd:P * hd + P], aT_l[1][:, k, o:o + n],
                                           start=(k == 0), stop=(k == KD - 1))
                        mm.then_inc(psum_filled, 1)

        def value_gate(name):
            kind, half, c = name
            j = (2 if kind == "v" else 4) + half
            if c == 0:
                unit_landed(pe, ("gla_in", j))
            w = unit(("gla_in", j)).rearrange("p (k c) -> p k c", k=KD)
            b = begin(name)
            for k in range(KD):
                mm = pe.matmul(b[:, :], aT_l[1][:, k, P * c:P * c + P], w[:, k, :],
                               start=(k == 0), stop=(k == KD - 1))
            mm.then_inc(psum_filled, 1)

        def attention(i):
            hd, lv = ITEMS[i]
            if lv == 0:
                q, key = qk[:, hd, 0, :], qk[:, hd, 1, :]
                evacuated(pe, ("qk", 0, hd, 0))
                evacuated(pe, ("qk", 1, hd, 0))
            else:
                q, key = lev[i % 3][:, 0:LAT], lev[i % 3][:, LAT:2 * LAT]
                pe.wait_ge(scaled_qk, scaled_items(i))
            if lv <= LEVELS + 1:
                b = begin(("att", i, 0))
                for s in range(CL):
                    u = s if lv <= LEVELS else s ^ 1
                    mm = pe.matmul(b[:, P * s:P * s + P], key[:, P * s:P * s + P], q[:, P * u:P * u + P],
                                   start=True, stop=True)
                mm.then_inc(psum_filled, 1)
            elif lv == LEVELS + 2:
                for h in (0, 1):
                    b = begin(("att", i, h))
                    for s in (0, 1):
                        sb, u = 2 * h + s, 2 * (1 - h)
                        mm = pe.matmul(b[:, 2 * P * s:2 * P * s + 2 * P], key[:, P * sb:P * sb + P],
                                       q[:, P * u:P * u + 2 * P], start=True, stop=True)
                    mm.then_inc(psum_filled, 1)
            elif lv == LV_CTX:
                b = begin(("kt", hd))
                for j in range(4):
                    mm = turn(b[:, P * j:P * j + P], lev[i % 3][:, P * j:P * j + P])
                mm.then_inc(psum_filled, 1)
            else:
                context_state(hd)
                outputs(i, hd)

        def context_state(hd):
            evacuated(pe, ("kt", hd))
            for c in (CL, CL + 1):
                evacuated(pe, ("v", hd // 2, c))
            b = begin(("st", hd))
            for r in (0, 1):
                for c in range(CC):
                    mm = pe.matmul(b[:, DVH * r:DVH * r + DVH], kt_rows[:, P * (CC * r + c):P * (CC * r + c) + P],
                                   v_rows[:, CL + c, DVH * hd:DVH * hd + DVH], start=(c == 0), stop=(c == CC - 1))
            mm.then_inc(psum_filled, 1)

        def outputs(i, hd):
            q = lev[i % 3]
            evacuated(pe, ("st", hd))
            pe.wait_ge(near_done, LEVELS * (hd + 1))
            for s in range(CL):
                evacuated(pe, ("v", hd // 2, s))
            j = i - 2
            evacuated(pe, ("att", j - 1, 0))
            evacuated(pe, ("att", j - 2, 0))
            evacuated(pe, ("att", N_LV * hd, 0))
            for h in (0, 1):
                evacuated(pe, ("att", j, h))
            for u in range(CL):
                b = begin(("o", hd, u))
                for s in range(CL):
                    if s == u:
                        a = att_near[:, P * s:P * s + P]
                    elif s == u ^ 1:
                        a = att_next[:, P * s:P * s + P]
                    else:
                        a = att_far[:, 2 * P * s + P * (u % 2):2 * P * s + P * (u % 2) + P]
                    pe.matmul(b[:, 0:DVH], a, v_rows[:, s, DVH * hd:DVH * hd + DVH], start=(s == 0), stop=False)
                for r in (0, 1):
                    mm = pe.matmul(b[:, 0:DVH], q[:, LAT * r + P * u:LAT * r + P * u + P], state[:, r, :],
                                   start=False, stop=(r == 1))
                mm.then_inc(psum_filled, 1)

        def output_columns():
            pe.wait_ge(y_rows_done, CL)
            for k in range(KD):
                b = begin(("yT", k))
                for c in range(CL):
                    mm = turn(b[:, P * c:P * c + P], r_rows[:, c, P * k:P * k + P])
                mm.then_inc(psum_filled, 1)
            for k in range(KD):
                evacuated(pe, ("yT", k))

        columns1()
        low_rank()
        queries_keys()
        gates(0)
        for i, (hd, lv) in enumerate(ITEMS):
            for name in PROJ_AT.get((hd, lv), []):
                value_gate(name)
            attention(i)
            if lv == 5 and hd + 1 < HEADS:
                gates(hd + 1)
        output_columns()
        finish(1)

    @block.scalar
    def _(act):
        links = [0]

        def link(ins):
            ins.then_inc(act_link, 1)
            links[0] += 1
            act.wait_ge(act_link, links[0])

        def early_loads():
            act.dma_start(keep[:, 0:128], t["ident"]).then_inc(keep_in, 16)
            act.dma_start(cond_rows[0:8, :], t["c"].rearrange("b (k p) -> (b k) p", p=P)).then_inc(cond_in, 16)
            act.dma_start(cond_rows[8:16, :], t["c_ctx"].rearrange("(k p) -> k p", p=P)).then_inc(cond_in, 16)
            act.dma_start(keep[:, 1984:1987], t["marks"]).then_inc(keep_in, 16)
            act.dma_start(small_rows[0:72, :],
                          t["hy_conv_w"].rearrange("o j (c p) -> (o j c) p", p=P)).then_inc(small_in, 16)
            act.dma_start(small_rows[72:96, :],
                          t["hy_b_in"].rearrange("o (c p) -> (o c) p", p=P)).then_inc(small_in, 16)
            act.dma_start(small_rows[96:120, :],
                          t["hy_conv_b"].rearrange("o (c p) -> (o c) p", p=P)).then_inc(small_in, 16)
            act.dma_start(small_rows[120:128, :],
                          t["gla_b_gate"].rearrange("o r (c p) -> (o r c) p", p=P)).then_inc(small_in, 16)
            act.wait_ge(mod_zeroed, 1)
            bias = t["b_mod"].rearrange("l (n q c) -> q (l n) c", q=4, c=P)
            for q in range(4):
                for r in range(2):
                    act.dma_start(mod_acc[32 * q + r:32 * q + r + 1, :, :],
                                  bias[q:q + 1]).then_inc(bias_in, 16)
            act.dma_start(x_rows[:, 0:CL, :],
                          t["x"].rearrange("b (c p) d -> p (b c) d", p=P)).then_inc(x_in, 16)
            act.dma_start(pe_rows, t["pos"].rearrange("(c p) d -> p c d", p=P)).then_inc(pe_in, 16)
            act.dma_start(x_rows[:, CL:6, :],
                          t["ctx"].rearrange("b (c p) d -> p (b c) d", p=P)).then_inc(ctx_in, 16)
            act.dma_start(zT, t["zT"]).then_inc(fw_in, 16)
            act.dma_start(f_w1, t["hy_f_w1"][0]).then_inc(fw_in, 16)
            act.dma_start(f_w2, t["hy_f_w2"][0]).then_inc(fw_in, 16)
            for i in (0, 1):
                act.dma_start(f_w3[:, HF * i:HF * i + HF], t["hy_f_w3"][0]).then_inc(fw_in, 16)
            act.dma_start(f_b[0:HF, 0:1], t["hy_f_b1"].rearrange("o p -> p o")).then_inc(fw_in, 16)
            act.dma_start(f_b[0:HF, 1:2], t["hy_f_b2"].rearrange("o p -> p o")).then_inc(fw_in, 16)
            for i in (0, 1):
                act.dma_start(f_b[HF * i:HF * i + HF, 2:3],
                              t["hy_f_b3"].rearrange("o p -> p o")).then_inc(fw_in, 16)

        def cond():
            act.wait_ge(cond_in, 32)
            act.activation(cond_rows, cond_rows, ACT.Silu).then_inc(cond_silu, 1)

        def store_mod():
            act.wait_ge(mod_drained, N_MOD + SLOTS)
            for q in range(4):
                act.dma_start(mod_d[:, :, q, :], mod_acc[32 * q:32 * q + 2, :, :]).then_inc(mod_stored, 16)
            act.wait_ge(mod_stored, 64)
            for l in range(2):
                for r in range(2):
                    rows = mod_d[r, 12 * l:12 * l + 12].rearrange("n q c -> (n q) c")
                    act.dma_start(mod_rows[48 * r:48 * r + 48, l, :], rows).then_inc(mod_back, 16)

        def store_h0():
            act.wait_ge(pe_added, 1)
            act.dma_start(h0_d.rearrange("(c p) d -> p c d", p=P), x_rows[:, 0:CL, :]).then_inc(h0_stored, 16)

        def sines(j):
            m = 2 * HF if j == 2 else HF
            dst = (hf1, hf2, hf_sum)[j]
            act.wait_ge(sin_arg, j + 1)
            act.activation(dst[0:m, :], arg_u[0:m, :], ACT.Sin).then_inc(sin_done, 1)

        def biased(ch):
            if ch == 0:
                act.wait_ge(edges_zeroed, 4)
                evacuated(act, "small_T")
            if ch >= 2:
                act.wait_ge(conv_done, ch - 1)
            tap = taps[ch % 2]
            for _, s, n, o in STREAMS:
                name = ("proj", s, ch)
                filled(act, name)
                lo = 1 + s * (LAT + 2)
                act.activation(tap[:, lo:lo + n], res(name)[:, 0:n], ACT.Identity,
                               bias=b_in(ch)).then_inc(drained(name), 1)

        def gather_rows(ch):
            if ch == 0:
                act.wait_ge(h0_stored, 16)
            dst = (v_t, x1_t)[ch // 8]
            for _, s, n, o in STREAMS:
                name = ("tm", s, ch)
                filled(act, name)
                act.copy(dst[:, CL * s:CL * s + n // P, P * (ch % 8):P * (ch % 8) + P],
                         res(name)[:, 0:n].rearrange("p (c x) -> p c x", x=P)).then_inc(drained(name), 1)

        def load_windows(i):
            s, half, o = STEPS[i]
            n = (CL, CC)[s]
            if i == 0:
                filled(act, ("proj", 1, 23))
            if i:
                act.wait_ge(skip_added, i)
            act.dma_start(skip_row, t["hy_skip"][0, o:o + 1, COL * half:COL * half + COL]).then_inc(skip_in, 16)
            for tc in range(n):
                g = win_loads[0]
                if g >= 2:
                    evacuated(act, win_use[g - 2])
                act.dma_start(win[g % 2], t[("window_lat", "window_ctx")[s]][
                    P * tc:P * tc + P, COL * half:COL * half + COL]).then_inc(win_in[g % 2], 16)
                win_loads[0] += 1

        win_loads = [0]
        win_use = [("filt", i, tc, 1) for i in range(len(STEPS)) for tc in range((CL, CC)[STEPS[i][0]])]

        def keep_spectra(i):
            for f in range(FREQ[STEPS[i][0]]):
                g = chunk_base(i) + f
                if g >= 2:
                    made(act, g - 1)
                if f == 0 and i:
                    made(act, chunk_base(i - 1) + 1)
                if g == 0:
                    filled(act, ("proj", 1, 23))
                k = k_parts[g % 2]
                for j in range(4):
                    name = ("k", j, i, f)
                    filled(act, name)
                    if f:
                        act.copy(k[:, j, :], res(name)[:, :]).then_inc(drained(name), 1)
                    elif j == 0:
                        act.copy(k_alt[:, 0, :], res(name)[:, :])
                        act.copy(k[:, 0, :], res(name)[:, :]).then_inc(drained(name), 1)
                    elif j == 1:
                        act.copy(k_alt[:, 1, :], res(name)[:, :])
                        act.copy(k_alt[:, 2, :], res(name)[:, :])
                        act.copy(k[:, 1, :], res(name)[:, :]).then_inc(drained(name), 1)
                        evacuated(act, ("k", 0, i, f))
                        filled(act, ("ny", 2, i, f))
                        act.copy(k_alt[0:1, 0, :], res(("ny", 2, i, f))[0:1, :]).then_inc(
                            drained(("ny", 2, i, f)), 1)
                    elif j == 2:
                        act.activation(k[:, 2, :], res(name)[:, :], ACT.Copy, scale=rowmask).then_inc(drained(name), 1)
                    else:
                        evacuated(act, ("k", 1, i, f))
                        act.activation(k_alt[0:1, 1, :], res(name)[0:1, :], ACT.Copy, scale=-1.0)
                        act.copy(k_alt[0:1, 2, :], res(name)[0:1, :])
                        act.activation(k[:, 3, :], res(name)[:, :], ACT.Copy, scale=rowmask).then_inc(drained(name), 1)

        early_loads()
        cond()
        store_h0()
        store_mod()
        for ch in range(24):
            if ch == 2:
                sines(1)
            if ch == 4:
                sines(2)
            if ch == 0:
                sines(0)
            biased(ch)
            if 1 <= ch <= 16:
                gather_rows(ch - 1)
        load_windows(0)
        for i in range(len(STEPS)):
            keep_spectra(i)
            if i < last_step:
                load_windows(i + 1)

        def load_vectors(l):
            def put(dst, row):
                act.dma_start(dst, row.partition_broadcast(P)).then_inc(bc_in, 16)

            def mod_row(r, v):
                return mod_d[r, 12 * l + 2 * v:12 * l + 2 * v + 2].rearrange("n q c -> (n q c)")

            vec = {"lng": t["ln_g"][l, 0], "lnb": t["ln_b"][l, 0], "g1l": mod_row(0, 2), "sh2l": mod_row(0, 3),
                   "sc2l": mod_row(0, 4)}
            if l == 0:
                vec.update({"bout": t["hy_b_out"][0], "g1c": mod_row(1, 2), "sh2c": mod_row(1, 3),
                            "sc2c": mod_row(1, 4)})
            for n in BC[l]:
                put(bcast[l][n], vec[n])

        def load_vectors2(l):
            def mod_row(r, v):
                return mod_d[r, 12 * l + 2 * v:12 * l + 2 * v + 2].rearrange("n q c -> (n q c)")

            for n, row in (("g2l", mod_row(0, 5)), ("g2c", mod_row(1, 5)), ("lng", t["ln_g"][l, 1]),
                           ("lnb", t["ln_b"][l, 1])):
                act.dma_start(bc2[n], row.partition_broadcast(P)).then_inc(bc2_in, 16)

        def load_router():
            filled(act, ("filt", last_step, CC - 1, 1))
            act.dma_start(router_w, t["router_w"].rearrange("(k p) e -> p k e", p=P)).then_inc(route_in, 16)
            act.dma_start(router_b, t["router_b"].partition_broadcast(P)).then_inc(route_in, 16)
            act.dma_start(keep[:, 416:690], t["route_c"]).then_inc(route_in, 16)

        def load_resid(l, c):
            if gchunk(l, c):
                act.wait_ge(res_used, gchunk(l, c))
            src = (h0_d, h1_d)[l][P * c:P * c + P] if c < CL else t["ctx"][0, P * (c - CL):P * (c - CL) + P]
            act.dma_start(resid, src).then_inc(res_in, 16)

        def deviation(n):
            act.wait_ge(var_ready, n)
            act.activation(dev, mean_var[:, 1:2], ACT.Sqrt, bias=eps).then_inc(dev_done, 1)

        def store_tokens(l, c):
            act.wait_ge(a2_done, gchunk(l, c) + 1)
            act.dma_start(tok_l[l][P * c:P * c + P], a2[c % 2]).then_inc(tok_stored, 16)

        def route_scores(l, c):
            for h in (0, 1):
                filled(act, ("a2T", l, c, h))
                act.copy(a2T[:, 4 * h:4 * h + 4, :], res(("a2T", l, c, h))[:, :].rearrange(
                    "p (k n) -> p k n", k=4)).then_inc(drained(("a2T", l, c, h)), 1)
            filled(act, ("logit", l, c))
            act.activation(scores[:, E_N * c:E_N * c + E_N], res(("logit", l, c))[:, 0:E_N],
                           ACT.Sigmoid).then_inc(drained(("logit", l, c)), 1)

        def scale_first(l, c):
            if c == 0:
                act.wait_ge(combine_go, l + 1)
            else:
                if c >= 2:
                    act.wait_ge(var_ready, norm2(l, c - 2))
            act.wait_ge(pair_in[c], 32 * (l + 1))
            act.activation(mix[c % 2], y_pair[c][0], ACT.Copy, scale=pair_w[:, 0, c:c + 1]).then_inc(first_scaled, 1)

        def store_out(c):
            act.wait_ge(h_next, gchunk(1, c) + 1)
            act.dma_start(out[0, P * c:P * c + P], h_rows[:, c, :]).then_inc(out_stored, 16)

        def clear_slots(l):
            act.wait_ge(slot_zero, l + 1)
            nb = blocks_max((NT, LAT)[l]) + 2
            act.dma_start(slot_l[l].rearrange("(b s) o -> b (s o)", s=SB), slot_rows[0:nb, :]).then_inc(slot_cleared, 16)

        def read_slots(l):
            n = 2 * (len(CHUNKS_OF[0]) if l == 0 else len(CHUNKS_OF[0]) + len(CHUNKS_OF[1]))
            act.wait_ge(scattered, 16 * n)
            nb = blocks_max((NT, LAT)[l]) + 2
            act.dma_start(slot_rows[0:nb, :], slot_l[l].rearrange("(b s) o -> b (s o)", s=SB)).then_inc(slots_back, 16)

        def experts(l):
            pG, pY = psum[1:3], psum[5]
            act.wait_ge(starts_done, l + 1)
            total = act.value_load(starts[:, E_N:E_N + 1], min_val=1, max_val=blocks_max(NT))
            with act.Fori(0, total) as b:
                for c in (0, 1):
                    act.wait_ge(up_filled[l], 2 * b + c + 1)
                    act.activation(gate_act[c], pG[c][:, 0:P], ACT.Silu).then_inc(gate_done[l], 1)
                act.wait_ge(y_stored[l], 32 * b + 32)
                act.wait_ge(y_filled[l], b + 1)
                act.copy(y_out, pY[:, :]).then_inc(y_copied[l], 1)
                act.wait_ge(y_copied[l], b + 2)
                rows = y_d.rearrange("(b s) d -> b s d", s=SB)[ds(b, 1)].rearrange("o s d -> (o s) d")
                for half in (0, 1):
                    act.dma_start(rows[:, COL * half:COL * half + COL],
                                  y_out[SB * half:SB * half + SB, :]).then_inc(y_stored[l], 16)

        def finish(l):
            chunks = CHUNKS_OF[l]
            for c in chunks:
                load_resid(l, c)
                deviation(gchunk(l, c) + 1 + 6 * l)
                if c:
                    route_scores(l, c - 1)
                store_tokens(l, c)
            route_scores(l, chunks[-1])
            clear_slots(l)
            read_slots(l)
            load_vectors2(l)
            experts(l)
            scale_first(l, 0)
            for c in chunks:
                if c + 1 in chunks:
                    scale_first(l, c + 1)
                deviation(norm2(l, c))
                if l and c:
                    store_out(c - 1)
            if l:
                store_out(chunks[-1])

        load_router()
        filled(act, ("x", 3, last_step, FREQ[1] - 1))
        evacuated(act, ("y", last_step - 1, CC - 1))
        load_vectors(0)
        filled(act, ("y", last_step, 3))
        finish(0)

        def spill():
            for c in range(CL):
                act.wait_ge(h_next, c + 1)
                act.dma_start(h1_d[P * c:P * c + P], h_rows[:, c, :]).then_inc(h1_stored, 16)

        def load_gla():
            filled(act, ("aT1", 1, KD - 1))
            act.dma_start(lr_w, t["gla_w_in"][0, :, 3072:3104].rearrange("(k p) c -> p k c", p=P)).then_inc(gla_in, 16)
            act.wait_ge(zero_w, 2)
            for r in (0, 1):
                act.dma_start(gate_w[r][16 * r:16 * r + 16, :], t["gla_w_gate"][0, r]).then_inc(gla_in, 16)
            act.dma_start(masks, t["masks"].rearrange("p (l n) -> p l n", n=P)).then_inc(gla_in, 16)
            for _, s, n, o in STREAMS:
                filled(act, ("lr", s))
                act.copy(lrT[:, o:o + n], res(("lr", s))[0:32, 0:n]).then_inc(drained(("lr", s)), 1)

        def gates(hd):
            for r in (0, 1):
                n_dir = 2 * hd + r
                if n_dir:
                    act.wait_ge(cum_done, 2 * n_dir)
                for _, s, n, o in STREAMS:
                    filled(act, ("g", hd, r, s))
                    act.activation(soft[:, o:o + n], res(("g", hd, r, s))[:, 0:n], ACT.Abs,
                                   bias=smallT[:, 120 + 4 * r + hd:121 + 4 * r + hd]).then_inc(gates_abs, 1)
                act.wait_ge(gates_abs, 2 * n_dir + 2)
                link(act.activation(soft, soft, ACT.Exp, scale=-1.0))
                act.activation(soft, soft, ACT.Ln, bias=1.0).then_inc(gates_ln, 1)

        def evac_qk():
            for m in (0, 1):
                for hd in range(HEADS):
                    for _, s, n, o in STREAMS[:1 + m]:
                        name = ("qk", m, hd, s)
                        filled(act, name)
                        dst = k_ctx[:, hd, :] if s else qk[:, hd, m, :]
                        act.activation(dst, res(name)[:, 0:n], ACT.Copy,
                                       scale=(1.0 if m else float(DKH) ** -0.5)).then_inc(drained(name), 1)

        def evac_value(name):
            kind, half, c = name
            dst = (v_rows if kind == "v" else r_rows)[:, c, COL * half:COL * half + COL]
            if kind == "r" and half == 0 and c == 0:
                act.wait_ge(h1_stored, 16 * CL)
            filled(act, name)
            act.copy(dst, res(name)[:, :]).then_inc(drained(name), 1)

        def exponentials(i):
            hd, lv = ITEMS[i]
            if lv == 0:
                return
            if lv == LV_STATE:
                buffer_free(act, i)
                act.activation(lev[i % 3].rearrange("p (r n) -> p r n", r=2), cums[hd % 2][:, :, 0:LAT],
                               ACT.Exp, scale=1.0 / TAU).then_inc(exps_done, 1)
            else:
                n = 2 * CTX if lv == LV_CTX else 2 * LAT
                act.wait_ge(args_done, arg_items(i))
                act.activation(lev[i % 3][:, 0:n], lev[i % 3][:, 0:n], ACT.Exp,
                               scale=1.0 / TAU).then_inc(exps_done, 1)

        def after_item(i):
            hd, lv = ITEMS[i]
            if lv == LEVELS + 2:
                for h in (0, 1):
                    filled(act, ("att", i, h))
                    act.copy(att_far[:, COL * h:COL * h + COL], res(("att", i, h))[:, :]).then_inc(
                        drained(("att", i, h)), 1)
            if lv == LV_CTX:
                filled(act, ("kt", hd))
                act.copy(kt_rows, res(("kt", hd))[:, :]).then_inc(drained(("kt", hd)), 1)
            if lv == LV_STATE:
                filled(act, ("st", hd))
                act.copy(state.rearrange("p r n -> p (r n)"), res(("st", hd))[:, :]).then_inc(drained(("st", hd)), 1)

        def head_deviation(hd):
            act.wait_ge(o_var, CL * (hd + 1))
            act.activation(g_dev, g_mv[:, :, 1], ACT.Sqrt, bias=eps).then_inc(o_dev, 1)

        def gla_tail():
            for c in range(CL):
                for half in (0, 1):
                    evacuated(act, ("r", half, c))
                act.activation(r_rows[:, c, :], r_rows[:, c, :], ACT.Silu).then_inc(silu_done, 1)
            for k in range(0, KD, 2):
                filled(act, ("yT", k))
                act.copy(mixed[1][:, k, :], res(("yT", k))[:, :]).then_inc(drained(("yT", k)), 1)

        spill()
        load_gla()
        evac_qk()
        gates(0)
        exponentials(1)
        for i, (hd, lv) in enumerate(ITEMS):
            if i and i + 1 < len(ITEMS):
                exponentials(i + 1)
            for name in PROJ_AT.get((hd, lv), []):
                evac_value(name)
            after_item(i)
            if lv == 5 and hd + 1 < HEADS:
                gates(hd + 1)
            if lv == 2 and hd:
                head_deviation(hd - 1)
        head_deviation(HEADS - 1)
        filled(act, ("r", 1, CL - 1))
        act.dma_start(norm_g, t["gla_norm_g"][0].partition_broadcast(P)).then_inc(norm_in, 16)
        gla_tail()
        filled(act, ("o", HEADS - 1, CL - 1))
        load_vectors(1)
        finish(1)

    @block.vector
    def _(dve):
        links = [0]

        def link(ins):
            ins.then_inc(dve_link, 1)
            links[0] += 1
            dve.wait_ge(dve_link, links[0])

        def start():
            dve.memset(mod_acc, 0.0).then_inc(mod_zeroed, 1)
            dve.memset(s_cols, 0.0).then_inc(cols_zeroed, 1)
            filled(dve, "cond_T")
            dve.wait_ge(cols_zeroed, 1)
            dve.tensor_copy(s_cols[:, :, 0:2], res("cond_T")[:, 0:16].rearrange("p (r k) -> p k r", r=2)) \
               .then_inc(drained("cond_T"), 1)
            filled(dve, "small_T")
            dve.tensor_copy(smallT, res("small_T")[:, 0:P]).then_inc(drained("small_T"), 1)
            dve.memset(keep[:, 1987:1988], 0.0).then_inc(mod_drained, SLOTS)

        def modulation():
            dve.wait_ge(bias_in, 16 * 8)
            dve.wait_ge(mod_zeroed, 1)
            with dve.Fori(0, N_MOD // SLOTS) as i:
                for u in range(SLOTS):
                    dve.wait_ge(mod_filled, SLOTS * i + u + 1)
                    cols = mod_acc[:, ds(SLOTS * i + u, 1), :].rearrange("p o c -> p (o c)")
                    dve.tensor_tensor(cols, psum[u][:, 0:P], cols, ALU.add).then_inc(mod_drained, 1)
            for l in range(2):
                filled(dve, ("mod_T", l))
                dve.tensor_copy(modT[:, l], res(("mod_T", l))[:, 0:96].rearrange(
                    "p (r v k) -> p r v k", r=2, v=6)).then_inc(drained(("mod_T", l)), 1)
            evacuated(dve, ("mod_T", 0))
            evacuated(dve, ("mod_T", 1))
            for l in range(2):
                scale = modT[:, l, :, 1, :]
                dve.tensor_scalar(scale, scale, 1.0, None, ALU.add).then_inc(modT_done, 1)

        def modulated(l, names):
            dve.wait_ge(modT_done, 2)
            for s, k in names:
                name = (f"aT{l}", s, k)
                n, o = ((LAT, 0), (CTX, LAT))[s]
                filled(dve, name)
                dve.tensor_scalar(aT_l[l][:, k, o:o + n], res(name)[:, 0:n], modT[:, l, s, 1, k:k + 1],
                                  modT[:, l, s, 0, k:k + 1], ALU.mult, ALU.add).then_inc(drained(name), 1)

        def sine_argument(j):
            m = 2 * HF if j == 2 else HF
            u, r = arg_u[0:m, :], arg_t[0:m, :]
            if j == 0:
                dve.wait_ge(fw_in, 16 * 9)
            else:
                dve.wait_ge(sin_done, j)
            for _, s, n, o in STREAMS:
                name = ("mlp", j, s)
                filled(dve, name)
                dve.tensor_scalar(u[:, o:o + n], res(name)[0:m, 0:n], f_b[0:m, j:j + 1], None,
                                  ALU.add).then_inc(drained(name), 1)
            evacuated(dve, ("mlp", j, 0))
            evacuated(dve, ("mlp", j, 1))
            link(dve.tensor_scalar(r, u, float(1.0 / (2.0 * np.pi)), MAGIC, ALU.mult, ALU.add))
            link(dve.tensor_scalar(r, r, MAGIC, None, ALU.subtract))
            link(dve.scalar_tensor_tensor(u, r, -PI2_HI, u, ALU.mult, ALU.add))
            link(dve.scalar_tensor_tensor(u, r, -PI2_LO, u, ALU.mult, ALU.add))
            dve.tensor_scalar(u, u, 3.1415925, -3.1415925, ALU.min, ALU.max).then_inc(sin_arg, 1)

        def short_conv(ch):
            if ch == 0:
                dve.wait_ge(mod_stored, 64)
            if ch < 16:
                dst = zc[ch % 2]
                if ch >= 2:
                    filled(dve, ("tm", 1, ch - 2))
            else:
                dst = x2T[:, ch - 16, :]
                if ch == 16:
                    filled(dve, ("tm", 1, 15))
            parts = []
            for _, s, n, o in STREAMS:
                evacuated(dve, ("proj", s, ch))
                tap = taps[ch % 2][:, s * (LAT + 2):s * (LAT + 2) + n + 2]
                parts.append((dst[:, o:o + n], tap, n))
            for y, tap, n in parts:
                ins = dve.tensor_scalar(y, tap[:, 1:n + 1], conv_w(1, ch), conv_b(ch), ALU.mult, ALU.add)
                ins.then_inc(dve_link, 1)
                links[0] += 1
            dve.wait_ge(dve_link, links[0])
            for y, tap, n in parts:
                ins = dve.scalar_tensor_tensor(y, tap[:, 0:n], conv_w(0, ch), y, ALU.mult, ALU.add)
                ins.then_inc(dve_link, 1)
                links[0] += 1
            dve.wait_ge(dve_link, links[0])
            (y0, tap0, n0), (y1, tap1, n1) = parts
            ins = dve.scalar_tensor_tensor(y0, tap0[:, 2:n0 + 2], conv_w(2, ch), y0, ALU.mult, ALU.add)
            link(ins)
            dve.scalar_tensor_tensor(y1, tap1[:, 2:n1 + 2], conv_w(2, ch), y1, ALU.mult,
                                     ALU.add).then_inc(conv_done, 1)

        windows = [0]

        def windowed(i):
            s, half, o = STEPS[i]
            n = (CL, CC)[s]
            for tc in range(n):
                g = windows[0]
                dve.wait_ge(win_in[g % 2], 16 * (g // 2 + 1))
                for a in (0, 1):
                    name = ("filt", i, tc, a)
                    filled(dve, name)
                    dve.tensor_tensor(filt[a][:, tc, :], res(name)[:, :], win[g % 2],
                                      ALU.mult).then_inc(drained(name), 1)
                windows[0] += 1
            evacuated(dve, ("filt", i, 0, 0))
            dve.wait_ge(skip_in, 16 * (i + 1))
            dve.tensor_tensor(filt[0][0:1, 0, :], filt[0][0:1, 0, :], skip_row, ALU.add).then_inc(skip_added, 1)

        def multiply(i):
            for f in range(FREQ[STEPS[i][0]]):
                g = chunk_base(i) + f
                for j in range(4):
                    evacuated(dve, ("k", j, i, f))
                if f == 0:
                    evacuated(dve, ("ny", 2, i, f))
                ec, oc, es, os = (k_parts[g % 2][:, j, :] for j in range(4))
                ec_s, oc_s, oc_d = (ec, oc, oc) if f else (k_alt[:, j, :] for j in range(3))
                factors = ((ec, oc, es, os), (oc, ec, os, es), (es, os, ec_s, oc_d), (os, es, oc_s, ec_s))
                for j in range(4):
                    if j and g:
                        dve.wait_ge(z_ready, 6 * (g - 1) + 2 * j)
                    name = ("x", j, i, f)
                    filled(dve, name)
                    for q, (a, par) in enumerate(PARTS):
                        dst = terms[j][:, a, par, :] if j else z[a][:, par, f, :]
                        ins = dve.tensor_tensor(dst, res(name)[:, :], factors[j][q], ALU.mult)
                    ins.then_inc(drained(name), 1)

        def gated(i):
            s, half, o = STEPS[i]
            n = (CL, CC)[s]
            if i == 0:
                evacuated(dve, ("tm", 0, 15))
                evacuated(dve, ("tm", 1, 15))
            if o == 0:
                for c in range(n):
                    name = ("y", i, c)
                    filled(dve, name)
                    cols = slice(COL * half, COL * half + COL)
                    dve.tensor_tensor(v_t[:, CL * s + c, cols], res(name)[:, :], x1_t[:, CL * s + c, cols],
                                      ALU.mult).then_inc(drained(name), 1)
            else:
                for cc in range(4):
                    name = ("y", i, cc)
                    filled(dve, name)
                    dst = x2T[:, 4 * half + cc, LAT * s:LAT * s + n * P].rearrange("p (n r) -> p r n", r=2)
                    y = res(name)[:, 0:n * P].rearrange("p (r n) -> p r n", r=2)
                    dve.tensor_tensor(dst, y, dst, ALU.mult).then_inc(drained(name), 1)

        start()
        modulation()
        sine_argument(0)
        modulated(0, [(0, k) for k in range(KD)] + [(1, k) for k in range(KD)])
        for tap in taps:
            for c in (0, LAT + 1, LAT + 2, LAT + 3 + CTX):
                ins = dve.memset(tap[:, c:c + 1], 0.0)
                if c in (0, LAT + 3 + CTX):
                    ins.then_inc(edges_zeroed, 1)
        for ch in range(24):
            if ch == 2:
                sine_argument(1)
            if ch == 4:
                sine_argument(2)
                dve.wait_ge(sin_done, 3)
                dve.wait_ge(keep_in, 32)
                dve.tensor_scalar(hf_diff, hf_sum, sgn, None, ALU.mult).then_inc(hf_done, 1)
            short_conv(ch)
        filled(dve, ("proj", 1, 23))
        windowed(0)
        for i in range(len(STEPS)):
            multiply(i)
            if i < last_step:
                windowed(i + 1)
            gated(i)

        def deviation_of(n, h):
            for half in (0, 1):
                ins = dve.bn_stats(stats[:, half, :], h[:, COL * half:COL * half + COL])
            link(ins)
            if n > 1:
                dve.wait_ge(dev_done, n - 1)
            dve.bn_aggr(mean_var, stats).then_inc(var_ready, 1)

        def centred(n, h):
            dve.wait_ge(dev_done, n)
            link(dve.reciprocal(rdev, dev))
            dve.wait_ge(var_ready, n)
            return dve.tensor_scalar(h, h, mean_var[:, 0:1], rdev, ALU.subtract, ALU.mult)

        def expert_inputs(l, c):
            r = "l" if c < CL else "c"
            g = gchunk(l, c)
            deviation_of(g + 1 + 6 * l, h_rows[:, c, :])
            link(centred(g + 1 + 6 * l, h_rows[:, c, :]))
            if c >= 2:
                dve.wait_ge(tok_stored, 16 * (g - 1))
                filled(dve, ("a2T", l, c - 2, 1))
            dve.tensor_tensor(a2[c % 2], h_rows[:, c, :], bcast[l]["sc2" + r], ALU.mult).then_inc(normed, 1)
            dve.wait_ge(normed, g + 1 + 6 * l)
            dve.tensor_tensor(a2[c % 2], a2[c % 2], bcast[l]["sh2" + r], ALU.add).then_inc(a2_done, 1)

        def residual(l, c):
            b = bcast[l]
            r = "l" if c < CL else "c"
            g = gchunk(l, c)
            if c == 0:
                dve.wait_ge(bc_in, 16 * (len(BC[0]) + (len(BC[1]) if l else 0)))
                for i, m in enumerate(("l", "c")[:2 - l]):
                    sc, sh = b["sc2" + m], b["sh2" + m]
                    dve.scalar_tensor_tensor(a2[i], sc, 1.0, b["lnb"], ALU.add, ALU.mult)
                    link(dve.scalar_tensor_tensor(sc, sc, 1.0, b["lng"], ALU.add, ALU.mult))
                    link(dve.tensor_tensor(sh, sh, a2[i], ALU.add))
            dve.wait_ge(res_in, 16 * (g + 1))
            for half in (0, 1):
                cols = slice(COL * half, COL * half + COL)
                name = ("out", l, c, half)
                filled(dve, name)
                if l == 0:
                    dve.tensor_tensor(tmp[half], res(name)[:, :], b["bout"][:, cols],
                                      ALU.add).then_inc(drained(name), 1)
                    evacuated(dve, name)
                    link(dve.tensor_tensor(tmp[half], tmp[half], b["g1" + r][:, cols], ALU.mult))
                else:
                    dve.tensor_tensor(tmp[half], res(name)[:, :], b["g1" + r][:, cols],
                                      ALU.mult).then_inc(drained(name), 1)
                    evacuated(dve, name)
                ins = dve.scalar_tensor_tensor(h_rows[:, c, cols], resid[:, cols], ALPHA, tmp[half],
                                               ALU.mult, ALU.add)
                if half:
                    ins.then_inc(res_used, 1)
                else:
                    link(ins)
            dve.wait_ge(res_used, g + 1)

        def choose(l):
            n = len(CHUNKS_OF[l])
            w = n * E_N
            BIG = -1.0e30

            def t4(x):
                return x[:, 0:w].rearrange("p (c g e) -> p c g e", c=n, g=GRP)

            def t3(x):
                return x[:, 0:w].rearrange("p (c e) -> p c e", c=n)

            def g3(x, m=GRP):
                return x[:, 0:n * m].rearrange("p (c g) -> p c g", c=n)

            def over8(x):
                return g3(x).unsqueeze(3).broadcast_to([P, n, GRP, GSZ])

            S = scores
            biased, first, second, work, m1, m2, gs, chosen, pick, gm = temps[0:10]
            dve.wait_ge(h_ready, gchunk(l, CHUNKS_OF[l][-1]) + 1)
            evacuated(dve, ("logit", l, n - 1))
            link(dve.tensor_tensor(t3(biased), t3(S), router_b.unsqueeze(1).broadcast_to([P, n, E_N]), ALU.add))

            def first_max(src, m, hot):
                link(dve.tensor_reduce(g3(m), t4(src), AX.X, ALU.max))
                link(dve.tensor_tensor(t4(work), t4(src), over8(m), ALU.is_equal))
                link(dve.tensor_tensor(t4(work), t4(work), ramp8.unsqueeze(1).unsqueeze(1).broadcast_to(
                    [P, n, GRP, GSZ]), ALU.mult))
                link(dve.tensor_reduce(g3(pick), t4(work), AX.X, ALU.max))
                link(dve.tensor_tensor(t4(hot), t4(work), over8(pick), ALU.is_equal))

            first_max(biased, m1, first)
            link(dve.scalar_tensor_tensor(biased[:, 0:w], first[:, 0:w], BIG, biased[:, 0:w], ALU.mult, ALU.add))
            first_max(biased, m2, second)
            link(dve.tensor_tensor(g3(gs), g3(m1), g3(m2), ALU.add))
            link(dve.tensor_reduce(gm[:, 0:n], g3(gs), AX.X, ALU.max))
            link(dve.tensor_tensor(g3(gs), g3(gs), gm[:, 0:n].unsqueeze(2).broadcast_to([P, n, GRP]), ALU.is_equal))
            link(dve.tensor_tensor(g3(gs), g3(gs), ramp4.unsqueeze(1).broadcast_to([P, n, GRP]), ALU.mult))
            link(dve.tensor_reduce(gm[:, 0:n], g3(gs), AX.X, ALU.max))
            link(dve.tensor_tensor(g3(gs), g3(gs), gm[:, 0:n].unsqueeze(2).broadcast_to([P, n, GRP]), ALU.is_equal))
            link(dve.tensor_tensor(t4(first), t4(first), over8(gs), ALU.mult))
            link(dve.tensor_tensor(t4(second), t4(second), over8(gs), ALU.mult))
            dve.tensor_tensor(chosen[:, 0:w], first[:, 0:w], second[:, 0:w], ALU.add).then_inc(picked, 1)

            for k, hot in enumerate((first, second)):
                link(dve.tensor_tensor(work[:, 0:w], S[:, 0:w], hot[:, 0:w], ALU.mult))
                link(dve.tensor_reduce(pair_w[:, k, 0:n], t3(work), AX.X, ALU.add))
            link(dve.tensor_tensor(gm[:, 0:n], pair_w[:, 0, 0:n], pair_w[:, 1, 0:n], ALU.add))
            link(dve.reciprocal(gm[:, 0:n], gm[:, 0:n]))
            for k in (0, 1):
                link(dve.tensor_tensor(pair_w[:, k, 0:n], pair_w[:, k, 0:n], gm[:, 0:n], ALU.mult))

            rank, blocks, ends, place = temps[10:14]
            blocks_i = blocks[:, 64:64 + E_N].bitcast(I32)
            filled(dve, ("count", l))
            dve.tensor_scalar(blocks_i, res(("count", l))[:, 0:E_N], float(SB - 1), None,
                              ALU.add).then_inc(drained(("count", l)), 1)
            evacuated(dve, ("count", l))
            link(dve.tensor_scalar(blocks_i, blocks_i, 6, None, ALU.logical_shift_right))
            link(dve.tensor_scalar(blocks[:, 0:E_N], blocks_i, 1.0, None, ALU.max))
            link(dve.memset(ends[:, 0:1], 0.0))
            link(dve.tensor_tensor_scan(ends[:, 1:E_N + 1], ones[:, 0:E_N], blocks[:, 0:E_N], 0.0,
                                        ALU.mult, ALU.add))
            dve.tensor_copy(starts[:, 0:E_N + 1], ends[0:1, 0:E_N + 1]).then_inc(starts_done, 1)
            link(dve.tensor_scalar(place[:, 0:E_N], ends[:, 0:E_N], float(SB), None, ALU.mult))
            dve.tensor_tensor(t3(rank), res(("rank", l))[:, 0:w].rearrange("p (c e) -> p c e", c=n),
                              place[:, 0:E_N].unsqueeze(1).broadcast_to([P, n, E_N]),
                              ALU.add).then_inc(drained(("rank", l)), 1)
            evacuated(dve, ("rank", l))
            for k, hot in enumerate((first, second)):
                link(dve.tensor_tensor(work[:, 0:w], rank[:, 0:w], hot[:, 0:w], ALU.mult))
                link(dve.tensor_reduce(gm[:, 6:6 + n], t3(work), AX.X, ALU.add))
                dve.tensor_copy(dest[:, k, 0:n], gm[:, 6:6 + n]).then_inc(dest_done, 1)

            nb = blocks_max((NT, LAT)[l]) + 2
            filled(dve, ("slots", l))
            dve.tensor_copy(slot_tok[:, 0:nb], res(("slots", l))[0:SB, 0:nb]).then_inc(drained(("slots", l)), 1)
            dve.memset(keep[:, 1988 + 2 * l:1989 + 2 * l], 0.0).then_inc(y_copied[l], 1)
            dve.memset(keep[:, 1989 + 2 * l:1990 + 2 * l], 0.0).then_inc(y_stored[l], 32)

        def experts(l):
            pX, pG, pH = psum[0], psum[1:3], psum[3:5]
            dve.wait_ge(starts_done, l + 1)
            total = dve.value_load(starts[:, E_N:E_N + 1], min_val=1, max_val=blocks_max(NT))
            dve.wait_ge(x_turned[l], 1)
            dve.tensor_copy(xT, pX[:, :].rearrange("p (k n) -> p k n", k=KD)).then_inc(xT_done[l], 1)
            with dve.Fori(0, total) as b:
                for c in (0, 1):
                    dve.wait_ge(gate_done[l], 2 * b + c + 1)
                    dve.tensor_tensor(hid[c], pG[c][:, P:2 * P], gate_act[c], ALU.mult).then_inc(hid_done[l], 1)
                for c in (0, 1):
                    dve.wait_ge(hid_turned[l], 2 * b + c + 1)
                    dve.tensor_copy(hidT[c], pH[c][:, 0:P]).then_inc(hidT_done[l], 1)
                dve.wait_ge(x_turned[l], b + 2)
                dve.tensor_copy(xT, pX[:, :].rearrange("p (k n) -> p k n", k=KD)).then_inc(xT_done[l], 1)

        def mix_pair(l, c):
            dve.wait_ge(pair_in[c], 32 * (l + 1))
            dve.wait_ge(first_scaled, gchunk(l, c) + 1)
            dve.scalar_tensor_tensor(mix[c % 2], y_pair[c][1], pair_w[:, 1, c:c + 1], mix[c % 2], ALU.mult,
                                     ALU.add).then_inc(mixed_done, 1)

        def add_mix(l, c):
            h = h_rows[:, c, :]
            dve.wait_ge(scaled, gchunk(l, c) + 1)
            link(dve.scalar_tensor_tensor(h, h, ALPHA, mix[c % 2], ALU.mult, ALU.add))
            deviation_of(norm2(l, c), h)

        def last_vector(l, c):
            dve.wait_ge(lng_done, gchunk(l, c) + 1)
            dve.tensor_tensor(h_rows[:, c, :], h_rows[:, c, :], bc2["lnb"], ALU.add).then_inc(h_next, 1)

        def combine(l):
            chunks = CHUNKS_OF[l]
            mix_pair(l, 0)
            dve.wait_ge(bc2_in, 64 * (l + 1))
            for c in chunks:
                if c + 1 in chunks:
                    mix_pair(l, c + 1)
                add_mix(l, c)
                if c:
                    last_vector(l, c - 1)
                centred(norm2(l, c), h_rows[:, c, :]).then_inc(normed, 1)
            last_vector(l, chunks[-1])

        def finish(l):
            for c in CHUNKS_OF[l]:
                residual(l, c)
                expert_inputs(l, c)
            filled(dve, ("logit", l, CHUNKS_OF[l][-1]))
            dve.memset(slot_rows, 0.0).then_inc(slot_zero, 1)
            choose(l)
            experts(l)
            combine(l)

        finish(0)

        def gates(hd):
            cum = cums[hd % 2]
            for r in (0, 1):
                n_dir = 2 * hd + r
                for _, s, n, o in STREAMS:
                    name = ("g", hd, r, s)
                    dve.wait_ge(gates_abs, 2 * n_dir + s + 1)
                    dve.tensor_scalar(cum[:, r, o:o + n], res(name)[:, 0:n],
                                      smallT[:, 120 + 4 * r + hd:121 + 4 * r + hd], 0.0,
                                      ALU.add, ALU.min).then_inc(drained(name), 1)
                dve.wait_ge(gates_ln, n_dir + 1)
                for _, s, n, o in STREAMS:
                    evacuated(dve, ("g", hd, r, s))
                    m, l = cum[:, r, o:o + n], soft[:, o:o + n]
                    if r:
                        m, l = backwards(m, n), backwards(l, n)
                    dve.tensor_tensor_scan(m, m, l, 0.0, ALU.add, ALU.subtract).then_inc(cum_done, 1)

        def backwards(x, n):
            return x[:, n - 1::-1]

        def arguments(i):
            hd, lv = ITEMS[i]
            if lv in (0, LV_STATE):
                return
            cum = cums[hd % 2]
            dve.wait_ge(cum_done, 4 * (hd + 1))
            buffer_free(dve, i)
            buf = lev[i % 3]
            if lv == LV_CTX:
                for r, edge in ((0, NT - 1), (1, LAT)):
                    ins = dve.tensor_scalar(buf[:, CTX * r:CTX * r + CTX], cum[:, r, LAT:NT], -1.0,
                                            cum[:, r, edge:edge + 1], ALU.mult, ALU.add)
                ins.then_inc(args_done, 1)
                return
            h = 1 << (lv - 1)
            f = cum[:, 0, 0:LAT].rearrange("p (b m h) -> p b m h", m=2, h=h)
            g = cum[:, 1, 0:LAT].rearrange("p (b m h) -> p b m h", m=2, h=h)
            q = buf[:, 0:LAT].rearrange("p (b m h) -> p b m h", m=2, h=h)
            k = buf[:, LAT:2 * LAT].rearrange("p (b m h) -> p b m h", m=2, h=h)
            shape = [P, LAT // (2 * h), h]
            mid_f = f[:, :, 0, h - 1:h].broadcast_to(shape)
            mid_g = g[:, :, 1, 0:1].broadcast_to(shape)
            dve.tensor_tensor(q[:, :, 1, :], f[:, :, 1, :], mid_f, ALU.subtract)
            dve.tensor_tensor(q[:, :, 0, :], g[:, :, 0, :], mid_g, ALU.subtract)
            dve.tensor_tensor(k[:, :, 0, :], mid_f, f[:, :, 0, :], ALU.subtract)
            dve.tensor_tensor(k[:, :, 1, :], mid_g, g[:, :, 1, :], ALU.subtract).then_inc(args_done, 1)

        def masked(i):
            hd, lv = ITEMS[i]
            if lv <= LEVELS:
                name = ("att", i, 0)
                filled(dve, name)
                pairs = res(name)[:, :].rearrange("p (b n) -> p b n", b=CL)
                if lv == 0:
                    if hd:
                        dve.wait_ge(near_done, LEVELS * hd)
                    dve.scalar_tensor_tensor(att_near.rearrange("p (b n) -> p b n", b=CL), pairs, 2.0,
                                             ident.unsqueeze(1).broadcast_to([P, CL, P]),
                                             ALU.mult, ALU.mult).then_inc(drained(name), 1)
                else:
                    n = LEVELS * hd + lv
                    if n > 1:
                        dve.wait_ge(near_done, n - 1)
                    dve.tensor_tensor(prod.rearrange("p (b n) -> p b n", b=CL), pairs,
                                      masks[:, lv - 1, :].unsqueeze(1).broadcast_to([P, CL, P]),
                                      ALU.mult).then_inc(drained(name), 1)
            elif lv == LEVELS + 1:
                name = ("att", i, 0)
                filled(dve, name)
                dve.tensor_copy(att_next, res(name)[:, :]).then_inc(drained(name), 1)
            elif lv == LV_STATE:
                for u in range(CL):
                    name = ("o", hd, u)
                    filled(dve, name)
                    if hd and u == 0:
                        dve.wait_ge(o_var, CL * hd)
                    dve.bn_stats(g_stats[:, u, :], res(name)[:, 0:DVH])
                    dve.tensor_copy(o_rows[:, u, DVH * hd:DVH * hd + DVH], res(name)[:, 0:DVH]).then_inc(
                        drained(name), 1)
                evacuated(dve, ("o", hd, CL - 1))
                if hd:
                    dve.wait_ge(o_normed, hd)
                for u in range(CL):
                    dve.bn_aggr(g_mv[:, u, :], g_stats[:, u, :]).then_inc(o_var, 1)

        def normalise_head(hd):
            dve.wait_ge(o_dev, hd + 1)
            link(dve.reciprocal(g_rdev, g_dev))
            dve.wait_ge(o_var, CL * (hd + 1))
            for u in range(CL):
                o = o_rows[:, u, DVH * hd:DVH * hd + DVH]
                ins = dve.tensor_scalar(o, o, g_mv[:, u, 0:1], g_rdev[:, u:u + 1], ALU.subtract, ALU.mult)
            ins.then_inc(o_normed, 1)

        dve.memset(gate_w[0], 0.0).then_inc(zero_w, 1)
        modulated(1, [(s, k) for s in (0, 1) for k in range(KD)])
        dve.memset(gate_w[1], 0.0).then_inc(zero_w, 1)
        filled(dve, ("qk", 1, HEADS - 1, 1))
        gates(0)
        arguments(1)
        for i, (hd, lv) in enumerate(ITEMS):
            if i and i + 1 < len(ITEMS):
                arguments(i + 1)
            masked(i)
            if lv == 5 and hd + 1 < HEADS:
                gates(hd + 1)
            if lv == 4 and hd:
                normalise_head(hd - 1)
        normalise_head(HEADS - 1)
        for c in (0, 2):
            dve.wait_ge(silu_done, c + 1)
            dve.wait_ge(o_gained, HEADS)
            dve.tensor_tensor(r_rows[:, c, :], r_rows[:, c, :], o_rows[:, c, :], ALU.mult).then_inc(y_rows_done, 1)
        for k in range(1, KD, 2):
            filled(dve, ("yT", k))
            dve.tensor_copy(mixed[1][:, k, :], res(("yT", k))[:, :]).then_inc(drained(("yT", k)), 1)
        finish(1)

    @block.gpsimd
    def _(pool):
        def positions():
            pool.wait_ge(x_in, 16)
            pool.wait_ge(pe_in, 16)
            pool.tensor_tensor(x_rows[:, 0:CL, :], x_rows[:, 0:CL, :], pe_rows, ALU.add).then_inc(pe_added, 1)

        def complex_sums():
            for g, (i, f) in enumerate(CHUNKS):
                for j in (1, 2, 3):
                    evacuated(pool, ("x", j, i, f))
                    for a in (0, 1):
                        if j > 1:
                            pool.wait_ge(z_ready, 6 * g + 2 * (j - 2) + a + 1)
                        op = ALU.subtract if j >= 2 and a == 0 else ALU.add
                        pool.tensor_tensor(z[a][:, :, f, :], z[a][:, :, f, :], terms[j][:, a, :, :],
                                           op).then_inc(z_ready, 1)

        positions()
        complex_sums()

        def linker():
            n = [0]

            def link(ins):
                ins.then_inc(pool_link, 1)
                n[0] += 1
                pool.wait_ge(pool_link, n[0])
            return link

        link = linker()

        def affine(l, c):
            b = bcast[l]
            g = gchunk(l, c)
            h = h_rows[:, c, :]
            pool.wait_ge(normed, g + 1 + 6 * l)
            link(pool.tensor_tensor(h, h, b["lng"], ALU.mult))
            pool.tensor_tensor(h, h, b["lnb"], ALU.add).then_inc(h_ready, 1)

        def scatter(l):
            chunks = CHUNKS_OF[l]
            pool.wait_ge(slot_cleared, 16 * (l + 1))
            for k in (0, 1):
                pool.wait_ge(dest_done, 2 * l + k + 1)
                for c in chunks:
                    pool.indirect_dma_start(
                        out=slot_l[l], out_offset=bass.IndirectOffsetOnAxis(ap=dest[:, k, c:c + 1], axis=0),
                        in_=token_id[:, c:c + 1], in_offset=None).then_inc(scattered, 16)

        def experts(l):
            def gather():
                pool.indirect_dma_start(
                    out=x_land, out_offset=None, in_=tok_l[l],
                    in_offset=bass.IndirectOffsetOnAxis(ap=cur_tok, axis=0)).then_inc(x_landed[l], 16)

            evacuated(pool, ("slots", l))
            pool.wait_ge(y_filled_up, 16)
            pool.wait_ge(tok_stored, 16 * (gchunk(l, CHUNKS_OF[l][-1]) + 1))
            pool.wait_ge(starts_done, l + 1)
            total = pool.value_load(starts[:, E_N:E_N + 1], min_val=1, max_val=blocks_max(NT))
            pool.tensor_copy(cur_tok, slot_tok[:, 0:1]).then_inc(x_copied[l], 1)
            pool.wait_ge(x_copied[l], 1)
            gather()
            pool.wait_ge(x_landed[l], 16)
            pool.tensor_copy(cur_tok, slot_tok[:, 1:2]).then_inc(x_copied[l], 1)
            pool.tensor_copy(x_slots, x_land).then_inc(x_moved[l], 1)
            pool.wait_ge(x_copied[l], 2)
            pool.wait_ge(x_moved[l], 1)
            gather()
            with pool.Fori(0, total) as b:
                pool.wait_ge(x_landed[l], 16 * b + 32)
                pool.tensor_copy(cur_tok, slot_tok[:, ds(b + 2, 1)]).then_inc(x_copied[l], 1)
                pool.wait_ge(x_turned[l], b + 1)
                pool.sem_inc(gather_go[l], 1)
                pool.tensor_copy(x_slots, x_land).then_inc(x_moved[l], 1)
                pool.wait_ge(x_copied[l], b + 3)
                pool.wait_ge(x_moved[l], b + 2)
                pool.sem_inc(gather_go[l], 1)
                gather()
            pool.wait_ge(y_stored[l], 32 * total + 32)
            pool.wait_ge(x_landed[l], 16 * total + 32)
            pool.wait_ge(gather_go[l], 2 * total)
            pool.wait_ge(xT_done[l], total + 1)
            pool.tensor_tensor(keep[:, 1992:1993], eps, eps, ALU.add).then_inc(combine_go, 1)
            pool.wait_ge(combine_go, l + 1)

        def combine(l):
            chunks = CHUNKS_OF[l]
            for c in chunks:
                for k in (0, 1):
                    pool.indirect_dma_start(
                        out=y_pair[c][k], out_offset=None, in_=y_d,
                        in_offset=bass.IndirectOffsetOnAxis(ap=dest[:, k, c:c + 1], axis=0)
                    ).then_inc(pair_in[c], 16)
            pool.wait_ge(bc2_in, 64 * (l + 1))
            gate_mix(l, 0)
            for c in chunks:
                if c + 1 in chunks:
                    gate_mix(l, c + 1)
                pool.wait_ge(normed, norm2(l, c))
                pool.tensor_tensor(h_rows[:, c, :], h_rows[:, c, :], bc2["lng"], ALU.mult).then_inc(lng_done, 1)

        def gate_mix(l, c):
            pool.wait_ge(mixed_done, gchunk(l, c) + 1)
            pool.tensor_tensor(mix[c % 2], mix[c % 2], bc2["g2" + ("l" if c < CL else "c")],
                               ALU.mult).then_inc(scaled, 1)

        def finish(l):
            for c in CHUNKS_OF[l]:
                affine(l, c)
            scatter(l)
            experts(l)
            combine(l)

        finish(0)

        def scale_qk(i):
            hd, lv = ITEMS[i]
            if lv == 0:
                return
            pool.wait_ge(exps_done, scaled_items(i))
            buf = lev[i % 3]
            if lv == LV_CTX:
                x = buf[:, 0:2 * CTX].rearrange("p (r n) -> p r n", r=2)
                y = k_ctx[:, hd, :].unsqueeze(1).broadcast_to([P, 2, CTX])
                evacuated(pool, ("qk", 1, hd, 1))
            elif lv == LV_STATE:
                x = buf.rearrange("p (r n) -> p r n", r=2)
                y = qk[:, hd, 0, :].unsqueeze(1).broadcast_to([P, 2, LAT])
            else:
                x = buf.rearrange("p (r n) -> p r n", r=2)
                y = qk[:, hd, :, :]
                evacuated(pool, ("qk", 0, hd, 0))
                evacuated(pool, ("qk", 1, hd, 0))
            pool.tensor_tensor(x, x, y, ALU.mult).then_inc(scaled_qk, 1)

        def add_near(i):
            hd, lv = ITEMS[i]
            if 1 <= lv <= LEVELS:
                evacuated(pool, ("att", i, 0))
                if lv == 1:
                    evacuated(pool, ("att", i - 1, 0))
                else:
                    pool.wait_ge(near_done, LEVELS * hd + lv - 1)
                pool.tensor_tensor(att_near, att_near, prod, ALU.add).then_inc(near_done, 1)

        def gain(hd):
            pool.wait_ge(o_normed, hd + 1)
            if hd == 0:
                pool.wait_ge(norm_in, 16)
            cols = slice(DVH * hd, DVH * hd + DVH)
            pool.tensor_tensor(o_rows[:, :, cols], o_rows[:, :, cols],
                               norm_g[:, cols].unsqueeze(1).broadcast_to([P, CL, DVH]),
                               ALU.mult).then_inc(o_gained, 1)

        scale_qk(1)
        for i, (hd, lv) in enumerate(ITEMS):
            if i and i + 1 < len(ITEMS):
                scale_qk(i + 1)
            add_near(i)
        for hd in range(HEADS):
            gain(hd)
        for c in (1, 3):
            pool.wait_ge(silu_done, c + 1)
            pool.wait_ge(o_gained, HEADS)
            pool.tensor_tensor(r_rows[:, c, :], r_rows[:, c, :], o_rows[:, c, :], ALU.mult).then_inc(y_rows_done, 1)
        finish(1)

    @block.sync
    def _(sp):
        def modulation():
            w = t["w_mod"].rearrange("l (k p) (h u c) -> l h u p k c", p=P, u=SLOTS, c=COL)
            for u in range(SLOTS):
                sp.dma_start(slot(u).rearrange("p (k c) -> p k c", k=KD), w[0, 0, u]).then_inc(landed[u], 16)
            for n in range(1, N_MOD // SLOTS):
                for u in range(SLOTS):
                    sp.wait_ge(mod_filled, SLOTS * (n - 1) + u + 1)
                    sp.dma_start(slot(u).rearrange("p (k c) -> p k c", k=KD),
                                 w[n // 2, n % 2, u]).then_inc(landed[u], 16)

        def hyena():
            w = t["hy_w_in"][0].rearrange("(k p) (j c) -> j p k c", p=P, c=COL)
            for j in range(6):
                sp.wait_ge(mod_filled, N_MOD - SLOTS + j + 1)
                s, _ = units.of[("hy_in", j)]
                sp.dma_start(slot(s).rearrange("p (k c) -> p k c", k=KD), w[j]).then_inc(landed[s], 16)
            filled(sp, ("proj", 1, 3))
            w4_d = t["hy_f_w4"][0].rearrange("f (o r c) -> r f o c", o=2, r=2)
            for r in (0, 1):
                sp.dma_start(w4[HF * r:HF * r + HF], w4_d[r]).then_inc(filt_in, 16)
            sp.dma_start(filt_u[:, 2 * D:3 * D], t["dft_small"]).then_inc(filt_in, 16)
            s, _ = units.of[("dft", 0)]
            filled(sp, ("proj", 1, 7))
            sp.dma_start(dft, t["dft"].rearrange("a r (c p) n -> p a r c n", p=P)).then_inc(landed[s], 16)
            s, _ = units.of[("idft", 0)]
            filled(sp, ("proj", 1, 11))
            sp.dma_start(idft, t["idft"].rearrange("a r (c p) n -> p a r c n", p=P)).then_inc(landed[s], 16)
            w = t["hy_w_out"][0].rearrange("(k p) (j c) -> j p k c", p=P, c=COL)
            for j in range(2):
                s, _ = units.of[("hy_out", j)]
                filled(sp, ("proj", 1, 4 * (3 + j) + 3))
                if j:
                    made(sp, len(CHUNKS))
                    sp.wait_ge(z_ready, 6 * len(CHUNKS))
                sp.dma_start(slot(s).rearrange("p (k c) -> p k c", k=KD), w[j]).then_inc(landed[s], 16)

        modulation()
        hyena()

        def experts(l):
            w1 = t["moe_w1"][l].rearrange("e (k p) c -> e p k c", p=P)
            w3 = t["moe_w3"][l].rearrange("e (k p) c -> e p k c", p=P)
            w2 = t["moe_w2"][l].rearrange("e (k p) c -> e p k c", p=P)

            for e in (0, 1):
                for q in range(3):
                    free_for_experts(l, 3 * e + q)
                    w = (w1, w3, w2)[q]
                    sp.dma_start(slot(3 * e + q).rearrange("p (k c) -> p k c", k=(8, 8, 4)[q]),
                                 w[e]).then_inc(landed[3 * e + q], 16)
            sp.wait_ge(starts_done, l + 1)
            with sp.Fori(1, E_N // 2) as pair:
                for par in (0, 1):
                    done = sp.value_load(starts[:, ds(2 * pair + par - 1, 1)], min_val=1, max_val=blocks_max(NT))
                    for q, w in enumerate((w1, w3, w2)):
                        if q == 0:
                            sp.wait_ge(up_filled[l], 2 * done)
                        if q == 2:
                            sp.wait_ge(y_filled[l], done)
                        sp.dma_start(slot(3 * par + q).rearrange("p (k c) -> p k c", k=(8, 8, 4)[q]),
                                     w[ds(2 * pair + par, 1)].rearrange("o p k c -> (o p) k c")
                                     ).then_inc(landed[3 * par + q], 16)

        def fill_outputs():
            rest = blocks_max(NT) - E_N
            src = t["zeros"].rearrange("s d -> () (s d)").broadcast_to([rest, SB * D])
            sp.dma_start(y_d[E_N * SB:].rearrange("(b s) d -> b (s d)", s=SB), src).then_inc(y_filled_up, 16)

        def free_for_experts(l, s):
            if l == 0:
                if s in (3, 4):
                    filled(sp, ("out", 0, 5, s - 3))
                else:
                    filled(sp, ("y", last_step, 3))
                    made(sp, len(CHUNKS))
                    sp.wait_ge(z_ready, 6 * len(CHUNKS))
                    sp.wait_ge(skip_added, len(STEPS))
            elif s < 4:
                filled(sp, ("o", HEADS - 1, CL - 1))
                if s == 2:
                    sp.wait_ge(y_rows_done, CL)
            else:
                filled(sp, ("out", 1, CL - 1, s - 4))

        fill_outputs()
        experts(0)

        def gla_weights():
            w = t["gla_w_in"][0, :, 0:3072].rearrange("(k p) (j c) -> j p k c", p=P, c=COL)
            wo = t["gla_w_out"][0].rearrange("(k p) (j c) -> j p k c", p=P, c=COL)
            sp.wait_ge(combine_go, 1)
            for j in range(6):
                s, _ = units.of[("gla_in", j)]
                sp.dma_start(slot(s).rearrange("p (k c) -> p k c", k=KD), w[j]).then_inc(landed[s], 16)
            for j in range(2):
                s, _ = units.of[("gla_out", j)]
                filled(sp, ("r", j, CL - 1))
                sp.dma_start(slot(s).rearrange("p (k c) -> p k c", k=KD), wo[j]).then_inc(landed[s], 16)

        gla_weights()
        experts(1)
        sp.wait_ge(out_stored, 16 * CL)

    ctx.close()


def constants():
    f8 = np.float64
    f4 = np.float32
    q = D // 4
    omega = 1.0 / (10000.0 ** (np.arange(q, dtype=f8) / q))
    pr = np.arange(LAT // 64, dtype=f8)[:, None] * omega
    pc = np.arange(64, dtype=f8)[:, None] * omega
    er = np.concatenate([np.sin(pr), np.cos(pr)], -1)
    ec = np.concatenate([np.sin(pc), np.cos(pc)], -1)
    pos = np.concatenate([np.broadcast_to(er[:, None, :], (LAT // 64, 64, 2 * q)),
                          np.broadcast_to(ec[None, :, :], (LAT // 64, 64, 2 * q))], -1).reshape(LAT, D)

    def features(n):
        x = np.linspace(0.0, 1.0, n)[:, None]
        w = 2.0 * np.pi * np.arange(n)[:, None] / n
        bands = np.linspace(1e-4, 15, 16)[None, :]
        return np.concatenate([x, np.cos(bands * w), -np.sin(bands * w)], -1)

    def window(n):
        deltas = np.abs(np.linspace(np.log(1e-2) / 1.5, np.log(1e-2) / 0.3, D))
        return np.exp(-np.linspace(0.0, 1.0, n)[:, None] * deltas)

    def by_parity(x):
        return np.concatenate([x[0::2], x[1::2]], 0)

    def transforms(n):
        fwd, inv = np.zeros((2, 2, n // 2, n // 2)), np.zeros((2, 2, n // 2, n // 2))
        for r in (0, 1):
            tok = np.arange(r, n, 2)
            ang = np.pi * np.outer(tok, np.arange(n // 2)) / n
            mid = -np.sin(np.pi * tok / 2) if r else np.cos(np.pi * tok / 2)
            fwd[0, r], fwd[1, r] = np.cos(ang), -np.sin(ang)
            fwd[1, r, :, 0] = mid
            inv[:, r] = fwd[:, r].transpose(0, 2, 1) * 2.0 / n
            inv[:, r, 0] /= 2.0
        return fwd, inv

    fwd, inv = transforms(LAT)
    small = np.stack(transforms(CTX))
    small = small.transpose(3, 0, 1, 2, 4).reshape(P, -1)
    marks = np.ones((P, 3))
    marks[HF:, 0] = -1.0
    marks[0, 1] = 0.0
    marks[:, 2] = EPS
    i = np.arange(P)
    masks = np.zeros((P, LEVELS, P))
    for l in range(LEVELS):
        same = i[:, None] // (2 << l) == i[None] // (2 << l)
        masks[:, l] = same & (i[:, None] // (1 << l) != i[None] // (1 << l))
    token = i[:, None] + P * np.arange(NT // P)[None]
    ramps = np.concatenate([np.arange(8, 0, -1), np.arange(4, 0, -1)])
    route = np.concatenate([(i[:, None] < i[None]), np.ones((P, P)), token,
                            np.broadcast_to(ramps, (P, 12))], 1)
    out = dict(ident=np.eye(P), marks=marks, pos=pos, dft=fwd, idft=inv, dft_small=small,
               window_lat=by_parity(window(LAT)), window_ctx=by_parity(window(CTX)),
               zT=np.concatenate([by_parity(features(LAT)), by_parity(features(CTX))], 0).T,
               masks=masks.reshape(P, -1), route_c=route, zeros=np.zeros((SB, D)))
    return {k: np.ascontiguousarray(v, dtype=f4) for k, v in out.items()}


_INS = ["x", "c", "ctx", "c_ctx", "w_mod", "b_mod", "ln_g", "ln_b", "hy_w_in", "hy_b_in", "hy_conv_w",
        "hy_conv_b", "hy_f_w1", "hy_f_b1", "hy_f_w2", "hy_f_b2", "hy_f_w3", "hy_f_b3", "hy_f_w4",
        "hy_skip", "hy_w_out", "hy_b_out", "gla_w_in", "gla_w_gate", "gla_b_gate", "gla_norm_g",
        "gla_w_out", "router_w", "router_b", "moe_w1", "moe_w3", "moe_w2"]


def kernel(**inputs):
    import numpy as _np
    import concourse.bacc as _bacc
    from concourse import mybir as _mybir
    from concourse.bass_utils import run_bass_kernel_spmd as _run

    nc = _bacc.Bacc("TRN2", target_bir_lowering=False, num_devices=1)
    arrays, tensors = {}, {}
    data = {n: _np.ascontiguousarray(inputs[n]) for n in _INS}
    for name, a in {**data, **constants()}.items():
        arrays[f"in_{name}"] = a
        tensors[name] = nc.dram_tensor(f"in_{name}", a.shape, _mybir.dt.from_np(a.dtype),
                                       kind="ExternalInput").ap()
    out = nc.dram_tensor("out_h", (1, LAT, D), F32, kind="ExternalOutput").ap()
    build(nc, tensors, out)
    r = _run(nc, [arrays], core_ids=[0])
    return r.results[0]["out_h"]
```

```python
from contextlib import ExitStack

import numpy as np
import concourse.bass as bass
import concourse.mybir as mybir

F32 = mybir.dt.float32
I32 = mybir.dt.int32
U32 = mybir.dt.uint32
ALU = mybir.AluOpType
ACT = mybir.ActivationFunctionType
AX = mybir.AxisListType
ds = bass.ds

P = 128
D = 1024
KD = D // P
LAT, CTX = 512, 256
NT = LAT + CTX
CL, CC = LAT // P, CTX // P
COL = 512
UNIT = KD * COL
SLOTS = 6
E_N, GRP, GSZ = 32, 4, 8
RING_EXPERTS = sum(e % 3 < 2 for e in range(E_N))
SB = 64
ALPHA = (2.0 * 2) ** 0.25
EPS = 1e-5
HF = 64
HEADS, DKH, DVH = 4, 128, 256
N_MOD = 24
TAU = 16.0
LEVELS = 7

MAGIC = 12582912.0
PI2_HI = 6.28125
PI2_LO = 2.0 * np.pi - 6.28125


def blocks_max(tokens):
    return 2 * tokens // SB + E_N


class PsumPlan:

    def __init__(self):
        self.total = 0
        self.used = [0] * 8
        self.of = {}

    def add(self, name, bank=None):
        bank = self.total % 8 if bank is None else bank
        self.total += 1
        self.of[name] = (bank, self.total, self.used[bank])
        self.used[bank] += 1
        return self.of[name]


class Ring:

    def __init__(self):
        self.at = 0
        self.loads = [0] * SLOTS
        self.of = {}

    def add(self, name, loads=1):
        slot = self.at % SLOTS
        self.of[name] = (slot, self.loads[slot])
        self.loads[slot] += loads
        self.at += 1

    def skip(self, n):
        self.at += n


def build(nc, t, out):
    ctx = ExitStack()

    def sem(name):
        return ctx.enter_context(nc.semaphore(name))

    def scratch(name, shape, dt=F32):
        return nc.dram_tensor(name, shape, dt, kind="Internal").ap()

    ring = ctx.enter_context(nc.sbuf_tensor("ring", [P, SLOTS * UNIT], F32))
    arena = ctx.enter_context(nc.sbuf_tensor("arena", [P, 26624], F32))
    keep = ctx.enter_context(nc.sbuf_tensor("keep", [P, 2000], F32))
    psum = [ctx.enter_context(nc.psum_tensor(f"bank{i}", [P, 512], F32)) for i in range(8)]

    KB = 256

    def at(kb, n, lo=0, hi=P):
        o = int(kb * KB)
        return arena[lo:hi, o:o + n]

    def slot(s, lo=0, n=UNIT):
        return ring[:, s * UNIT + lo:s * UNIT + lo + n]

    mod_d = scratch("mod_d", [2, N_MOD, 4, P])
    h0_d = scratch("h0_d", [LAT, D])

    ident = keep[:, 0:128]
    hf_sum = keep[:, 128:128 + NT]
    hf_diff = keep[:, 896:896 + NT]
    modT = keep[:, 1664:1856].rearrange("p (l r v k) -> p l r v k", l=2, r=2, v=6)
    smallT = keep[:, 1856:1984]
    sgn, rowmask, eps = keep[:, 1984:1985], keep[:, 1985:1986], keep[:, 1986:1987]

    def conv_w(j, ch):
        return smallT[:, 24 * j + ch:24 * j + ch + 1]

    def b_in(ch):
        return smallT[:, 72 + ch:73 + ch]

    def conv_b(ch):
        return smallT[:, 96 + ch:97 + ch]

    aT = at(0, KD * NT).rearrange("p (k n) -> p k n", k=KD)
    aT1 = at(24, KD * NT).rearrange("p (k n) -> p k n", k=KD)
    x_rows = at(24, 6 * D).rearrange("p (c d) -> p c d", c=6)
    pos_rows = at(48, CL * COL).rearrange("p (c d) -> p c d", c=CL)
    pos_cols = at(56, COL)
    mod_acc = at(72, N_MOD * P).rearrange("p (n c) -> p n c", n=N_MOD)
    cond_rows = at(84, P, 0, 16)
    s_cols = at(84.5, KD * 32).rearrange("p (k c) -> p k c", k=KD)
    small_rows = at(86, P)
    mod_rows = at(87, 2 * P, 0, 96).rearrange("p (l c) -> p l c", l=2)
    hf1, hf2 = at(88, NT, 0, HF), at(91, NT, 0, HF)
    arg_u, arg_t = at(64, NT), at(67, NT)
    zT = at(96, NT, 0, 33)
    taps = [at(96, 772), arena[:, 96 * KB + 772:96 * KB + 1544]]
    fw = arena[:, 26120:26120 + 256]
    f_w1, f_w2, f_w3 = fw[0:33, 0:HF], fw[0:HF, HF:2 * HF], fw[0:HF, 2 * HF:4 * HF]
    f_b = arena[:, 26376:26380]
    zc = [at(72, NT), at(75, NT)]
    v_t = at(24, 6 * D).rearrange("p (c d) -> p c d", c=6)
    x1_t = at(48, 6 * D).rearrange("p (c d) -> p c d", c=6)
    x2T = at(72, KD * NT).rearrange("p (k n) -> p k n", k=KD)
    filt = [at(8 * i, 4 * COL).rearrange("p (c d) -> p c d", c=4) for i in (0, 1)]
    z = [at(kb, 4 * COL).rearrange("p (r f d) -> p r f d", r=2, f=2) for kb in (16, 96)]

    units = Ring()
    for u in range(N_MOD):
        units.add(("mod", u))
    for j in range(6):
        units.add(("hy_in", j))
    units.add(("filt", 0), 0)
    units.add(("dft", 0))
    units.add(("idft", 0))
    units.add(("hy_out", 0))
    units.add(("hy_out", 1))
    units.skip(1)
    moe_first = {}
    moe_first[0] = list(units.loads)
    assert units.at % SLOTS == 0
    for u in range(3 * RING_EXPERTS):
        units.add(("moe0", u))
    for j in range(6):
        units.add(("gla_in", j))
    units.skip(4)
    for j in range(2):
        units.add(("gla_out", j))
    moe_first[1] = list(units.loads)

    HALF = UNIT // 2
    k_parts = [slot(5, HALF * i, HALF).rearrange("p (j d) -> p j d", j=4) for i in (0, 1)]
    win = [slot(0, 6 * COL + COL * i, COL) for i in (0, 1)]
    k_alt = slot(1, HALF, 3 * COL).rearrange("p (j d) -> p j d", j=3)
    skip_row = ring[0:1, 1 * UNIT + HALF + 3 * COL:1 * UNIT + HALF + 4 * COL]
    terms = [None] + [x.rearrange("p (a r d) -> p a r d", a=2, r=2)
                      for x in (slot(2, HALF, HALF), slot(4, 0, HALF), slot(4, HALF, HALF))]

    landed = [sem(f"landed{i}") for i in range(SLOTS)]
    psum_filled = sem("psum_filled")
    psum_drained = [sem(f"psum_drained{i}") for i in range(8)]
    keep_in, cond_in, small_in, x_in, pe_in, ctx_in, fw_in = (
        sem(n) for n in ("keep_in", "cond_in", "small_in", "x_in", "pe_in", "ctx_in", "fw_in"))
    bias_in, filt_in = sem("bias_in"), sem("filt_in")
    mod_zeroed, cols_zeroed, cond_silu = sem("mod_zeroed"), sem("cols_zeroed"), sem("cond_silu")
    mod_filled, mod_drained, mod_stored = sem("mod_filled"), sem("mod_drained"), sem("mod_stored")
    mod_back, modT_done, a_done = sem("mod_back"), sem("modT_done"), sem("a_done")
    pe_added, h0_stored = sem("pe_added"), sem("h0_stored")
    act_link, dve_link, pool_link = sem("act_link"), sem("dve_link"), sem("pool_link")
    sin_arg, sin_done, hf_done = sem("sin_arg"), sem("sin_done"), sem("hf_done")
    edges_zeroed, conv_done = sem("edges_zeroed"), sem("conv_done")
    win_in = [sem("win_in0"), sem("win_in1")]
    skip_in, skip_added = sem("skip_in"), sem("skip_added")
    z_ready, merged = sem("z_ready"), sem("merged")

    router_w = keep[:, 128:384].rearrange("p (k e) -> p k e", k=KD)
    router_b = keep[:, 384:416]
    before, ones = keep[:, 416:544], keep[:, 544:672]
    token_id, ramp8, ramp4 = keep[:, 672:678], keep[:, 678:686], keep[:, 686:690]
    scores = keep[:, 690:882]
    pair_w = keep[:, 882:894].rearrange("p (k c) -> p k c", k=2)
    dest = keep[:, 894:906].bitcast(U32).rearrange("p (k c) -> p k c", k=2)
    starts = keep[0:1, 906:940].bitcast(I32)
    slot_tok = keep[0:SB, 940:998].bitcast(U32)
    cur_tok = keep[0:SB, 998:999].bitcast(U32)
    stats = keep[:, 1000:1012].rearrange("p (h s) -> p h s", h=2)
    mean_var, dev, rdev = keep[:, 1012:1014], keep[:, 1014:1015], keep[:, 1015:1016]
    h_rows = at(0, 6 * D).rearrange("p (c d) -> p c d", c=6)
    temps = [at(72 + 0.75 * i, 192) for i in range(16)]
    ramp64 = keep[:, 1568:1568 + SB]
    chosen_before = at(84, 7 * E_N)
    hot_slot = at(85, 12 * SB).rearrange("p (j s) -> p j s", j=12)
    hot_block = at(88, 12 * SB).rearrange("p (j b) -> p j b", j=12)

    tok_l = [scratch(f"tok{l}", [(NT, LAT)[l], D]) for l in (0, 1)]
    y_d = scratch("y", [blocks_max(NT) * SB, D])

    CHUNKS_OF = [list(range(6)), list(range(CL))]
    mixed = [x2T, at(24, KD * LAT).rearrange("p (k n) -> p k n", k=KD)]
    BC = [["bout", "g1l", "g1c", "lng", "lnb", "sc2l", "sc2c", "sh2l", "sh2c"],
          ["g1l", "lng", "lnb", "sc2l", "sh2l"]]
    bc0 = [24, 72]
    bcast = [{n: at(bc0[l] + 4 * i, D) for i, n in enumerate(BC[l])} for l in (0, 1)]
    a2 = [at(60, D), at(64, D)]
    a2T = at(68, D).rearrange("p (k n) -> p k n", k=KD)
    tmp = [at(100, COL), at(102, COL)]

    x_land, x_slots = at(52, D, 0, SB), at(24, D, 0, SB)
    xT = at(28, KD * SB).rearrange("p (k n) -> p k n", k=KD)
    gate_act = [at(30, P), at(30.5, P)]
    hid = [at(31, P), at(31.5, P)]
    hidT = [at(32, P), at(32.5, P)]
    y_out = at(33, COL)
    expert_units = [[slot(3 * buf + q) for q in range(3)] for buf in (0, 1)] + [
        [at(kb, UNIT) for kb in (60, 76, 36)]]
    expert_w13 = [x.rearrange("p (m k c) -> p m k c", m=2, k=KD)
                  for x in (ring[:, 0:2 * UNIT], ring[:, 3 * UNIT:5 * UNIT], at(60, 2 * UNIT))]
    expert_w2 = [expert_units[buf][2].rearrange("p (f c) -> p f c", f=4) for buf in range(3)]
    expert_in = [landed[0:3], landed[3:6], [sem(f"third_in{q}") for q in range(3)]]
    y_pair = [[at(kb, D), at(kb + 4, D)] for kb in (36, 44, 76, 84, 92)] + [[at(100, D), slot(5, 0, D)]]
    mix = [at(52, D), at(56, D)]
    bc2 = {n: at(60 + 4 * i, D) for i, n in enumerate(["g2l", "g2c", "lng", "lnb"])}

    bc_in, res_in = sem("bc_in"), [sem(f"res_in{c}") for c in range(6)]
    var_ready, dev_done, normed, a2_done = sem("var_ready"), sem("dev_done"), sem("normed"), sem("a2_done")
    tok_stored = [sem("tok_stored0"), sem("tok_stored1")]
    route_in, h_ready = sem("route_in"), sem("h_ready")
    picked, starts_done, dest_done, hots_done = (
        sem("picked"), sem("starts_done"), sem("dest_done"), sem("hots_done"))
    L2 = (0, 1)
    x_copied = [sem(f"x_copied{l}") for l in L2]
    x_landed = [sem(f"x_landed{l}") for l in L2]
    x_moved = [sem(f"x_moved{l}") for l in L2]
    x_turned = [sem(f"x_turned{l}") for l in L2]
    paced = [sem(f"paced{l}") for l in L2]
    gather_go = [sem(f"gather_go{l}") for l in L2]
    xT_done = [sem(f"xT_done{l}") for l in L2]
    up_filled = [sem(f"up_filled{l}") for l in L2]
    gate_done = [sem(f"gate_done{l}") for l in L2]
    hid_done = [sem(f"hid_done{l}") for l in L2]
    hid_turned = [sem(f"hid_turned{l}") for l in L2]
    hidT_done = [sem(f"hidT_done{l}") for l in L2]
    y_filled = [sem(f"y_filled{l}") for l in L2]
    y_copied = [sem(f"y_copied{l}") for l in L2]
    y_stored = [sem(f"y_stored{l}") for l in L2]
    pair_in = [sem(f"pair_in{c}") for c in range(6)]
    bc2_in, first_scaled, mixed_done = sem("bc2_in"), sem("first_scaled"), sem("mixed_done")
    lng_done, h_next = sem("lng_done"), sem("h_next")
    y_filled_up, combine_go = sem("y_filled_up"), sem("combine_go")
    scaled, out_stored = sem("scaled"), sem("out_stored")

    def expert_first(l, buf, q):
        return moe_first[l][3 * buf + q] if buf < 2 else l * (E_N // 3)

    def norm2(l, c):
        return gchunk(l, c) + 1 + len(CHUNKS_OF[0]) + (len(CHUNKS_OF[1]) if l else 0)

    def gchunk(l, c):
        return c + len(CHUNKS_OF[0]) * l


    h1_d = scratch("h1_d", [LAT, D])
    r_rows = at(0, CL * D).rearrange("p (c d) -> p c d", c=CL)
    masks = at(16, LEVELS * P).rearrange("p (l n) -> p l n", l=LEVELS)
    prod = at(19.5, 4 * P)
    gate_w = [keep[0:32, 1016:1016 + COL], at(21.5, COL, 0, 32)]
    qk = at(48, HEADS * 2 * LAT).rearrange("p (h m n) -> p h m n", h=HEADS, m=2)
    k_ctx = at(64, HEADS * CTX).rearrange("p (h n) -> p h n", h=HEADS)
    v_rows = at(68, 6 * D).rearrange("p (c d) -> p c d", c=6)
    lrT = at(92, NT, 0, 32)
    soft = at(95, NT)
    kt_rows = at(99, 4 * P)
    state = at(101, 2 * DVH).rearrange("p (r n) -> p r n", r=2)
    lr_w = at(103, KD * 32).rearrange("p (k c) -> p k c", k=KD)
    norm_g = at(40, D)
    g_stats = keep[:, 1528:1552].rearrange("p (c s) -> p c s", c=CL)
    g_mv = keep[:, 1552:1560].rearrange("p (c s) -> p c s", c=CL)
    g_dev, g_rdev = keep[:, 1560:1564], keep[:, 1564:1568]
    cums = [ring[:, 1536 * i:1536 * (i + 1)].rearrange("p (r n) -> p r n", r=2) for i in (0, 1)]
    att_near = ring[:, 3072:3584]
    att_next = ring[:, 3584:4096]
    lev = [ring[:, UNIT + 1024 * i:UNIT + 1024 * i + 1024] for i in range(3)]
    att_far = ring[:, UNIT + 3072:UNIT + 4096]
    o_rows = slot(2).rearrange("p (c d) -> p c d", c=CL)

    h1_stored, gla_in, zero_w, gates_abs = sem("h1_stored"), sem("gla_small_in"), sem("zero_w"), sem("gates_abs")
    gates_ln, cum_done, args_done, exps_done = sem("gates_ln"), sem("cum_done"), sem("args_done"), sem("exps_done")
    scaled_qk, near_done = sem("scaled_qk"), sem("near_done")
    norm_in, o_var, o_dev, o_normed, rows_gated = (
        sem("norm_in"), sem("o_var"), sem("o_dev"), sem("o_normed"), sem("rows_gated"))
    gain_done = [sem(f"gain_done{c}") for c in range(CL)]
    silu_done, y_rows_done = sem("silu_done"), sem("y_rows_done")

    N_LV = LEVELS + 5
    LV_CTX, LV_STATE = LEVELS + 3, LEVELS + 4
    ITEMS = [(h, lv) for h in range(HEADS) for lv in range(N_LV)]

    PROJ = ([("v", 0, c) for c in range(6)] + [("v", 1, c) for c in range(6)] +
            [("r", half, c) for half in (0, 1) for c in range(CL)])
    PROJ_AT = {}
    at_levels = ((0, 2, 4, 6, 6, 8), (0, 3, 6, 6, 8), (0, 3, 6, 6, 8), (0, 2, 4, 6))
    for hd in range(HEADS):
        for lv in at_levels[hd]:
            PROJ_AT.setdefault((hd, lv), []).append(PROJ.pop(0))

    def gated_rows(eng, c):
        eng.wait_ge(silu_done, c + 1)
        eng.wait_ge(norm_in, 16)
        eng.tensor_tensor(r_rows[:, c, :], r_rows[:, c, :], norm_g, ALU.mult).then_inc(gain_done[c], 1)
        eng.wait_ge(gain_done[c], 1)
        eng.wait_ge(o_normed, HEADS - 1)
        cols = slice(0, DVH * (HEADS - 1))
        eng.tensor_tensor(r_rows[:, c, cols], r_rows[:, c, cols], o_rows[:, c, cols], ALU.mult).then_inc(rows_gated, 1)

    def last_use(i):
        hd, lv = ITEMS[i]
        if lv == LV_CTX:
            return ("kt", hd)
        if lv == LV_STATE:
            return ("o", hd, CL - 1)
        if lv == LEVELS + 2:
            return ("att", i, 1)
        return ("att", i, 0)

    def buffer_free(eng, i):
        if i >= 3 and ITEMS[i - 3][1] != 0:
            filled(eng, last_use(i - 3))

    def scaled_items(i):
        return sum(1 for q in range(i + 1) if ITEMS[q][1] != 0)

    def arg_items(i):
        return sum(1 for q in range(i + 1) if ITEMS[q][1] not in (0, LV_STATE))

    plan = PsumPlan()

    def filled(eng, name):
        eng.wait_ge(psum_filled, plan.of[name][1])

    def evacuated(eng, name):
        b, _, used = plan.of[name]
        eng.wait_ge(psum_drained[b], used + 1)

    def drained(name):
        return psum_drained[plan.of[name][0]]

    def res(name):
        return psum[plan.of[name][0]]

    def unit_landed(eng, name):
        s, k = units.of[name]
        eng.wait_ge(landed[s], 16 * (k + 1))

    def unit(name):
        return slot(units.of[name][0])

    def made(eng, n):
        i, f = CHUNKS[n - 1]
        evacuated(eng, ("x", 3, i, f))

    STREAMS = [("lat", 0, LAT, 0), ("ctx", 1, CTX, LAT)]

    STEPS = [(s, half, o) for s in (0, 1) for o in (0, 1) for half in (0, 1)]
    last_step = len(STEPS) - 1
    FREQ = (CL // 2, CC // 2)
    CHUNKS = [(i, f) for i, (s, _, _) in enumerate(STEPS) for f in range(FREQ[s])]

    def chunk_base(i):
        return sum(FREQ[s] for s, _, _ in STEPS[:i])

    PARTS = [(0, 0), (0, 1), (1, 0), (1, 1)]

    filt_u = slot(units.of[("filt", 0)][0])
    w4 = filt_u[:, 0:2 * D].rearrange("p (o c) -> p o c", o=2)
    c_small = filt_u[:, 2 * D:3 * D].rearrange("p (i a r c n) -> p i a r c n", i=2, a=2, r=2, c=1)
    dft = slot(units.of[("dft", 0)][0], 0, HALF).rearrange("p (a r c n) -> p a r c n", a=2, r=2, c=2)
    idft = slot(units.of[("idft", 0)][0], 0, HALF).rearrange("p (a r c n) -> p a r c n", a=2, r=2, c=2)

    def basis(s, inverse, a, par):
        if s:
            return c_small[:, inverse, a, par]
        return (idft if inverse else dft)[:, a, par]

    block = ctx.enter_context(nc.Block())

    @block.tensor
    def _(pe):
        def begin(name, bank=None):
            b, _, used = plan.add(name, bank)
            if used:
                pe.wait_ge(psum_drained[b], used)
            return psum[b]

        def turn(dst, src, n=P):
            return pe.transpose(dst, src, ident[0:n, 0:n])

        def cond_columns():
            pe.wait_ge(keep_in, 32)
            pe.wait_ge(cond_silu, 1)
            turn(begin("cond_T", 6)[:, 0:16], cond_rows[:, :], 16).then_inc(psum_filled, 1)
            pe.wait_ge(small_in, 16 * 4)
            turn(begin("small_T", 7)[:, 0:P], small_rows[:, :]).then_inc(psum_filled, 1)

        def modulation():
            evacuated(pe, "cond_T")
            with pe.Fori(0, N_MOD // SLOTS) as i:
                for u in range(SLOTS):
                    pe.wait_ge(landed[u], 16 * i + 16)
                    pe.wait_ge(mod_drained, SLOTS * i + u + 1)
                    w = slot(u).rearrange("p (k c) -> p k c", k=KD)
                    for k in range(KD):
                        for q in range(4):
                            mm = pe.matmul(psum[u][32 * q:32 * q + 32, 0:P], s_cols[:, k, :],
                                           w[:, k, P * q:P * q + P], start=(k == 0), stop=(k == KD - 1))
                    mm.then_inc(mod_filled, 1)
            pe.wait_ge(mod_drained, N_MOD + SLOTS)

        def modulation_columns():
            pe.wait_ge(mod_back, 64)
            for l in range(2):
                turn(begin(("mod_T", l))[:, 0:96], mod_rows[:, l, :], 96).then_inc(psum_filled, 1)

        def stream_columns():
            pe.wait_ge(pe_added, 1)
            for k in range(KD):
                b = begin(("aT0", 0, k))
                for c in range(CL):
                    mm = turn(b[:, P * c:P * c + P], x_rows[:, c, P * k:P * k + P])
                mm.then_inc(psum_filled, 1)
            pe.wait_ge(ctx_in, 16)
            for k in range(KD):
                b = begin(("aT0", 1, k))
                for c in range(CC):
                    mm = turn(b[:, P * c:P * c + P], x_rows[:, CL + c, P * k:P * k + P])
                mm.then_inc(psum_filled, 1)

        def filter_mlp(j):
            w = (f_w1, f_w2, f_w3)[j]
            x = (zT, hf1, hf2)[j]
            m = 2 * HF if j == 2 else HF
            if j == 0:
                pe.wait_ge(fw_in, 16 * 9)
            else:
                pe.wait_ge(sin_done, j)
            for _, s, n, o in STREAMS:
                pe.matmul(begin(("mlp", j, s))[0:m, 0:n], w, x[:, o:o + n],
                          start=True, stop=True).then_inc(psum_filled, 1)

        def project(ch):
            j, cc = ch // 4, ch % 4
            if ch == 0:
                pe.wait_ge(a_done, KD)
            if cc == 0:
                unit_landed(pe, ("hy_in", j))
            w = unit(("hy_in", j)).rearrange("p (k c) -> p k c", k=KD)
            for _, s, n, o in STREAMS:
                b = begin(("proj", s, ch))
                for k in range(KD):
                    mm = pe.matmul(b[:, 0:n], w[:, k, P * cc:P * cc + P], aT[:, k, o:o + n],
                                   start=(k == 0), stop=(k == KD - 1))
                mm.then_inc(psum_filled, 1)

        def token_major(ch):
            pe.wait_ge(conv_done, ch + 1)
            for _, s, n, o in STREAMS:
                b = begin(("tm", s, ch))
                for c in range(n // P):
                    par, q = divmod(c, n // P // 2)
                    mm = turn(b[:, P * c:P * c + P], zc[ch % 2][:, o + 2 * P * q + par:o + 2 * P * (q + 1):2])
                mm.then_inc(psum_filled, 1)

        def filters(i):
            s, half, o = STEPS[i]
            if i == 0:
                pe.wait_ge(hf_done, 1)
                pe.wait_ge(filt_in, 48)
            for tc in range((CL, CC)[s]):
                for a, hf in enumerate((hf_sum, hf_diff)):
                    col = LAT * s + P * tc
                    pe.matmul(begin(("filt", i, tc, a))[:, :], hf[:, col:col + P],
                              w4[:, o, COL * half:COL * half + COL],
                              start=True, stop=True).then_inc(psum_filled, 1)

        def taps_spectrum(i, f):
            s, half, o = STEPS[i]
            n = (CL, CC)[s]
            m = n // 2
            pe.wait_ge(skip_added, i + 1)
            for a in (0, 1):
                evacuated(pe, ("filt", i, n - 1, a))
            if i == 0:
                unit_landed(pe, ("dft", 0))
            parts = [("k", 0, P), ("k", 1, P)] + [("ny", 2, 1)] * (f == 0) + [("k", 2, P), ("k", 3, P)]
            for name, j, rows in parts:
                a, par = PARTS[j]
                b = begin((name, j, i, f))
                src = filt[0] if name == "ny" else filt[a]
                for c in range(m):
                    mm = pe.matmul(b[0:rows, :], basis(s, 0, a, par)[:, c, P * f:P * f + rows],
                                   src[:, m * par + c, :], start=(c == 0), stop=(c == m - 1))
                mm.then_inc(psum_filled, 1)

        def signal_spectrum(i, f):
            s, half, o = STEPS[i]
            n = (CL, CC)[s]
            m = n // 2
            if o:
                evacuated(pe, ("y", STEPS.index((s, half, 0)), n - 1))
            elif i == 0:
                evacuated(pe, ("tm", 0, 15))
                evacuated(pe, ("tm", 1, 15))
            for j, (a, par) in enumerate(PARTS):
                b = begin(("x", j, i, f))
                for c in range(m):
                    mm = pe.matmul(b[:, :], basis(s, 0, a, par)[:, c, P * f:P * f + P],
                                   v_t[:, CL * s + m * par + c, COL * half:COL * half + COL],
                                   start=(c == 0), stop=(c == m - 1))
                mm.then_inc(psum_filled, 1)

        def inverse(i):
            s, half, o = STEPS[i]
            n = (CL, CC)[s]
            m = n // 2
            pe.wait_ge(z_ready, 5 * chunk_base(i + 1))
            if i == 0:
                unit_landed(pe, ("idft", 0))
            if o == 0:
                for c in range(n):
                    par, q = divmod(c, m)
                    b = begin(("y", i, c))
                    for f in range(m):
                        for a in (0, 1):
                            mm = pe.matmul(b[:, :], basis(s, 1, a, par)[:, f, P * q:P * q + P], z[a][:, par, f, :],
                                           start=(f == 0 and a == 0), stop=(f == m - 1 and a == 1))
                    mm.then_inc(psum_filled, 1)
            else:
                for cc in range(4):
                    b = begin(("y", i, cc))
                    for par in (0, 1):
                        for f in range(m):
                            for a in (0, 1):
                                mm = pe.matmul(b[:, m * P * par:m * P * par + m * P],
                                               z[a][:, par, f, P * cc:P * cc + P], basis(s, 1, a, par)[:, f, :],
                                               start=(f == 0 and a == 0), stop=(f == m - 1 and a == 1))
                    mm.then_inc(psum_filled, 1)

        cond_columns()
        modulation()
        filter_mlp(0)
        stream_columns()
        modulation_columns()
        for ch in range(24):
            project(ch)
            if ch in (1, 3):
                filter_mlp((ch + 1) // 2)
            if 1 <= ch <= 16:
                token_major(ch - 1)
        filters(0)
        for i, f in CHUNKS:
            taps_spectrum(i, f)
            if f == FREQ[STEPS[i][0]] - 1 and i < last_step:
                filters(i + 1)
            signal_spectrum(i, f)
            if f == 0 and i:
                inverse(i - 1)

        def out_project(l, c, halves=(0, 1)):
            src = mixed[l]
            w = ("hy_out", "gla_out")[l]
            for half in halves:
                if c == 0:
                    unit_landed(pe, (w, half))
                b = begin(("out", l, c, half))
                wt = unit((w, half)).rearrange("p (k c) -> p k c", k=KD)
                for k in range(KD):
                    mm = pe.matmul(b[:, :], src[:, k, P * c:P * c + P], wt[:, k, :],
                                   start=(k == 0), stop=(k == KD - 1))
                mm.then_inc(psum_filled, 1)

        def route_logits(l, c):
            g = gchunk(l, c)
            pe.wait_ge(a2_done, g + 1)
            for h in (0, 1):
                b = begin(("a2T", l, c, h))
                for k in range(4):
                    mm = turn(b[:, P * k:P * k + P], a2[c % 2][:, P * (4 * h + k):P * (4 * h + k) + P])
                mm.then_inc(psum_filled, 1)
            for h in (0, 1):
                evacuated(pe, ("a2T", l, c, h))
            if c == 0 and l == 0:
                pe.wait_ge(route_in, 64)
            b = begin(("logit", l, c))
            for k in range(KD):
                mm = pe.matmul(b[:, 0:E_N], a2T[:, k, :], router_w[:, k, :],
                               start=(k == 0), stop=(k == KD - 1))
            mm.then_inc(psum_filled, 1)

        def ranks(l):
            n = len(CHUNKS_OF[l])
            w = E_N * n
            pe.wait_ge(picked, l + 1)
            b = begin(("rank", l))
            pe.matmul(b[:, 0:w], before, temps[7][:, 0:w], start=True, stop=False)
            pe.matmul(b[:, 0:w], ones, chosen_before[:, 0:w], start=False, stop=True).then_inc(psum_filled, 1)
            pe.matmul(begin(("count", l))[:, 0:E_N], ones, chosen_before[:, w:w + E_N],
                      start=True, stop=True).then_inc(psum_filled, 1)

        def slot_table(l):
            n = 2 * len(CHUNKS_OF[l])
            nb = blocks_max((NT, LAT)[l]) + 2
            pe.wait_ge(hots_done, l + 1)
            b = begin(("slots", l))
            for j in range(n):
                mm = pe.matmul(b[0:SB, 0:nb], hot_slot[:, j, :], hot_block[:, j, 0:nb],
                               start=(j == 0), stop=(j == n - 1))
            mm.then_inc(psum_filled, 1)

        def experts(l):
            pX, pG, pH, pY = psum[0], psum[1:3], psum[3:5], psum[5]
            for b in range(6):
                if plan.used[b]:
                    pe.wait_ge(psum_drained[b], plan.used[b])
            pe.wait_ge(starts_done, l + 1)

            def turn_rows():
                for k in range(KD):
                    mm = turn(pX[:, SB * k:SB * k + SB], x_slots[:, P * k:P * k + P], SB)
                mm.then_inc(x_turned[l], 1)

            pe.wait_ge(x_landed[l], 16)
            turn_rows()

            def expert(e, buf, turn_no):
                lo = pe.value_load(starts[:, e], min_val=0, max_val=blocks_max(NT))
                hi = pe.value_load(starts[:, (ds(e.start + 1, 1) if isinstance(e, bass.DynSlice)
                                              else slice(e.start + 1, e.start + 2))],
                                   min_val=1, max_val=blocks_max(NT))
                w13 = expert_w13[buf]
                w2 = expert_w2[buf]
                with pe.Fori(lo, hi) as b:
                    for q in (0, 1):
                        pe.wait_ge(expert_in[buf][q], turn_no + 16 * (expert_first(l, buf, q) + 1))
                    pe.wait_ge(xT_done[l], b + 1)
                    for c in (0, 1):
                        for k in range(KD):
                            for half in (0, 1):
                                col = 256 * half + P * c
                                mm = pe.matmul(pG[c][SB * half:SB * half + SB, 0:256].rearrange(
                                    "p (m c) -> p m c", m=2), xT[:, k, :], w13[:, :, k, col:col + P],
                                    start=(k == 0), stop=(k == KD - 1))
                        mm.then_inc(up_filled[l], 1)
                    pe.wait_ge(x_moved[l], b + 1)
                    pe.wait_ge(hid_done[l], 2 * b + 1)
                    turn(pH[0][:, 0:P], hid[0]).then_inc(hid_turned[l], 1)
                    turn_rows()
                    pe.wait_ge(hid_done[l], 2 * b + 2)
                    turn(pH[1][:, 0:P], hid[1]).then_inc(hid_turned[l], 1)
                    pe.wait_ge(expert_in[buf][2], turn_no + 16 * (expert_first(l, buf, 2) + 1))
                    pe.wait_ge(y_copied[l], b + 1)
                    for c in (0, 1):
                        pe.wait_ge(hidT_done[l], 2 * b + c + 1)
                        for f in (0, 1):
                            for half in (0, 1):
                                mm = pe.matmul(pY[SB * half:SB * half + SB, :],
                                               hidT[c][:, SB * f:SB * f + SB],
                                               w2[:, 2 * f + c, COL * half:COL * half + COL],
                                               start=(c == 0 and f == 0), stop=(c == 1 and f == 1))
                    mm.then_inc(y_filled[l], 1)

            with pe.Fori(0, E_N // 3) as third:
                for buf in range(3):
                    expert(ds(3 * third + buf, 1), buf, 16 * third)
            for e in range(E_N - E_N % 3, E_N):
                expert(slice(e, e + 1), e % 3, 16 * (e // 3))
            total = pe.value_load(starts[:, E_N:E_N + 1], min_val=1, max_val=blocks_max(NT))
            pe.wait_ge(xT_done[l], total + 1)
            pe.wait_ge(y_copied[l], total + 1)
            pe.wait_ge(starts_done, l + 1)

        def finish(l):
            last = len(CHUNKS_OF[l]) - 1
            for c in CHUNKS_OF[l]:
                out_project(l, c, (1,) if (l, c) in ((0, 0), (0, 1)) else (0, 1))
                if c:
                    route_logits(l, c - 1)
            route_logits(l, last)
            ranks(l)
            slot_table(l)
            experts(l)

        for i in (2, 3):
            evacuated(pe, ("y", i, 3))
        for c in (0, 1):
            out_project(0, c, (0,))
        inverse(last_step)
        evacuated(pe, ("y", last_step, 3))
        finish(0)

        def columns1(chunks):
            for c in chunks:
                pe.wait_ge(h_next, c + 1)
                for h in (0, 1):
                    b = begin(("aT1", c, h))
                    for j in range(4):
                        k = 4 * h + j
                        mm = turn(b[:, P * j:P * j + P], h_rows[:, c, P * k:P * k + P])
                    mm.then_inc(psum_filled, 1)

        def low_rank():
            pe.wait_ge(gla_in, 16 * 4)
            for c in range(6):
                for h in (0, 1):
                    evacuated(pe, ("aT1", c, h))
            for _, s, n, o in STREAMS:
                b = begin(("lr", s))
                for k in range(KD):
                    mm = pe.matmul(b[0:32, 0:n], lr_w[:, k, :], aT1[:, k, o:o + n],
                                   start=(k == 0), stop=(k == KD - 1))
                mm.then_inc(psum_filled, 1)

        def gates(hd):
            if hd == 0:
                evacuated(pe, ("lr", 0))
                evacuated(pe, ("lr", 1))
                pe.wait_ge(zero_w, 1)
            for r in (0, 1):
                for _, s, n, o in STREAMS:
                    pe.matmul(begin(("g", hd, r, s))[:, 0:n], gate_w[r][:, P * hd:P * hd + P], lrT[:, o:o + n],
                              start=True, stop=True).then_inc(psum_filled, 1)

        def queries_keys(m):
            if m == 0:
                for c in range(CL):
                    for h in (0, 1):
                        evacuated(pe, ("aT1", c, h))
            unit_landed(pe, ("gla_in", m))
            w = unit(("gla_in", m)).rearrange("p (k c) -> p k c", k=KD)
            for hd in range(HEADS):
                for _, s, n, o in STREAMS[:1 + m]:
                    b = begin(("qk", m, hd, s))
                    for k in range(KD):
                        mm = pe.matmul(b[:, 0:n], w[:, k, P * hd:P * hd + P], aT1[:, k, o:o + n],
                                       start=(k == 0), stop=(k == KD - 1))
                    mm.then_inc(psum_filled, 1)

        def value_gate(name):
            kind, half, c = name
            j = (2 if kind == "v" else 4) + half
            if c == 0:
                unit_landed(pe, ("gla_in", j))
            w = unit(("gla_in", j)).rearrange("p (k c) -> p k c", k=KD)
            b = begin(name)
            for k in range(KD):
                mm = pe.matmul(b[:, :], aT1[:, k, P * c:P * c + P], w[:, k, :],
                               start=(k == 0), stop=(k == KD - 1))
            mm.then_inc(psum_filled, 1)

        def attention(i):
            hd, lv = ITEMS[i]
            if lv == 0:
                q, key = qk[:, hd, 0, :], qk[:, hd, 1, :]
                evacuated(pe, ("qk", 0, hd, 0))
                evacuated(pe, ("qk", 1, hd, 0))
            else:
                q, key = lev[i % 3][:, 0:LAT], lev[i % 3][:, LAT:2 * LAT]
                pe.wait_ge(scaled_qk, scaled_items(i))
            if lv <= LEVELS + 1:
                b = begin(("att", i, 0))
                for s in range(CL):
                    u = s if lv <= LEVELS else s ^ 1
                    mm = pe.matmul(b[:, P * s:P * s + P], key[:, P * s:P * s + P], q[:, P * u:P * u + P],
                                   start=True, stop=True)
                mm.then_inc(psum_filled, 1)
            elif lv == LEVELS + 2:
                for h in (0, 1):
                    b = begin(("att", i, h))
                    for s in (0, 1):
                        sb, u = 2 * h + s, 2 * (1 - h)
                        mm = pe.matmul(b[:, 2 * P * s:2 * P * s + 2 * P], key[:, P * sb:P * sb + P],
                                       q[:, P * u:P * u + 2 * P], start=True, stop=True)
                    mm.then_inc(psum_filled, 1)
            elif lv == LV_CTX:
                b = begin(("kt", hd))
                for j in range(4):
                    mm = turn(b[:, P * j:P * j + P], lev[i % 3][:, P * j:P * j + P])
                mm.then_inc(psum_filled, 1)
            else:
                context_state(hd)
                outputs(i, hd)

        def context_state(hd):
            evacuated(pe, ("kt", hd))
            for c in (CL, CL + 1):
                evacuated(pe, ("v", hd // 2, c))
            b = begin(("st", hd))
            for r in (0, 1):
                for c in range(CC):
                    mm = pe.matmul(b[:, DVH * r:DVH * r + DVH], kt_rows[:, P * (CC * r + c):P * (CC * r + c) + P],
                                   v_rows[:, CL + c, DVH * hd:DVH * hd + DVH], start=(c == 0), stop=(c == CC - 1))
            mm.then_inc(psum_filled, 1)

        def outputs(i, hd):
            q = lev[i % 3]
            evacuated(pe, ("st", hd))
            pe.wait_ge(near_done, LEVELS * (hd + 1))
            for s in range(CL):
                evacuated(pe, ("v", hd // 2, s))
            j = i - 2
            evacuated(pe, ("att", j - 1, 0))
            evacuated(pe, ("att", j - 2, 0))
            evacuated(pe, ("att", N_LV * hd, 0))
            for h in (0, 1):
                evacuated(pe, ("att", j, h))
            for u in range(CL):
                b = begin(("o", hd, u))
                for s in range(CL):
                    if s == u:
                        a = att_near[:, P * s:P * s + P]
                    elif s == u ^ 1:
                        a = att_next[:, P * s:P * s + P]
                    else:
                        a = att_far[:, 2 * P * s + P * (u % 2):2 * P * s + P * (u % 2) + P]
                    pe.matmul(b[:, 0:DVH], a, v_rows[:, s, DVH * hd:DVH * hd + DVH], start=(s == 0), stop=False)
                for r in (0, 1):
                    mm = pe.matmul(b[:, 0:DVH], q[:, LAT * r + P * u:LAT * r + P * u + P], state[:, r, :],
                                   start=False, stop=(r == 1))
                mm.then_inc(psum_filled, 1)

        def output_columns():
            pe.wait_ge(y_rows_done, 1)
            for k in range(KD):
                b = begin(("yT", k))
                for c in range(CL):
                    mm = turn(b[:, P * c:P * c + P], r_rows[:, c, P * k:P * k + P])
                mm.then_inc(psum_filled, 1)
            for k in range(KD):
                evacuated(pe, ("yT", k))

        columns1(range(CL))
        queries_keys(0)
        columns1(range(CL, 6))
        low_rank()
        gates(0)
        queries_keys(1)
        for i, (hd, lv) in enumerate(ITEMS):
            for name in PROJ_AT.get((hd, lv), []):
                value_gate(name)
            attention(i)
            if lv == 5 and hd + 1 < HEADS:
                gates(hd + 1)
        output_columns()
        finish(1)

    @block.scalar
    def _(act):
        links = [0]

        def link(ins):
            ins.then_inc(act_link, 1)
            links[0] += 1
            act.wait_ge(act_link, links[0])

        def early_loads():
            act.dma_start(keep[:, 0:128], t["ident"]).then_inc(keep_in, 16)
            act.dma_start(cond_rows[0:8, :], t["c"].rearrange("b (k p) -> (b k) p", p=P)).then_inc(cond_in, 16)
            act.dma_start(cond_rows[8:16, :], t["c_ctx"].rearrange("(k p) -> k p", p=P)).then_inc(cond_in, 16)
            act.dma_start(keep[:, 1984:1987], t["marks"]).then_inc(keep_in, 16)
            act.dma_start(small_rows[0:72, :],
                          t["hy_conv_w"].rearrange("o j (c p) -> (o j c) p", p=P)).then_inc(small_in, 16)
            act.dma_start(small_rows[72:96, :],
                          t["hy_b_in"].rearrange("o (c p) -> (o c) p", p=P)).then_inc(small_in, 16)
            act.dma_start(small_rows[96:120, :],
                          t["hy_conv_b"].rearrange("o (c p) -> (o c) p", p=P)).then_inc(small_in, 16)
            act.dma_start(small_rows[120:128, :],
                          t["gla_b_gate"].rearrange("o r (c p) -> (o r c) p", p=P)).then_inc(small_in, 16)
            act.wait_ge(mod_zeroed, 1)
            bias = t["b_mod"].rearrange("l (n q c) -> q (l n) c", q=4, c=P)
            for q in range(4):
                for r in range(2):
                    act.dma_start(mod_acc[32 * q + r:32 * q + r + 1, :, :],
                                  bias[q:q + 1]).then_inc(bias_in, 16)
            act.dma_start(x_rows[:, 0:CL, :],
                          t["x"].rearrange("b (c p) d -> p (b c) d", p=P)).then_inc(x_in, 16)
            act.dma_start(pos_rows, t["pos_rows"].rearrange("(c p) d -> p c d", p=P)).then_inc(pe_in, 16)
            act.dma_start(pos_cols, t["pos_cols"]).then_inc(pe_in, 16)
            act.dma_start(x_rows[:, CL:6, :],
                          t["ctx"].rearrange("b (c p) d -> p (b c) d", p=P)).then_inc(ctx_in, 16)
            act.dma_start(zT, t["zT"]).then_inc(fw_in, 16)
            act.dma_start(f_w1, t["hy_f_w1"][0]).then_inc(fw_in, 16)
            act.dma_start(f_w2, t["hy_f_w2"][0]).then_inc(fw_in, 16)
            for i in (0, 1):
                act.dma_start(f_w3[:, HF * i:HF * i + HF], t["hy_f_w3"][0]).then_inc(fw_in, 16)
            act.dma_start(f_b[0:HF, 0:1], t["hy_f_b1"].rearrange("o p -> p o")).then_inc(fw_in, 16)
            act.dma_start(f_b[0:HF, 1:2], t["hy_f_b2"].rearrange("o p -> p o")).then_inc(fw_in, 16)
            for i in (0, 1):
                act.dma_start(f_b[HF * i:HF * i + HF, 2:3],
                              t["hy_f_b3"].rearrange("o p -> p o")).then_inc(fw_in, 16)

        def cond():
            act.wait_ge(cond_in, 32)
            act.activation(cond_rows, cond_rows, ACT.Silu).then_inc(cond_silu, 1)

        def store_mod():
            act.wait_ge(mod_drained, N_MOD + SLOTS)
            for q in range(4):
                act.dma_start(mod_d[:, :, q, :], mod_acc[32 * q:32 * q + 2, :, :]).then_inc(mod_stored, 16)
            stream_columns(0)
            act.wait_ge(mod_stored, 64)
            for l in range(2):
                for r in range(2):
                    rows = mod_d[r, 12 * l:12 * l + 12].rearrange("n q c -> (n q) c")
                    act.dma_start(mod_rows[48 * r:48 * r + 48, l, :], rows).then_inc(mod_back, 16)

        def stream_columns(s):
            n, o = STREAMS[s][2:]
            for k in range(KD):
                name = ("aT0", s, k)
                filled(act, name)
                act.copy(aT[:, k, o:o + n], res(name)[:, 0:n]).then_inc(drained(name), 1)

        def modulate_odd():
            act.wait_ge(modT_done, 2)
            for k in range(1, KD, 2):
                for _, s, n, o in STREAMS:
                    evacuated(act, ("aT0", s, k))
                    ins = act.activation(aT[:, k, o:o + n], aT[:, k, o:o + n], ACT.Identity,
                                         scale=modT[:, 0, s, 1, k:k + 1], bias=modT[:, 0, s, 0, k:k + 1])
                ins.then_inc(a_done, 1)

        def store_h0():
            act.wait_ge(pe_added, 1)
            act.dma_start(h0_d.rearrange("(c p) d -> p c d", p=P), x_rows[:, 0:CL, :]).then_inc(h0_stored, 16)

        def sines(j):
            m = 2 * HF if j == 2 else HF
            dst = (hf1, hf2, hf_sum)[j]
            act.wait_ge(sin_arg, j + 1)
            act.activation(dst[0:m, :], arg_u[0:m, :], ACT.Sin).then_inc(sin_done, 1)

        def biased(ch):
            if ch == 0:
                act.wait_ge(edges_zeroed, 4)
                evacuated(act, "small_T")
            if ch >= 2:
                act.wait_ge(conv_done, ch - 1)
            tap = taps[ch % 2]
            for _, s, n, o in STREAMS:
                name = ("proj", s, ch)
                filled(act, name)
                lo = 1 + s * (LAT + 2)
                act.activation(tap[:, lo:lo + n], res(name)[:, 0:n], ACT.Identity,
                               bias=b_in(ch)).then_inc(drained(name), 1)

        def gather_rows(ch):
            if ch == 0:
                act.wait_ge(h0_stored, 16)
            dst = (v_t, x1_t)[ch // 8]
            for _, s, n, o in STREAMS:
                name = ("tm", s, ch)
                filled(act, name)
                act.copy(dst[:, CL * s:CL * s + n // P, P * (ch % 8):P * (ch % 8) + P],
                         res(name)[:, 0:n].rearrange("p (c x) -> p c x", x=P)).then_inc(drained(name), 1)

        def load_windows(i, tiles):
            s, half, o = STEPS[i]
            if 0 in tiles:
                if i == 0:
                    filled(act, ("proj", 1, 23))
                else:
                    act.wait_ge(skip_added, i)
                act.dma_start(skip_row, t["hy_skip"][0, o:o + 1, COL * half:COL * half + COL]).then_inc(skip_in, 16)
            for tc in tiles:
                g = win_loads[0]
                if g >= 2:
                    evacuated(act, win_use[g - 2])
                act.dma_start(win[g % 2], t[("window_lat", "window_ctx")[s]][
                    P * tc:P * tc + P, COL * half:COL * half + COL]).then_inc(win_in[g % 2], 16)
                win_loads[0] += 1

        win_loads = [0]
        win_use = [("filt", i, tc, 1) for i in range(len(STEPS)) for tc in range((CL, CC)[STEPS[i][0]])]

        def keep_spectrum(i, f):
            g = chunk_base(i) + f
            if g >= 2:
                made(act, g - 1)
            if f == 0 and i:
                made(act, chunk_base(i - 1) + 1)
            if g == 0:
                filled(act, ("proj", 1, 23))
            k = k_parts[g % 2]
            for j in range(4):
                name = ("k", j, i, f)
                filled(act, name)
                if f:
                    act.copy(k[:, j, :], res(name)[:, :]).then_inc(drained(name), 1)
                elif j == 0:
                    act.copy(k_alt[:, 0, :], res(name)[:, :])
                    act.copy(k[:, 0, :], res(name)[:, :]).then_inc(drained(name), 1)
                elif j == 1:
                    act.copy(k_alt[:, 1, :], res(name)[:, :])
                    act.copy(k_alt[:, 2, :], res(name)[:, :])
                    act.copy(k[:, 1, :], res(name)[:, :]).then_inc(drained(name), 1)
                    evacuated(act, ("k", 0, i, f))
                    filled(act, ("ny", 2, i, f))
                    act.copy(k_alt[0:1, 0, :], res(("ny", 2, i, f))[0:1, :]).then_inc(
                        drained(("ny", 2, i, f)), 1)
                elif j == 2:
                    act.activation(k[:, 2, :], res(name)[:, :], ACT.Copy, scale=rowmask).then_inc(drained(name), 1)
                else:
                    evacuated(act, ("k", 1, i, f))
                    act.activation(k_alt[0:1, 1, :], res(name)[0:1, :], ACT.Copy, scale=-1.0)
                    act.copy(k_alt[0:1, 2, :], res(name)[0:1, :])
                    act.activation(k[:, 3, :], res(name)[:, :], ACT.Copy, scale=rowmask).then_inc(drained(name), 1)

        early_loads()
        cond()
        store_mod()
        store_h0()
        stream_columns(1)
        sines(0)
        modulate_odd()
        for ch in range(24):
            if ch == 2:
                sines(1)
            if ch == 4:
                sines(2)
            biased(ch)
            if 1 <= ch <= 16:
                gather_rows(ch - 1)
        load_windows(0, range(CL))
        for i, f in CHUNKS:
            ahead = f == FREQ[STEPS[i][0]] - 1 and i < last_step
            if ahead:
                load_windows(i + 1, (0, 1))
            keep_spectrum(i, f)
            if ahead:
                load_windows(i + 1, range(2, (CL, CC)[STEPS[i + 1][0]]))

        def load_vectors(l):
            def put(dst, row):
                act.dma_start(dst, row.partition_broadcast(P)).then_inc(bc_in, 16)

            def mod_row(r, v):
                return mod_d[r, 12 * l + 2 * v:12 * l + 2 * v + 2].rearrange("n q c -> (n q c)")

            vec = {"lng": t["ln_g"][l, 0], "lnb": t["ln_b"][l, 0], "g1l": mod_row(0, 2), "sh2l": mod_row(0, 3),
                   "sc2l": mod_row(0, 4)}
            if l == 0:
                vec.update({"bout": t["hy_b_out"][0], "g1c": mod_row(1, 2), "sh2c": mod_row(1, 3),
                            "sc2c": mod_row(1, 4)})
            for n in BC[l]:
                put(bcast[l][n], vec[n])

        def load_vectors2(l):
            def mod_row(r, v):
                return mod_d[r, 12 * l + 2 * v:12 * l + 2 * v + 2].rearrange("n q c -> (n q c)")

            for n, row in (("g2l", mod_row(0, 5)), ("g2c", mod_row(1, 5)), ("lng", t["ln_g"][l, 1]),
                           ("lnb", t["ln_b"][l, 1])):
                act.dma_start(bc2[n], row.partition_broadcast(P)).then_inc(bc2_in, 16)

        def load_router():
            filled(act, ("filt", last_step, CC - 1, 1))
            act.dma_start(router_w, t["router_w"].rearrange("(k p) e -> p k e", p=P)).then_inc(route_in, 16)
            act.dma_start(router_b, t["router_b"].partition_broadcast(P)).then_inc(route_in, 16)
            act.dma_start(keep[:, 416:690], t["route_c"][:, 0:274]).then_inc(route_in, 16)
            act.dma_start(ramp64, t["route_c"][:, 274:274 + SB]).then_inc(route_in, 16)

        def load_resid(l, c):
            src = (h0_d, h1_d)[l][P * c:P * c + P] if c < CL else t["ctx"][0, P * (c - CL):P * (c - CL) + P]
            act.dma_start(h_rows[:, c, :], src).then_inc(res_in[c], 16)

        def deviation(n):
            act.wait_ge(var_ready, n)
            act.activation(dev, mean_var[:, 1:2], ACT.Sqrt, bias=eps).then_inc(dev_done, 1)

        def store_tokens(l, c):
            act.wait_ge(a2_done, gchunk(l, c) + 1)
            act.dma_start(tok_l[l][P * c:P * c + P], a2[c % 2]).then_inc(tok_stored[c % 2], 16)

        def route_scores(l, c):
            for h in (0, 1):
                filled(act, ("a2T", l, c, h))
                act.copy(a2T[:, 4 * h:4 * h + 4, :], res(("a2T", l, c, h))[:, :].rearrange(
                    "p (k n) -> p k n", k=4)).then_inc(drained(("a2T", l, c, h)), 1)
            filled(act, ("logit", l, c))
            act.activation(scores[:, E_N * c:E_N * c + E_N], res(("logit", l, c))[:, 0:E_N],
                           ACT.Sigmoid).then_inc(drained(("logit", l, c)), 1)

        def scale_first(l, c):
            if c == 0:
                act.wait_ge(combine_go, l + 1)
            else:
                if c >= 2:
                    act.wait_ge(var_ready, norm2(l, c - 2))
            act.wait_ge(pair_in[c], 32 * (l + 1))
            act.activation(mix[c % 2], y_pair[c][0], ACT.Copy, scale=pair_w[:, 0, c:c + 1]).then_inc(first_scaled, 1)

        def pass_on(l, c):
            act.wait_ge(h_next, gchunk(l, c) + 1)
            if l:
                act.dma_start(out[0, P * c:P * c + P], h_rows[:, c, :]).then_inc(out_stored, 16)
                return
            if c < CL:
                act.dma_start(h1_d[P * c:P * c + P], h_rows[:, c, :]).then_inc(h1_stored, 16)
            s = int(c >= CL)
            for h in (0, 1):
                name = ("aT1", c, h)
                filled(act, name)
                for j in range(4):
                    k = 4 * h + j
                    ins = act.activation(aT1[:, k, P * c:P * c + P], res(name)[:, P * j:P * j + P], ACT.Identity,
                                         scale=modT[:, 1, s, 1, k:k + 1], bias=modT[:, 1, s, 0, k:k + 1])
                ins.then_inc(drained(name), 1)

        def experts(l):
            pG, pY = psum[1:3], psum[5]
            act.wait_ge(starts_done, l + 1)
            total = act.value_load(starts[:, E_N:E_N + 1], min_val=1, max_val=blocks_max(NT))
            with act.Fori(0, total) as b:
                for c in (0, 1):
                    act.wait_ge(up_filled[l], 2 * b + c + 1)
                    act.activation(gate_act[c], pG[c][:, 0:P], ACT.Silu).then_inc(gate_done[l], 1)
                act.wait_ge(y_stored[l], 32 * b + 32)
                act.wait_ge(y_filled[l], b + 1)
                act.copy(y_out, pY[:, :]).then_inc(y_copied[l], 1)
                act.wait_ge(y_copied[l], b + 2)
                rows = y_d.rearrange("(b s) d -> b s d", s=SB)[ds(b, 1)].rearrange("o s d -> (o s) d")
                for half in (0, 1):
                    act.dma_start(rows[:, COL * half:COL * half + COL],
                                  y_out[SB * half:SB * half + SB, :]).then_inc(y_stored[l], 16)

        def finish(l):
            chunks = CHUNKS_OF[l]
            for c in chunks:
                if c:
                    route_scores(l, c - 1)
                deviation(gchunk(l, c) + 1 + 6 * l)
                store_tokens(l, c)
            route_scores(l, chunks[-1])
            experts(l)
            load_vectors2(l)
            scale_first(l, 0)
            scale_first(l, 1)
            for c in chunks:
                deviation(norm2(l, c))
                if c + 2 in chunks:
                    scale_first(l, c + 2)
                if c:
                    pass_on(l, c - 1)
            pass_on(l, chunks[-1])

        load_router()
        filled(act, ("k", 3, last_step, 0))
        for c in range(CL):
            load_resid(0, c)
        filled(act, ("x", 3, last_step, FREQ[1] - 1))
        evacuated(act, ("y", last_step - 1, CC - 1))
        load_vectors(0)
        filled(act, ("y", last_step, 3))
        for c in (CL, CL + 1):
            load_resid(0, c)
        finish(0)

        def load_gla():
            act.dma_start(lr_w, t["gla_w_in"][0, :, 3072:3104].rearrange("(k p) c -> p k c", p=P)).then_inc(gla_in, 16)
            act.wait_ge(zero_w, 2)
            for r in (0, 1):
                act.dma_start(gate_w[r][16 * r:16 * r + 16, :], t["gla_w_gate"][0, r]).then_inc(gla_in, 16)
            act.dma_start(masks, t["masks"].rearrange("p (l n) -> p l n", n=P)).then_inc(gla_in, 16)
            evac_qk(0)
            for _, s, n, o in STREAMS:
                filled(act, ("lr", s))
                act.copy(lrT[:, o:o + n], res(("lr", s))[0:32, 0:n]).then_inc(drained(("lr", s)), 1)

        def gates(hd):
            for r in (0, 1):
                n_dir = 2 * hd + r
                if n_dir:
                    act.wait_ge(cum_done, 2 * n_dir)
                for _, s, n, o in STREAMS:
                    filled(act, ("g", hd, r, s))
                    act.activation(soft[:, o:o + n], res(("g", hd, r, s))[:, 0:n], ACT.Abs,
                                   bias=smallT[:, 120 + 4 * r + hd:121 + 4 * r + hd]).then_inc(gates_abs, 1)
                act.wait_ge(gates_abs, 2 * n_dir + 2)
                link(act.activation(soft, soft, ACT.Exp, scale=-1.0))
                act.activation(soft, soft, ACT.Ln, bias=1.0).then_inc(gates_ln, 1)

        def evac_qk(m):
            for hd in range(HEADS):
                for _, s, n, o in STREAMS[:1 + m]:
                    name = ("qk", m, hd, s)
                    filled(act, name)
                    dst = k_ctx[:, hd, :] if s else qk[:, hd, m, :]
                    act.activation(dst, res(name)[:, 0:n], ACT.Copy,
                                   scale=(1.0 if m else float(DKH) ** -0.5)).then_inc(drained(name), 1)

        def evac_value(name):
            kind, half, c = name
            dst = (v_rows if kind == "v" else r_rows)[:, c, COL * half:COL * half + COL]
            if kind == "r" and half == 0 and c == 0:
                act.wait_ge(h1_stored, 16 * CL)
            filled(act, name)
            act.copy(dst, res(name)[:, :]).then_inc(drained(name), 1)

        def exponentials(i):
            hd, lv = ITEMS[i]
            if lv == 0:
                return
            if lv == LV_STATE:
                buffer_free(act, i)
                act.activation(lev[i % 3].rearrange("p (r n) -> p r n", r=2), cums[hd % 2][:, :, 0:LAT],
                               ACT.Exp, scale=1.0 / TAU).then_inc(exps_done, 1)
            else:
                n = 2 * CTX if lv == LV_CTX else 2 * LAT
                act.wait_ge(args_done, arg_items(i))
                act.activation(lev[i % 3][:, 0:n], lev[i % 3][:, 0:n], ACT.Exp,
                               scale=1.0 / TAU).then_inc(exps_done, 1)

        def after_item(i):
            hd, lv = ITEMS[i]
            if lv == LEVELS + 2:
                for h in (0, 1):
                    filled(act, ("att", i, h))
                    act.copy(att_far[:, COL * h:COL * h + COL], res(("att", i, h))[:, :]).then_inc(
                        drained(("att", i, h)), 1)
            if lv == LV_CTX:
                filled(act, ("kt", hd))
                act.copy(kt_rows, res(("kt", hd))[:, :]).then_inc(drained(("kt", hd)), 1)
            if lv == LV_STATE:
                filled(act, ("st", hd))
                act.copy(state.rearrange("p r n -> p (r n)"), res(("st", hd))[:, :]).then_inc(drained(("st", hd)), 1)

        def head_deviation(hd):
            act.wait_ge(o_var, CL * (hd + 1))
            act.activation(g_dev, g_mv[:, :, 1], ACT.Sqrt, bias=eps).then_inc(o_dev, 1)

        def silus():
            for c in range(CL):
                for half in (0, 1):
                    evacuated(act, ("r", half, c))
                act.activation(r_rows[:, c, :], r_rows[:, c, :], ACT.Silu).then_inc(silu_done, 1)

        def gla_tail():
            for k in range(0, KD, 2):
                filled(act, ("yT", k))
                act.copy(mixed[1][:, k, :], res(("yT", k))[:, :]).then_inc(drained(("yT", k)), 1)

        load_gla()
        gates(0)
        evac_qk(1)
        exponentials(1)
        exponentials(2)
        for i, (hd, lv) in enumerate(ITEMS):
            if i and i + 2 < len(ITEMS):
                exponentials(i + 2)
            for name in PROJ_AT.get((hd, lv), []):
                evac_value(name)
            after_item(i)
            if (hd, lv) == (HEADS - 1, LEVELS + 2):
                filled(act, ("r", 1, CL - 1))
                act.dma_start(norm_g, t["gla_norm_g"][0].partition_broadcast(P)).then_inc(norm_in, 16)
            if (hd, lv) == (HEADS - 1, LV_STATE):
                silus()
            if lv == 5 and hd + 1 < HEADS:
                gates(hd + 1)
            if lv == 2 and hd:
                head_deviation(hd - 1)
        head_deviation(HEADS - 1)
        gla_tail()
        filled(act, ("yT", KD - 1))
        for c in range(CL):
            load_resid(1, c)
        load_vectors(1)
        finish(1)

    @block.vector
    def _(dve):
        links = [0]

        def link(ins):
            ins.then_inc(dve_link, 1)
            links[0] += 1
            dve.wait_ge(dve_link, links[0])

        def start():
            dve.memset(mod_acc, 0.0).then_inc(mod_zeroed, 1)
            dve.memset(s_cols, 0.0).then_inc(cols_zeroed, 1)
            filled(dve, "cond_T")
            dve.wait_ge(cols_zeroed, 1)
            dve.tensor_copy(s_cols[:, :, 0:2], res("cond_T")[:, 0:16].rearrange("p (r k) -> p k r", r=2)) \
               .then_inc(drained("cond_T"), 1)
            filled(dve, "small_T")
            dve.tensor_copy(smallT, res("small_T")[:, 0:P]).then_inc(drained("small_T"), 1)
            dve.memset(keep[:, 1987:1988], 0.0).then_inc(mod_drained, SLOTS)

        def modulation():
            dve.wait_ge(bias_in, 16 * 8)
            dve.wait_ge(mod_zeroed, 1)
            with dve.Fori(0, N_MOD // SLOTS) as i:
                for u in range(SLOTS):
                    dve.wait_ge(mod_filled, SLOTS * i + u + 1)
                    cols = mod_acc[:, ds(SLOTS * i + u, 1), :].rearrange("p o c -> p (o c)")
                    dve.tensor_tensor(cols, psum[u][:, 0:P], cols, ALU.add).then_inc(mod_drained, 1)

        def modulation_columns():
            for l in range(2):
                filled(dve, ("mod_T", l))
                dve.tensor_copy(modT[:, l], res(("mod_T", l))[:, 0:96].rearrange(
                    "p (r v k) -> p r v k", r=2, v=6)).then_inc(drained(("mod_T", l)), 1)
            evacuated(dve, ("mod_T", 0))
            evacuated(dve, ("mod_T", 1))
            for l in range(2):
                scale = modT[:, l, :, 1, :]
                dve.tensor_scalar(scale, scale, 1.0, None, ALU.add).then_inc(modT_done, 1)

        def modulate_even():
            dve.wait_ge(modT_done, 2)
            for k in range(0, KD, 2):
                for _, s, n, o in STREAMS:
                    evacuated(dve, ("aT0", s, k))
                    ins = dve.tensor_scalar(aT[:, k, o:o + n], aT[:, k, o:o + n], modT[:, 0, s, 1, k:k + 1],
                                            modT[:, 0, s, 0, k:k + 1], ALU.mult, ALU.add)
                ins.then_inc(a_done, 1)

        def sine_argument(j):
            m = 2 * HF if j == 2 else HF
            u, r = arg_u[0:m, :], arg_t[0:m, :]
            if j == 0:
                dve.wait_ge(fw_in, 16 * 9)
            else:
                dve.wait_ge(sin_done, j)
            for _, s, n, o in STREAMS:
                name = ("mlp", j, s)
                filled(dve, name)
                dve.tensor_scalar(u[:, o:o + n], res(name)[0:m, 0:n], f_b[0:m, j:j + 1], None,
                                  ALU.add).then_inc(drained(name), 1)
            evacuated(dve, ("mlp", j, 0))
            evacuated(dve, ("mlp", j, 1))
            link(dve.tensor_scalar(r, u, float(1.0 / (2.0 * np.pi)), MAGIC, ALU.mult, ALU.add))
            link(dve.tensor_scalar(r, r, MAGIC, None, ALU.subtract))
            link(dve.scalar_tensor_tensor(u, r, -PI2_HI, u, ALU.mult, ALU.add))
            link(dve.scalar_tensor_tensor(u, r, -PI2_LO, u, ALU.mult, ALU.add))
            dve.tensor_scalar(u, u, 3.1415925, -3.1415925, ALU.min, ALU.max).then_inc(sin_arg, 1)

        def short_conv(ch):
            if ch == 0:
                dve.wait_ge(mod_stored, 64)
            if ch < 16:
                dst = zc[ch % 2]
                if ch >= 2:
                    filled(dve, ("tm", 1, ch - 2))
            else:
                dst = x2T[:, ch - 16, :]
                if ch == 16:
                    filled(dve, ("tm", 1, 15))
            parts = []
            for _, s, n, o in STREAMS:
                evacuated(dve, ("proj", s, ch))
                tap = taps[ch % 2][:, s * (LAT + 2):s * (LAT + 2) + n + 2]
                parts.append((dst[:, o:o + n], tap, n))
            for y, tap, n in parts:
                ins = dve.tensor_scalar(y, tap[:, 1:n + 1], conv_w(1, ch), conv_b(ch), ALU.mult, ALU.add)
                ins.then_inc(dve_link, 1)
                links[0] += 1
            dve.wait_ge(dve_link, links[0])
            for y, tap, n in parts:
                ins = dve.scalar_tensor_tensor(y, tap[:, 0:n], conv_w(0, ch), y, ALU.mult, ALU.add)
                ins.then_inc(dve_link, 1)
                links[0] += 1
            dve.wait_ge(dve_link, links[0])
            (y0, tap0, n0), (y1, tap1, n1) = parts
            ins = dve.scalar_tensor_tensor(y0, tap0[:, 2:n0 + 2], conv_w(2, ch), y0, ALU.mult, ALU.add)
            link(ins)
            dve.scalar_tensor_tensor(y1, tap1[:, 2:n1 + 2], conv_w(2, ch), y1, ALU.mult,
                                     ALU.add).then_inc(conv_done, 1)

        windows = [0]

        def windowed(i):
            s, half, o = STEPS[i]
            n = (CL, CC)[s]
            for tc in range(n):
                g = windows[0]
                dve.wait_ge(win_in[g % 2], 16 * (g // 2 + 1))
                for a in (0, 1):
                    name = ("filt", i, tc, a)
                    filled(dve, name)
                    dve.tensor_tensor(filt[a][:, tc, :], res(name)[:, :], win[g % 2],
                                      ALU.mult).then_inc(drained(name), 1)
                windows[0] += 1
            evacuated(dve, ("filt", i, 0, 0))
            dve.wait_ge(skip_in, 16 * (i + 1))
            dve.tensor_tensor(filt[0][0:1, 0, :], filt[0][0:1, 0, :], skip_row, ALU.add).then_inc(skip_added, 1)

        def multiply(i, f):
            g = chunk_base(i) + f
            for j in range(4):
                evacuated(dve, ("k", j, i, f))
            if f == 0:
                evacuated(dve, ("ny", 2, i, f))
            ec, oc, es, os = (k_parts[g % 2][:, j, :] for j in range(4))
            ec_s, oc_s, oc_d = (ec, oc, oc) if f else (k_alt[:, j, :] for j in range(3))
            factors = ((ec, oc, es, os), (oc, ec, os, es), (es, os, ec_s, oc_d), (os, es, oc_s, ec_s))
            for j in range(4):
                if j and g:
                    dve.wait_ge(z_ready, 5 * (g - 1) + (0, 2, 3, 5)[j])
                name = ("x", j, i, f)
                filled(dve, name)
                for q, (a, par) in enumerate(PARTS):
                    dst = terms[j][:, a, par, :] if j else z[a][:, par, f, :]
                    ins = dve.tensor_tensor(dst, res(name)[:, :], factors[j][q], ALU.mult)
                ins.then_inc(drained(name), 1)
            evacuated(dve, ("x", 3, i, f))
            dve.tensor_tensor(terms[3][:, 1], terms[3][:, 1], terms[2][:, 1], ALU.add).then_inc(merged, 1)

        def gated(i):
            s, half, o = STEPS[i]
            n = (CL, CC)[s]
            if i == 0:
                evacuated(dve, ("tm", 0, 15))
                evacuated(dve, ("tm", 1, 15))
            if o == 0:
                for c in range(n):
                    name = ("y", i, c)
                    filled(dve, name)
                    cols = slice(COL * half, COL * half + COL)
                    dve.tensor_tensor(v_t[:, CL * s + c, cols], res(name)[:, :], x1_t[:, CL * s + c, cols],
                                      ALU.mult).then_inc(drained(name), 1)
            else:
                for cc in range(4):
                    name = ("y", i, cc)
                    filled(dve, name)
                    dst = x2T[:, 4 * half + cc, LAT * s:LAT * s + n * P].rearrange("p (n r) -> p r n", r=2)
                    y = res(name)[:, 0:n * P].rearrange("p (r n) -> p r n", r=2)
                    dve.tensor_tensor(dst, y, dst, ALU.mult).then_inc(drained(name), 1)

        start()
        modulation()
        sine_argument(0)
        modulation_columns()
        modulate_even()
        for tap in taps:
            for c in (0, LAT + 1, LAT + 2, LAT + 3 + CTX):
                ins = dve.memset(tap[:, c:c + 1], 0.0)
                if c in (0, LAT + 3 + CTX):
                    ins.then_inc(edges_zeroed, 1)
        for ch in range(24):
            if ch == 2:
                sine_argument(1)
            if ch == 4:
                sine_argument(2)
                dve.wait_ge(sin_done, 3)
                dve.wait_ge(keep_in, 32)
                dve.tensor_scalar(hf_diff, hf_sum, sgn, None, ALU.mult).then_inc(hf_done, 1)
            short_conv(ch)
        filled(dve, ("proj", 1, 23))
        windowed(0)
        for i, f in CHUNKS:
            if f == FREQ[STEPS[i][0]] - 1 and i < last_step:
                windowed(i + 1)
            if f == 0 and i:
                gated(i - 1)
            multiply(i, f)
        gated(last_step)

        def deviation_of(n, h):
            for half in (0, 1):
                ins = dve.bn_stats(stats[:, half, :], h[:, COL * half:COL * half + COL])
            link(ins)
            if n > 1:
                dve.wait_ge(dev_done, n - 1)
            dve.bn_aggr(mean_var, stats).then_inc(var_ready, 1)

        def centred(n, h):
            dve.wait_ge(dev_done, n)
            link(dve.reciprocal(rdev, dev))
            dve.wait_ge(var_ready, n)
            return dve.tensor_scalar(h, h, mean_var[:, 0:1], rdev, ALU.subtract, ALU.mult)

        def expert_inputs(l, c):
            r = "l" if c < CL else "c"
            g = gchunk(l, c)
            deviation_of(g + 1 + 6 * l, h_rows[:, c, :])
            link(centred(g + 1 + 6 * l, h_rows[:, c, :]))
            if c >= 2:
                dve.wait_ge(tok_stored[c % 2], 16 * (3 * l + c // 2))
                filled(dve, ("a2T", l, c - 2, 1))
            dve.tensor_tensor(a2[c % 2], h_rows[:, c, :], bcast[l]["sc2" + r], ALU.mult).then_inc(normed, 1)
            dve.wait_ge(normed, g + 1 + 6 * l)
            dve.tensor_tensor(a2[c % 2], a2[c % 2], bcast[l]["sh2" + r], ALU.add).then_inc(a2_done, 1)

        def residual(l, c):
            b = bcast[l]
            r = "l" if c < CL else "c"
            g = gchunk(l, c)
            if c == 0:
                dve.wait_ge(bc_in, 16 * (len(BC[0]) + (len(BC[1]) if l else 0)))
                for i, m in enumerate(("l", "c")[:2 - l]):
                    sc, sh = b["sc2" + m], b["sh2" + m]
                    dve.scalar_tensor_tensor(a2[i], sc, 1.0, b["lnb"], ALU.add, ALU.mult)
                    link(dve.scalar_tensor_tensor(sc, sc, 1.0, b["lng"], ALU.add, ALU.mult))
                    link(dve.tensor_tensor(sh, sh, a2[i], ALU.add))
            dve.wait_ge(res_in[c], 16 * (l + 1))
            for half in (0, 1):
                cols = slice(COL * half, COL * half + COL)
                name = ("out", l, c, half)
                filled(dve, name)
                if l == 0:
                    dve.tensor_tensor(tmp[half], res(name)[:, :], b["bout"][:, cols],
                                      ALU.add).then_inc(drained(name), 1)
                    evacuated(dve, name)
                    link(dve.tensor_tensor(tmp[half], tmp[half], b["g1" + r][:, cols], ALU.mult))
                else:
                    dve.tensor_tensor(tmp[half], res(name)[:, :], b["g1" + r][:, cols],
                                      ALU.mult).then_inc(drained(name), 1)
                    evacuated(dve, name)
                link(dve.scalar_tensor_tensor(h_rows[:, c, cols], h_rows[:, c, cols], ALPHA, tmp[half],
                                              ALU.mult, ALU.add))

        def choose(l):
            n = len(CHUNKS_OF[l])
            w = n * E_N
            BIG = -1.0e30
            dve.memset(chosen_before[:, 0:E_N], 0.0)

            def t4(x):
                return x[:, 0:w].rearrange("p (c g e) -> p c g e", c=n, g=GRP)

            def t3(x):
                return x[:, 0:w].rearrange("p (c e) -> p c e", c=n)

            def g3(x, m=GRP):
                return x[:, 0:n * m].rearrange("p (c g) -> p c g", c=n)

            def over8(x):
                return g3(x).unsqueeze(3).broadcast_to([P, n, GRP, GSZ])

            S = scores
            biased, first, second, work, m1, m2, gs, chosen, pick, gm = temps[0:10]
            dve.wait_ge(h_ready, gchunk(l, CHUNKS_OF[l][-1]) + 1)
            evacuated(dve, ("logit", l, n - 1))
            link(dve.tensor_tensor(t3(biased), t3(S), router_b.unsqueeze(1).broadcast_to([P, n, E_N]), ALU.add))

            def first_max(src, m, hot):
                link(dve.tensor_reduce(g3(m), t4(src), AX.X, ALU.max))
                link(dve.tensor_tensor(t4(work), t4(src), over8(m), ALU.is_equal))
                link(dve.tensor_tensor(t4(work), t4(work), ramp8.unsqueeze(1).unsqueeze(1).broadcast_to(
                    [P, n, GRP, GSZ]), ALU.mult))
                link(dve.tensor_reduce(g3(pick), t4(work), AX.X, ALU.max))
                link(dve.tensor_tensor(t4(hot), t4(work), over8(pick), ALU.is_equal))

            first_max(biased, m1, first)
            link(dve.scalar_tensor_tensor(biased[:, 0:w], first[:, 0:w], BIG, biased[:, 0:w], ALU.mult, ALU.add))
            first_max(biased, m2, second)
            link(dve.tensor_tensor(g3(gs), g3(m1), g3(m2), ALU.add))
            link(dve.tensor_reduce(gm[:, 0:n], g3(gs), AX.X, ALU.max))
            link(dve.tensor_tensor(g3(gs), g3(gs), gm[:, 0:n].unsqueeze(2).broadcast_to([P, n, GRP]), ALU.is_equal))
            link(dve.tensor_tensor(g3(gs), g3(gs), ramp4.unsqueeze(1).broadcast_to([P, n, GRP]), ALU.mult))
            link(dve.tensor_reduce(gm[:, 0:n], g3(gs), AX.X, ALU.max))
            link(dve.tensor_tensor(g3(gs), g3(gs), gm[:, 0:n].unsqueeze(2).broadcast_to([P, n, GRP]), ALU.is_equal))
            link(dve.tensor_tensor(t4(first), t4(first), over8(gs), ALU.mult))
            link(dve.tensor_tensor(t4(second), t4(second), over8(gs), ALU.mult))
            link(dve.tensor_tensor(chosen[:, 0:w], first[:, 0:w], second[:, 0:w], ALU.add))
            for c in range(n):
                ins = dve.tensor_tensor(chosen_before[:, E_N * (c + 1):E_N * (c + 2)],
                                        chosen_before[:, E_N * c:E_N * (c + 1)],
                                        chosen[:, E_N * c:E_N * (c + 1)], ALU.add)
                if c < n - 1:
                    link(ins)
            ins.then_inc(picked, 1)

            rank, blocks, ends, place = temps[10:14]
            blocks_i = blocks[:, 64:64 + E_N].bitcast(I32)
            filled(dve, ("count", l))
            dve.tensor_scalar(blocks_i, res(("count", l))[:, 0:E_N], float(SB - 1), None,
                              ALU.add).then_inc(drained(("count", l)), 1)
            evacuated(dve, ("count", l))
            link(dve.tensor_scalar(blocks_i, blocks_i, 6, None, ALU.logical_shift_right))
            link(dve.tensor_scalar(blocks[:, 0:E_N], blocks_i, 1.0, None, ALU.max))
            link(dve.memset(ends[:, 0:1], 0.0))
            link(dve.tensor_tensor_scan(ends[:, 1:E_N + 1], ones[:, 0:E_N], blocks[:, 0:E_N], 0.0,
                                        ALU.mult, ALU.add))
            dve.tensor_copy(starts[:, 0:E_N + 1], ends[0:1, 0:E_N + 1]).then_inc(starts_done, 1)
            link(dve.tensor_scalar(place[:, 0:E_N], ends[:, 0:E_N], float(SB), None, ALU.mult))
            dve.tensor_tensor(t3(rank), res(("rank", l))[:, 0:w].rearrange("p (c e) -> p c e", c=n),
                              place[:, 0:E_N].unsqueeze(1).broadcast_to([P, n, E_N]),
                              ALU.add).then_inc(drained(("rank", l)), 1)
            evacuated(dve, ("rank", l))
            dest_f, block_f = temps[14], temps[15]
            for k, hot in enumerate((first, second)):
                link(dve.tensor_tensor(work[:, 0:w], rank[:, 0:w], hot[:, 0:w], ALU.mult))
                link(dve.tensor_reduce(dest_f[:, n * k:n * k + n], t3(work), AX.X, ALU.add))
            dve.tensor_copy(dest[:, :, 0:n], dest_f[:, 0:2 * n].rearrange("p (k c) -> p k c", k=2)).then_inc(dest_done, 1)
            dve.wait_ge(dest_done, l + 1)

            nb = blocks_max((NT, LAT)[l]) + 2
            block_i = block_f[:, 64:64 + 2 * n].bitcast(U32)
            link(dve.tensor_scalar(block_i.rearrange("p (k c) -> p k c", k=2), dest[:, :, 0:n], 6, None,
                                   ALU.logical_shift_right))
            link(dve.tensor_scalar(block_f[:, 0:2 * n], block_i, 0.0, None, ALU.max))
            link(dve.scalar_tensor_tensor(dest_f[:, 0:2 * n], block_f[:, 0:2 * n], -float(SB), dest_f[:, 0:2 * n],
                                          ALU.mult, ALU.add))

            def one_hot(dst, x, m):
                return dve.tensor_tensor(dst[:, 0:2 * n, 0:m], x[:, 0:2 * n].unsqueeze(2).broadcast_to([P, 2 * n, m]),
                                         ramp64[:, 0:m].unsqueeze(1).broadcast_to([P, 2 * n, m]), ALU.is_equal)

            one_hot(hot_slot, dest_f, SB)
            link(one_hot(hot_block, block_f, nb))
            for k in (0, 1):
                part = hot_block[:, n * k:n * k + n, 0:nb]
                ins = dve.tensor_tensor(part, part, token_id[:, 0:n].unsqueeze(2).broadcast_to([P, n, nb]), ALU.mult)
            ins.then_inc(hots_done, 1)

            for k, hot in enumerate((first, second)):
                link(dve.tensor_tensor(work[:, 0:w], S[:, 0:w], hot[:, 0:w], ALU.mult))
                link(dve.tensor_reduce(pair_w[:, k, 0:n], t3(work), AX.X, ALU.add))
            link(dve.tensor_tensor(gm[:, 0:n], pair_w[:, 0, 0:n], pair_w[:, 1, 0:n], ALU.add))
            link(dve.reciprocal(gm[:, 0:n], gm[:, 0:n]))
            for k in (0, 1):
                link(dve.tensor_tensor(pair_w[:, k, 0:n], pair_w[:, k, 0:n], gm[:, 0:n], ALU.mult))

            filled(dve, ("slots", l))
            dve.tensor_copy(slot_tok[:, 0:nb], res(("slots", l))[0:SB, 0:nb]).then_inc(drained(("slots", l)), 1)
            dve.memset(keep[:, 1988 + 2 * l:1989 + 2 * l], 0.0).then_inc(y_copied[l], 1)
            dve.memset(keep[:, 1989 + 2 * l:1990 + 2 * l], 0.0).then_inc(y_stored[l], 32)

        def experts(l):
            pX, pG, pH = psum[0], psum[1:3], psum[3:5]
            dve.wait_ge(starts_done, l + 1)
            total = dve.value_load(starts[:, E_N:E_N + 1], min_val=1, max_val=blocks_max(NT))
            dve.wait_ge(x_turned[l], 1)
            dve.tensor_copy(xT, pX[:, :].rearrange("p (k n) -> p k n", k=KD)).then_inc(xT_done[l], 1)
            with dve.Fori(0, total) as b:
                for c in (0, 1):
                    dve.wait_ge(gate_done[l], 2 * b + c + 1)
                    dve.tensor_tensor(hid[c], pG[c][:, P:2 * P], gate_act[c], ALU.mult).then_inc(hid_done[l], 1)
                for c in (0, 1):
                    dve.wait_ge(hid_turned[l], 2 * b + c + 1)
                    dve.tensor_copy(hidT[c], pH[c][:, 0:P]).then_inc(hidT_done[l], 1)
                dve.wait_ge(x_turned[l], b + 2)
                dve.tensor_copy(xT, pX[:, :].rearrange("p (k n) -> p k n", k=KD)).then_inc(xT_done[l], 1)

        def mix_pair(l, c):
            dve.wait_ge(pair_in[c], 32 * (l + 1))
            dve.wait_ge(first_scaled, gchunk(l, c) + 1)
            dve.scalar_tensor_tensor(mix[c % 2], y_pair[c][1], pair_w[:, 1, c:c + 1], mix[c % 2], ALU.mult,
                                     ALU.add).then_inc(mixed_done, 1)

        def add_mix(l, c):
            h = h_rows[:, c, :]
            dve.wait_ge(scaled, gchunk(l, c) + 1)
            link(dve.scalar_tensor_tensor(h, h, ALPHA, mix[c % 2], ALU.mult, ALU.add))
            deviation_of(norm2(l, c), h)

        def last_vector(l, c):
            dve.wait_ge(lng_done, gchunk(l, c) + 1)
            dve.tensor_tensor(h_rows[:, c, :], h_rows[:, c, :], bc2["lnb"], ALU.add).then_inc(h_next, 1)

        def combine(l):
            chunks = CHUNKS_OF[l]
            mix_pair(l, 0)
            dve.wait_ge(bc2_in, 64 * (l + 1))
            for c in chunks:
                if c + 1 in chunks:
                    mix_pair(l, c + 1)
                add_mix(l, c)
                if c:
                    last_vector(l, c - 1)
                centred(norm2(l, c), h_rows[:, c, :]).then_inc(normed, 1)
            last_vector(l, chunks[-1])

        def finish(l):
            for c in CHUNKS_OF[l]:
                residual(l, c)
                expert_inputs(l, c)
            choose(l)
            experts(l)
            combine(l)

        finish(0)

        def gates(hd):
            cum = cums[hd % 2]
            for r in (0, 1):
                n_dir = 2 * hd + r
                for _, s, n, o in STREAMS:
                    name = ("g", hd, r, s)
                    dve.wait_ge(gates_abs, 2 * n_dir + s + 1)
                    dve.tensor_scalar(cum[:, r, o:o + n], res(name)[:, 0:n],
                                      smallT[:, 120 + 4 * r + hd:121 + 4 * r + hd], 0.0,
                                      ALU.add, ALU.min).then_inc(drained(name), 1)
                dve.wait_ge(gates_ln, n_dir + 1)
                for _, s, n, o in STREAMS:
                    evacuated(dve, ("g", hd, r, s))
                    m, l = cum[:, r, o:o + n], soft[:, o:o + n]
                    if r:
                        m, l = backwards(m, n), backwards(l, n)
                    dve.tensor_tensor_scan(m, m, l, 0.0, ALU.add, ALU.subtract).then_inc(cum_done, 1)

        def backwards(x, n):
            return x[:, n - 1::-1]

        def arguments(i):
            hd, lv = ITEMS[i]
            if lv in (0, LV_STATE):
                return
            cum = cums[hd % 2]
            dve.wait_ge(cum_done, 4 * (hd + 1))
            buffer_free(dve, i)
            buf = lev[i % 3]
            if lv == LV_CTX:
                for r, edge in ((0, NT - 1), (1, LAT)):
                    ins = dve.tensor_scalar(buf[:, CTX * r:CTX * r + CTX], cum[:, r, LAT:NT], -1.0,
                                            cum[:, r, edge:edge + 1], ALU.mult, ALU.add)
                ins.then_inc(args_done, 1)
                return
            h = 1 << (lv - 1)
            f = cum[:, 0, 0:LAT].rearrange("p (b m h) -> p b m h", m=2, h=h)
            g = cum[:, 1, 0:LAT].rearrange("p (b m h) -> p b m h", m=2, h=h)
            q = buf[:, 0:LAT].rearrange("p (b m h) -> p b m h", m=2, h=h)
            k = buf[:, LAT:2 * LAT].rearrange("p (b m h) -> p b m h", m=2, h=h)
            shape = [P, LAT // (2 * h), h]
            mid_f = f[:, :, 0, h - 1:h].broadcast_to(shape)
            mid_g = g[:, :, 1, 0:1].broadcast_to(shape)
            dve.tensor_tensor(q[:, :, 1, :], f[:, :, 1, :], mid_f, ALU.subtract)
            dve.tensor_tensor(q[:, :, 0, :], g[:, :, 0, :], mid_g, ALU.subtract)
            dve.tensor_tensor(k[:, :, 0, :], mid_f, f[:, :, 0, :], ALU.subtract)
            dve.tensor_tensor(k[:, :, 1, :], mid_g, g[:, :, 1, :], ALU.subtract).then_inc(args_done, 1)

        def masked(i):
            hd, lv = ITEMS[i]
            if lv <= LEVELS:
                name = ("att", i, 0)
                filled(dve, name)
                pairs = res(name)[:, :].rearrange("p (b n) -> p b n", b=CL)
                if lv == 0:
                    if hd:
                        dve.wait_ge(near_done, LEVELS * hd)
                    dve.scalar_tensor_tensor(att_near.rearrange("p (b n) -> p b n", b=CL), pairs, 2.0,
                                             ident.unsqueeze(1).broadcast_to([P, CL, P]),
                                             ALU.mult, ALU.mult).then_inc(drained(name), 1)
                else:
                    n = LEVELS * hd + lv
                    if n > 1:
                        dve.wait_ge(near_done, n - 1)
                    dve.tensor_tensor(prod.rearrange("p (b n) -> p b n", b=CL), pairs,
                                      masks[:, lv - 1, :].unsqueeze(1).broadcast_to([P, CL, P]),
                                      ALU.mult).then_inc(drained(name), 1)
            elif lv == LEVELS + 1:
                name = ("att", i, 0)
                filled(dve, name)
                dve.tensor_copy(att_next, res(name)[:, :]).then_inc(drained(name), 1)
            elif lv == LV_STATE:
                for u in range(CL):
                    name = ("o", hd, u)
                    filled(dve, name)
                    if hd and u == 0:
                        dve.wait_ge(o_var, CL * hd)
                    dve.bn_stats(g_stats[:, u, :], res(name)[:, 0:DVH])
                    dve.tensor_copy(o_rows[:, u, DVH * hd:DVH * hd + DVH], res(name)[:, 0:DVH]).then_inc(
                        drained(name), 1)
                evacuated(dve, ("o", hd, CL - 1))
                if hd:
                    dve.wait_ge(o_normed, hd)
                for u in range(CL):
                    dve.bn_aggr(g_mv[:, u, :], g_stats[:, u, :]).then_inc(o_var, 1)

        def normalise_head(hd):
            dve.wait_ge(o_dev, hd + 1)
            link(dve.reciprocal(g_rdev, g_dev))
            dve.wait_ge(o_var, CL * (hd + 1))
            for u in range(CL):
                o = o_rows[:, u, DVH * hd:DVH * hd + DVH]
                ins = dve.tensor_scalar(o, o, g_mv[:, u, 0:1], g_rdev[:, u:u + 1], ALU.subtract, ALU.mult)
            ins.then_inc(o_normed, 1)

        dve.memset(gate_w[0], 0.0).then_inc(zero_w, 1)
        filled(dve, ("aT1", 5, 1))
        dve.memset(gate_w[1], 0.0).then_inc(zero_w, 1)
        filled(dve, ("qk", 0, HEADS - 1, 0))
        gates(0)
        filled(dve, ("qk", 1, HEADS - 1, 1))
        arguments(1)
        arguments(2)
        for i, (hd, lv) in enumerate(ITEMS):
            if i and i + 2 < len(ITEMS):
                arguments(i + 2)
            if (hd, lv) == (HEADS - 1, LV_STATE):
                for c in (0, 2):
                    gated_rows(dve, c)
            masked(i)
            if lv == 5 and hd + 1 < HEADS:
                gates(hd + 1)
            if lv == 4 and hd:
                normalise_head(hd - 1)
        normalise_head(HEADS - 1)
        dve.wait_ge(o_normed, HEADS)
        dve.wait_ge(rows_gated, CL)
        cols = slice(DVH * (HEADS - 1), D)
        dve.tensor_tensor(r_rows[:, :, cols], r_rows[:, :, cols], o_rows[:, :, cols], ALU.mult).then_inc(y_rows_done, 1)
        for k in range(1, KD, 2):
            filled(dve, ("yT", k))
            dve.tensor_copy(mixed[1][:, k, :], res(("yT", k))[:, :]).then_inc(drained(("yT", k)), 1)
        finish(1)

    @block.gpsimd
    def _(pool):
        def positions():
            pool.wait_ge(x_in, 16)
            pool.wait_ge(pe_in, 32)
            left, right = x_rows[:, 0:CL, 0:COL], x_rows[:, 0:CL, COL:D]
            pool.tensor_tensor(left, left, pos_rows, ALU.add)
            pool.tensor_tensor(right, right, pos_cols.unsqueeze(1).broadcast_to([P, CL, COL]),
                               ALU.add).then_inc(pe_added, 1)

        def complex_sums():
            for g, (i, f) in enumerate(CHUNKS):
                for n, (j, a) in enumerate(((1, 0), (1, 1), (2, 0), (3, 0), (3, 1))):
                    evacuated(pool, ("x", j, i, f))
                    if j > 1:
                        pool.wait_ge(z_ready, 5 * g + n)
                    if (j, a) == (3, 1):
                        pool.wait_ge(merged, g + 1)
                    op = ALU.subtract if j >= 2 and a == 0 else ALU.add
                    pool.tensor_tensor(z[a][:, :, f, :], z[a][:, :, f, :], terms[j][:, a, :, :],
                                       op).then_inc(z_ready, 1)

        positions()
        complex_sums()

        def linker():
            n = [0]

            def link(ins):
                ins.then_inc(pool_link, 1)
                n[0] += 1
                pool.wait_ge(pool_link, n[0])
            return link

        link = linker()

        def affine(l, c):
            b = bcast[l]
            g = gchunk(l, c)
            h = h_rows[:, c, :]
            pool.wait_ge(normed, g + 1 + 6 * l)
            link(pool.tensor_tensor(h, h, b["lng"], ALU.mult))
            pool.tensor_tensor(h, h, b["lnb"], ALU.add).then_inc(h_ready, 1)

        def experts(l):
            def gather(dst):
                pool.indirect_dma_start(
                    out=dst, out_offset=None, in_=tok_l[l],
                    in_offset=bass.IndirectOffsetOnAxis(ap=cur_tok, axis=0)).then_inc(x_landed[l], 16)

            evacuated(pool, ("slots", l))
            pool.wait_ge(dest_done, l + 1)
            pool.wait_ge(y_filled_up, 16)
            for par in (0, 1):
                pool.wait_ge(tok_stored[par], 16 * (3 + 2 * l))
            pool.wait_ge(starts_done, l + 1)
            total = pool.value_load(starts[:, E_N:E_N + 1], min_val=1, max_val=blocks_max(NT))
            pool.tensor_copy(cur_tok, slot_tok[:, 0:1]).then_inc(x_copied[l], 1)
            pool.wait_ge(x_copied[l], 1)
            gather(x_slots)
            pool.wait_ge(x_landed[l], 16)
            pool.tensor_copy(cur_tok, slot_tok[:, 1:2]).then_inc(x_copied[l], 1)
            pool.wait_ge(x_copied[l], 2)
            gather(x_land)
            with pool.Fori(0, total) as b:
                pool.wait_ge(x_landed[l], 16 * b + 32)
                pool.tensor_copy(cur_tok, slot_tok[:, ds(b + 2, 1)]).then_inc(x_copied[l], 1)
                pool.wait_ge(x_turned[l], b + 1)
                pool.sem_inc(gather_go[l], 1)
                pool.tensor_copy(x_slots, x_land).then_inc(x_moved[l], 1)
                pool.wait_ge(x_copied[l], b + 3)
                pool.wait_ge(x_moved[l], b + 1)
                pool.sem_inc(gather_go[l], 1)
                gather(x_land)
            pool.wait_ge(y_stored[l], 32 * total + 32)
            pool.wait_ge(x_landed[l], 16 * total + 32)
            pool.wait_ge(gather_go[l], 2 * total)
            pool.wait_ge(xT_done[l], total + 1)
            pool.tensor_tensor(keep[:, 1992:1993], eps, eps, ALU.add).then_inc(combine_go, 1)
            pool.wait_ge(combine_go, l + 1)

        def combine(l):
            chunks = CHUNKS_OF[l]
            for c in (0, 1, 2):
                gather_pair(c)
            pool.wait_ge(bc2_in, 64 * (l + 1))
            gate_mix(l, 0)
            for c in chunks:
                if c + 3 in chunks:
                    gather_pair(c + 3)
                if c + 1 in chunks:
                    gate_mix(l, c + 1)
                pool.wait_ge(normed, norm2(l, c))
                pool.tensor_tensor(h_rows[:, c, :], h_rows[:, c, :], bc2["lng"], ALU.mult).then_inc(lng_done, 1)

        def gather_pair(c):
            for k in (0, 1):
                pool.indirect_dma_start(
                    out=y_pair[c][k], out_offset=None, in_=y_d,
                    in_offset=bass.IndirectOffsetOnAxis(ap=dest[:, k, c:c + 1], axis=0)).then_inc(pair_in[c], 16)

        def gate_mix(l, c):
            pool.wait_ge(mixed_done, gchunk(l, c) + 1)
            pool.tensor_tensor(mix[c % 2], mix[c % 2], bc2["g2" + ("l" if c < CL else "c")],
                               ALU.mult).then_inc(scaled, 1)

        def finish(l):
            for c in CHUNKS_OF[l]:
                affine(l, c)
            experts(l)
            combine(l)

        finish(0)

        def scale_qk(i):
            hd, lv = ITEMS[i]
            if lv == 0:
                return
            pool.wait_ge(exps_done, scaled_items(i))
            buf = lev[i % 3]
            if lv == LV_CTX:
                x = buf[:, 0:2 * CTX].rearrange("p (r n) -> p r n", r=2)
                y = k_ctx[:, hd, :].unsqueeze(1).broadcast_to([P, 2, CTX])
                evacuated(pool, ("qk", 1, hd, 1))
            elif lv == LV_STATE:
                x = buf.rearrange("p (r n) -> p r n", r=2)
                y = qk[:, hd, 0, :].unsqueeze(1).broadcast_to([P, 2, LAT])
            else:
                x = buf.rearrange("p (r n) -> p r n", r=2)
                y = qk[:, hd, :, :]
                evacuated(pool, ("qk", 0, hd, 0))
                evacuated(pool, ("qk", 1, hd, 0))
            pool.tensor_tensor(x, x, y, ALU.mult).then_inc(scaled_qk, 1)

        def add_near(i):
            hd, lv = ITEMS[i]
            if 1 <= lv <= LEVELS:
                evacuated(pool, ("att", i, 0))
                if lv == 1:
                    evacuated(pool, ("att", i - 1, 0))
                else:
                    pool.wait_ge(near_done, LEVELS * hd + lv - 1)
                pool.tensor_tensor(att_near, att_near, prod, ALU.add).then_inc(near_done, 1)

        scale_qk(1)
        scale_qk(2)
        for i, (hd, lv) in enumerate(ITEMS):
            if i and i + 2 < len(ITEMS):
                scale_qk(i + 2)
            add_near(i)
        for c in (1, 3):
            gated_rows(pool, c)
        finish(1)

    @block.sync
    def _(sp):
        def modulation():
            w = t["w_mod"].rearrange("l (k p) (h u c) -> l h u p k c", p=P, u=SLOTS, c=COL)
            for u in range(SLOTS):
                sp.dma_start(slot(u).rearrange("p (k c) -> p k c", k=KD), w[0, 0, u]).then_inc(landed[u], 16)
            for n in range(1, N_MOD // SLOTS):
                for u in range(SLOTS):
                    sp.wait_ge(mod_filled, SLOTS * (n - 1) + u + 1)
                    sp.dma_start(slot(u).rearrange("p (k c) -> p k c", k=KD),
                                 w[n // 2, n % 2, u]).then_inc(landed[u], 16)

        def hyena():
            w = t["hy_w_in"][0].rearrange("(k p) (j c) -> j p k c", p=P, c=COL)
            for j in range(6):
                sp.wait_ge(mod_filled, N_MOD - SLOTS + j + 1)
                if j == 1:
                    sp.wait_ge(mod_back, 64)
                s, _ = units.of[("hy_in", j)]
                sp.dma_start(slot(s).rearrange("p (k c) -> p k c", k=KD), w[j]).then_inc(landed[s], 16)
            filled(sp, ("proj", 1, 3))
            w4_d = t["hy_f_w4"][0].rearrange("f (o r c) -> r f o c", o=2, r=2)
            for r in (0, 1):
                sp.dma_start(w4[HF * r:HF * r + HF], w4_d[r]).then_inc(filt_in, 16)
            sp.dma_start(filt_u[:, 2 * D:3 * D], t["dft_small"]).then_inc(filt_in, 16)
            s, _ = units.of[("dft", 0)]
            filled(sp, ("proj", 1, 7))
            sp.dma_start(dft, t["dft"].rearrange("a r (c p) n -> p a r c n", p=P)).then_inc(landed[s], 16)
            s, _ = units.of[("idft", 0)]
            filled(sp, ("proj", 1, 11))
            sp.dma_start(idft, t["idft"].rearrange("a r (c p) n -> p a r c n", p=P)).then_inc(landed[s], 16)
            w = t["hy_w_out"][0].rearrange("(k p) (j c) -> j p k c", p=P, c=COL)
            for j in range(2):
                s, _ = units.of[("hy_out", j)]
                filled(sp, ("proj", 1, 4 * (3 + j) + 3))
                if j:
                    made(sp, len(CHUNKS))
                    sp.wait_ge(z_ready, 5 * len(CHUNKS))
                sp.dma_start(slot(s).rearrange("p (k c) -> p k c", k=KD), w[j]).then_inc(landed[s], 16)

        modulation()
        hyena()

        def experts(l):
            w1 = t["moe_w1"][l].rearrange("e (k p) c -> e p k c", p=P)
            w3 = t["moe_w3"][l].rearrange("e (k p) c -> e p k c", p=P)
            w2 = t["moe_w2"][l].rearrange("e (k p) c -> e p k c", p=P)

            for c in range(CL):
                sp.wait_ge(res_in[c], 16 * (l + 1))
            for e in (0, 1):
                for q in range(3):
                    free_for_experts(l, 3 * e + q)
                    w = (w1, w3, w2)[q]
                    sp.dma_start(slot(3 * e + q).rearrange("p (k c) -> p k c", k=(8, 8, 4)[q]),
                                 w[e]).then_inc(landed[3 * e + q], 16)

            def load(e, buf, turn_no, done):
                for q, w in enumerate((w1, w3, w2)):
                    b2, q2 = (buf, 0) if q == 2 else ((buf - 1) % 3, q + 1)
                    before = turn_no - (16 if q < 2 and buf == 0 else 0)
                    sp.wait_ge(expert_in[b2][q2], before + 16 * (expert_first(l, b2, q2) + 1))
                    if done is not None and q != 1:
                        sp.sem_inc(paced[l], 1)
                    if done is not None and q == 0:
                        sp.wait_ge(up_filled[l], 2 * done)
                    if done is not None and q == 2:
                        sp.wait_ge(y_filled[l], done)
                    sp.dma_start(expert_units[buf][q].rearrange("p (k c) -> p k c", k=(8, 8, 4)[q]),
                                 w[e].rearrange("o p k c -> (o p) k c")).then_inc(expert_in[buf][q], 16)

            sp.wait_ge(y_copied[l], 1)
            sp.wait_ge(x_landed[l], 16)
            load(slice(2, 3), 2, 0, None)
            with sp.Fori(1, E_N // 3) as third:
                for buf in range(3):
                    done = sp.value_load(starts[:, ds(3 * third + buf - 2, 1)], min_val=1, max_val=blocks_max(NT))
                    load(ds(3 * third + buf, 1), buf, 16 * third, done)
            for e in range(E_N - E_N % 3, E_N):
                done = sp.value_load(starts[:, e - 2:e - 1], min_val=1, max_val=blocks_max(NT))
                load(slice(e, e + 1), e % 3, 16 * (e // 3), done)
            sp.wait_ge(paced[l], 2 * (E_N - 3))

        def fill_outputs():
            rest = blocks_max(NT) - E_N
            src = t["zeros"].rearrange("s d -> () (s d)").broadcast_to([rest, SB * D])
            sp.dma_start(y_d[E_N * SB:].rearrange("(b s) d -> b (s d)", s=SB), src).then_inc(y_filled_up, 16)

        def free_for_experts(l, s):
            if l == 0:
                if s in (3, 4):
                    filled(sp, ("out", 0, 5, s - 3))
                else:
                    filled(sp, ("y", last_step, 3))
                    made(sp, len(CHUNKS))
                    sp.wait_ge(z_ready, 5 * len(CHUNKS))
                    sp.wait_ge(skip_added, len(STEPS))
            elif s < 4:
                filled(sp, ("o", HEADS - 1, CL - 1))
                if s == 2:
                    sp.wait_ge(y_rows_done, 1)
            else:
                filled(sp, ("out", 1, CL - 1, s - 4))

        fill_outputs()
        experts(0)

        def gla_weights():
            w = t["gla_w_in"][0, :, 0:3072].rearrange("(k p) (j c) -> j p k c", p=P, c=COL)
            wo = t["gla_w_out"][0].rearrange("(k p) (j c) -> j p k c", p=P, c=COL)
            for c in range(6):
                sp.wait_ge(pair_in[c], 32)
            for j in range(6):
                s, _ = units.of[("gla_in", j)]
                if j == 5:
                    sp.wait_ge(mixed_done, 6)
                sp.dma_start(slot(s).rearrange("p (k c) -> p k c", k=KD), w[j]).then_inc(landed[s], 16)
            for j in range(2):
                s, _ = units.of[("gla_out", j)]
                filled(sp, ("r", j, CL - 1))
                sp.dma_start(slot(s).rearrange("p (k c) -> p k c", k=KD), wo[j]).then_inc(landed[s], 16)

        gla_weights()
        experts(1)
        sp.wait_ge(out_stored, 16 * CL)

    ctx.close()


def constants():
    f8 = np.float64
    f4 = np.float32
    q = D // 4
    omega = 1.0 / (10000.0 ** (np.arange(q, dtype=f8) / q))
    pr = np.arange(LAT // 64, dtype=f8)[:, None] * omega
    pc = np.arange(64, dtype=f8)[:, None] * omega
    er = np.concatenate([np.sin(pr), np.cos(pr)], -1)
    ec = np.concatenate([np.sin(pc), np.cos(pc)], -1)
    pos_rows = np.repeat(er, 64, 0)
    pos_cols = np.tile(ec, (P // 64, 1))

    def features(n):
        x = np.linspace(0.0, 1.0, n)[:, None]
        w = 2.0 * np.pi * np.arange(n)[:, None] / n
        bands = np.linspace(1e-4, 15, 16)[None, :]
        return np.concatenate([x, np.cos(bands * w), -np.sin(bands * w)], -1)

    def window(n):
        deltas = np.abs(np.linspace(np.log(1e-2) / 1.5, np.log(1e-2) / 0.3, D))
        return np.exp(-np.linspace(0.0, 1.0, n)[:, None] * deltas)

    def by_parity(x):
        return np.concatenate([x[0::2], x[1::2]], 0)

    def transforms(n):
        fwd, inv = np.zeros((2, 2, n // 2, n // 2)), np.zeros((2, 2, n // 2, n // 2))
        for r in (0, 1):
            tok = np.arange(r, n, 2)
            ang = np.pi * np.outer(tok, np.arange(n // 2)) / n
            mid = -np.sin(np.pi * tok / 2) if r else np.cos(np.pi * tok / 2)
            fwd[0, r], fwd[1, r] = np.cos(ang), -np.sin(ang)
            fwd[1, r, :, 0] = mid
            inv[:, r] = fwd[:, r].transpose(0, 2, 1) * 2.0 / n
            inv[:, r, 0] /= 2.0
        return fwd, inv

    fwd, inv = transforms(LAT)
    small = np.stack(transforms(CTX))
    small = small.transpose(3, 0, 1, 2, 4).reshape(P, -1)
    marks = np.ones((P, 3))
    marks[HF:, 0] = -1.0
    marks[0, 1] = 0.0
    marks[:, 2] = EPS
    i = np.arange(P)
    masks = np.zeros((P, LEVELS, P))
    for l in range(LEVELS):
        same = i[:, None] // (2 << l) == i[None] // (2 << l)
        masks[:, l] = same & (i[:, None] // (1 << l) != i[None] // (1 << l))
    token = i[:, None] + P * np.arange(NT // P)[None]
    ramps = np.concatenate([np.arange(8, 0, -1), np.arange(4, 0, -1)])
    route = np.concatenate([(i[:, None] < i[None]), np.ones((P, P)), token,
                            np.broadcast_to(ramps, (P, 12)), np.broadcast_to(np.arange(SB), (P, SB))], 1)
    out = dict(ident=np.eye(P), marks=marks, pos_rows=pos_rows, pos_cols=pos_cols, dft=fwd, idft=inv, dft_small=small,
               window_lat=by_parity(window(LAT)), window_ctx=by_parity(window(CTX)),
               zT=np.concatenate([by_parity(features(LAT)), by_parity(features(CTX))], 0).T,
               masks=masks.reshape(P, -1), route_c=route, zeros=np.zeros((SB, D)))
    return {k: np.ascontiguousarray(v, dtype=f4) for k, v in out.items()}


_INS = ["x", "c", "ctx", "c_ctx", "w_mod", "b_mod", "ln_g", "ln_b", "hy_w_in", "hy_b_in", "hy_conv_w",
        "hy_conv_b", "hy_f_w1", "hy_f_b1", "hy_f_w2", "hy_f_b2", "hy_f_w3", "hy_f_b3", "hy_f_w4",
        "hy_skip", "hy_w_out", "hy_b_out", "gla_w_in", "gla_w_gate", "gla_b_gate", "gla_norm_g",
        "gla_w_out", "router_w", "router_b", "moe_w1", "moe_w3", "moe_w2"]


def kernel(**inputs):
    import numpy as _np
    import concourse.bacc as _bacc
    from concourse import mybir as _mybir
    from concourse.bass_utils import run_bass_kernel_spmd as _run

    nc = _bacc.Bacc("TRN2", target_bir_lowering=False, num_devices=1)
    arrays, tensors = {}, {}
    data = {n: _np.ascontiguousarray(inputs[n]) for n in _INS}
    for name, a in {**data, **constants()}.items():
        arrays[f"in_{name}"] = a
        tensors[name] = nc.dram_tensor(f"in_{name}", a.shape, _mybir.dt.from_np(a.dtype),
                                       kind="ExternalInput").ap()
    out = nc.dram_tensor("out_h", (1, LAT, D), F32, kind="ExternalOutput").ap()
    build(nc, tensors, out)
    r = _run(nc, [arrays], core_ids=[0])
    return r.results[0]["out_h"]
```
